# Optimizing a Trainium2 kernel written in Bass

```python
import math
import jax, jax.numpy as jnp
from jax import lax
import numpy as np

D_MODEL = 1024
BATCH = 1
SEQ = 512
DEPTH = 2

CTX_LEN = 256
GRID_W = 64
W_BRANCH = 512
N_BRANCH = 3
N_HEADS = 8
N_KV_HEADS = 2
GROUP = N_HEADS // N_KV_HEADS
HEAD_DIM = 64
ROPE_FREQS = HEAD_DIM // 4
ROPE_BASE = 10000.0
Q_BLOCK = 128
ATTN_SCALE = HEAD_DIM ** -0.5
HYENA_ORDER = 2
FILTER_EMB = 33
FILTER_BANDS = (FILTER_EMB - 1) // 2
FILTER_HIDDEN = 64
HYENA_TARGET = 1e-2
FAST_DECAY_PCT = 0.3
SLOW_DECAY_PCT = 1.5
MIN_DECAY = math.log(HYENA_TARGET) / SLOW_DECAY_PCT
MAX_DECAY = math.log(HYENA_TARGET) / FAST_DECAY_PCT
EPS = 1e-6

A_COLS = 4 * W_BRANCH
H_COLS = 4 * W_BRANCH
Q_COLS = N_HEADS * HEAD_DIM
KV_COLS = N_KV_HEADS * HEAD_DIM
H_OFF = A_COLS
C_OFF = H_OFF + H_COLS
K_OFF = C_OFF + Q_COLS
V_OFF = K_OFF + KV_COLS
Z_OFF = V_OFF + KV_COLS
G_OFF = Z_OFF + W_BRANCH
IN_COLS = G_OFF + N_BRANCH * D_MODEL

kernel_name = 'hybrid_conv_hyena_gqa_dit_block'

def _rms_norm(x, g):
    xf = x.astype(jnp.float32)
    y = xf * lax.rsqrt(jnp.mean(xf * xf, axis=-1, keepdims=True) + EPS)
    return (y * g.astype(jnp.float32)).astype(x.dtype)

def _short_conv(u, w):
    up = jnp.pad(u, ((0, 0), (1, 1), (0, 0)))
    return up[:, :-2] * w[0] + up[:, 1:-1] * w[1] + up[:, 2:] * w[2]

def _rope_tables(L):
    rows = L // GRID_W
    row = jnp.repeat(jnp.arange(rows, dtype=jnp.float32), GRID_W)
    col = jnp.tile(jnp.arange(GRID_W, dtype=jnp.float32), rows)
    inv = ROPE_BASE ** (-jnp.arange(ROPE_FREQS, dtype=jnp.float32) / ROPE_FREQS)
    ang = jnp.stack([row[:, None] * inv, col[:, None] * inv], axis=1)
    return jnp.cos(ang)[:, None], jnp.sin(ang)[:, None]

def _apply_rope(x, cos, sin):
    B_, L, H, _ = x.shape
    xf = x.astype(jnp.float32).reshape(B_, L, H, 2, 2, ROPE_FREQS)
    x1, x2 = xf[..., 0, :], xf[..., 1, :]
    out = jnp.stack([x1 * cos - x2 * sin, x2 * cos + x1 * sin], axis=-2)
    return out.reshape(x.shape).astype(x.dtype)

def _hyena_kernels_f(L, w1, b1, w2, b2, w3, b3, freq):
    f32 = jnp.float32
    t = jnp.linspace(0.0, 1.0, L, dtype=f32)[:, None]
    bands = jnp.linspace(1e-4, FILTER_BANDS - 1, FILTER_BANDS, dtype=f32)
    w = (2.0 * math.pi / L) * jnp.arange(L, dtype=f32)[:, None]
    feats = jnp.concatenate([t, jnp.cos(w * bands), jnp.sin(w * bands)], axis=-1)
    h = jnp.sin(freq[0].astype(f32) * (feats @ w1.astype(f32) + b1.astype(f32)))
    h = jnp.sin(freq[1].astype(f32) * (h @ w2.astype(f32) + b2.astype(f32)))
    h = (h @ w3.astype(f32) + b3.astype(f32)).reshape(L, HYENA_ORDER, 2, W_BRANCH)
    deltas = jnp.abs(jnp.linspace(MIN_DECAY, MAX_DECAY, W_BRANCH, dtype=f32))
    h = h * jnp.exp(-t[:, :, None, None] * deltas)
    kern = jnp.concatenate([h[:, :, 0], jnp.zeros((1, HYENA_ORDER, W_BRANCH), f32),
                            h[:0:-1, :, 1]], axis=0)
    kern = kern / jnp.sum(jnp.abs(kern), axis=0, keepdims=True)
    return jnp.fft.rfft(kern, axis=0)

def _long_conv(u, kf, bias):
    L = u.shape[1]
    uf = u.astype(jnp.float32)
    U = jnp.fft.rfft(uf, n=2 * L, axis=1)
    y = jnp.fft.irfft(U * kf, n=2 * L, axis=1)[:, :L]
    return (y + uf * bias.astype(jnp.float32)).astype(u.dtype)

def _q_heads(p, q_g):
    B_, L, _ = p.shape
    return _rms_norm(p[..., C_OFF:K_OFF].reshape(B_, L, N_HEADS, HEAD_DIM), q_g)

def _kv_heads(pkv, k_g):
    B_, L, _ = pkv.shape
    k = _rms_norm(pkv[..., :KV_COLS].reshape(B_, L, N_KV_HEADS, HEAD_DIM), k_g)
    v = pkv[..., KV_COLS:].reshape(B_, L, N_KV_HEADS, HEAD_DIM)
    return k, v

def _gqa(q, keys, vals):
    B_, Q, _, _ = q.shape
    qg = q.reshape(B_, Q, N_KV_HEADS, GROUP, HEAD_DIM)
    s = jnp.einsum('bqkgd,bskd->bkgqs', qg, keys).astype(jnp.float32) * ATTN_SCALE
    p = jax.nn.softmax(s, axis=-1).astype(vals.dtype)
    o = jnp.einsum('bkgqs,bskd->bqkgd', p, vals)
    return o.reshape(B_, Q, N_HEADS * HEAD_DIM)

def _latent_attention(q, k, v, k_c, v_c):
    B_, S, H, Dh = q.shape
    keys = jnp.concatenate([k_c, k], axis=1)
    vals = jnp.concatenate([v_c, v], axis=1)
    qb = q.reshape(B_, S // Q_BLOCK, Q_BLOCK, H, Dh).swapaxes(0, 1)
    o = lax.map(lambda qblk: _gqa(qblk, keys, vals), qb)
    return o.swapaxes(0, 1).reshape(B_, S, H * Dh)

def _mixer(p, attn_out, conv_a, conv_h, kern_f, hyena_bias, w_branch, w_out):
    B_, L, _ = p.shape
    xa, ba, ca, za = jnp.split(p[..., :A_COLS], 4, axis=-1)
    y_a = ba * _short_conv(ca * xa, conv_a) * jax.nn.silu(za)
    v, x1, x2 = jnp.split(_short_conv(p[..., H_OFF:H_OFF + 3 * W_BRANCH], conv_h), 3, axis=-1)
    z = x1 * _long_conv(v, kern_f[:, 0], hyena_bias[0])
    z = x2 * _long_conv(z, kern_f[:, 1], hyena_bias[1])
    y_b = z * jax.nn.silu(p[..., H_OFF + 3 * W_BRANCH:C_OFF])
    y_c = attn_out * jax.nn.silu(p[..., Z_OFF:G_OFF])
    gates = jax.nn.sigmoid(p[..., G_OFF:].astype(jnp.float32)).reshape(B_, L, N_BRANCH, D_MODEL)
    proj = jnp.einsum('blnw,nwd->blnd', jnp.stack([y_a, y_b, y_c], axis=2), w_branch)
    merged = jnp.sum(gates * proj.astype(jnp.float32), axis=2).astype(p.dtype)
    return merged @ w_out

def setup_inputs(seed: int = 0) -> dict:
    key = jax.random.key(seed)
    ks = jax.random.split(key, 22)
    f32 = jnp.float32
    nrm = lambda k, shape, s: jax.random.normal(k, shape, f32) * s
    return {
        'x': nrm(ks[0], (BATCH, SEQ, D_MODEL), 1.0),
        'c': nrm(ks[1], (BATCH, D_MODEL), 1.0),
        'ctx': nrm(ks[2], (BATCH, CTX_LEN, D_MODEL), 1.0),
        'c_ctx': nrm(ks[3], (D_MODEL,), 1.0),
        'norm_g': 1.0 + nrm(ks[4], (DEPTH, D_MODEL), 0.02),
        'w_mod': nrm(ks[5], (DEPTH, D_MODEL, 3 * D_MODEL), 0.5 * D_MODEL ** -0.5),
        'b_mod': nrm(ks[6], (DEPTH, 3 * D_MODEL), 0.02),
        'w_in': nrm(ks[7], (DEPTH, D_MODEL, IN_COLS), D_MODEL ** -0.5),
        'conv_a': nrm(ks[8], (DEPTH, 3, W_BRANCH), 3 ** -0.5),
        'conv_h': nrm(ks[9], (DEPTH, 3, 3 * W_BRANCH), 3 ** -0.5),
        'filt_w1': nrm(ks[10], (DEPTH, FILTER_EMB, FILTER_HIDDEN), FILTER_EMB ** -0.5),
        'filt_b1': nrm(ks[11], (DEPTH, FILTER_HIDDEN), 0.02),
        'filt_w2': nrm(ks[12], (DEPTH, FILTER_HIDDEN, FILTER_HIDDEN), FILTER_HIDDEN ** -0.5),
        'filt_b2': nrm(ks[13], (DEPTH, FILTER_HIDDEN), 0.02),
        'filt_w3': nrm(ks[14], (DEPTH, FILTER_HIDDEN, HYENA_ORDER * 2 * W_BRANCH), FILTER_HIDDEN ** -0.5),
        'filt_b3': nrm(ks[15], (DEPTH, HYENA_ORDER * 2 * W_BRANCH), 0.02),
        'filt_freq': 1.0 + nrm(ks[16], (DEPTH, 2, FILTER_HIDDEN), 0.1),
        'hyena_bias': nrm(ks[17], (DEPTH, HYENA_ORDER, W_BRANCH), 0.5),
        'q_norm_g': 1.0 + nrm(ks[18], (DEPTH, HEAD_DIM), 0.02),
        'k_norm_g': 1.0 + nrm(ks[19], (DEPTH, HEAD_DIM), 0.02),
        'w_branch': nrm(ks[20], (DEPTH, N_BRANCH, W_BRANCH, D_MODEL), W_BRANCH ** -0.5),
        'w_out': nrm(ks[21], (DEPTH, D_MODEL, D_MODEL), D_MODEL ** -0.5),
    }

def reference(x, c, ctx, c_ctx, norm_g, w_mod, b_mod, w_in, conv_a, conv_h, filt_w1, filt_b1,
              filt_w2, filt_b2, filt_w3, filt_b3, filt_freq, hyena_bias, q_norm_g, k_norm_g,
              w_branch, w_out):
    S = x.shape[1]
    C_L = ctx.shape[1]
    cos, sin = _rope_tables(S)
    for i in range(DEPTH):
        last = i == DEPTH - 1
        filt = (filt_w1[i], filt_b1[i], filt_w2[i], filt_b2[i], filt_w3[i], filt_b3[i], filt_freq[i])
        sh, sc, gt = jnp.split(jax.nn.silu(c) @ w_mod[i] + b_mod[i], 3, axis=-1)
        sh_c, sc_c, gt_c = jnp.split(jax.nn.silu(c_ctx) @ w_mod[i] + b_mod[i], 3, axis=-1)
        h = _rms_norm(x, norm_g[i]) * (1.0 + sc[:, None]) + sh[:, None]
        hc = _rms_norm(ctx, norm_g[i]) * (1.0 + sc_c) + sh_c
        if last:
            k_c, v_c = _kv_heads(hc @ w_in[i][:, K_OFF:Z_OFF], k_norm_g[i])
        else:
            pc = hc @ w_in[i]
            k_c, v_c = _kv_heads(pc[..., K_OFF:Z_OFF], k_norm_g[i])
            attn_c = _gqa(_q_heads(pc, q_norm_g[i]), k_c, v_c)
            out_c = _mixer(pc, attn_c, conv_a[i], conv_h[i], _hyena_kernels_f(C_L, *filt),
                           hyena_bias[i], w_branch[i], w_out[i])
            ctx_next = ctx + gt_c * out_c
        p = h @ w_in[i]
        q = _apply_rope(_q_heads(p, q_norm_g[i]), cos, sin)
        k, v = _kv_heads(p[..., K_OFF:Z_OFF], k_norm_g[i])
        k = _apply_rope(k, cos, sin)
        attn = _latent_attention(q, k, v, k_c, v_c)
        out = _mixer(p, attn, conv_a[i], conv_h[i], _hyena_kernels_f(S, *filt),
                     hyena_bias[i], w_branch[i], w_out[i])
        x = x + gt[:, None] * out
        if not last:
            ctx = ctx_next
    return x


_drawn_inputs = setup_inputs


def setup_inputs(seed=0):
    import zlib

    import numpy as np

    out = dict(_drawn_inputs(seed))
    spreads = {}
    factors = {'ctx': 8.0,
     'c_ctx': 3.853,
     'norm_g': 7.014,
     'b_mod': 3.115,
     'filt_w1': 3.404,
     'filt_b1': 8.0,
     'filt_w2': 3.196,
     'filt_b2': 8.0,
     'filt_w3': 3.877,
     'filt_b3': 59.463,
     'filt_freq': 8.0,
     'q_norm_g': 64.0,
     'k_norm_g': 64.0}
    for name, (base, spread) in spreads.items():
        noise = np.random.default_rng([zlib.crc32(name.encode()), seed]).standard_normal(out[name].shape)
        drawn = base * np.exp(spread * noise) if base else spread * noise
        out[name] = __import__('jax').numpy.asarray(drawn.astype(out[name].dtype))
    for name, factor in factors.items():
        out[name] = (out[name] * factor).astype(out[name].dtype)
    return out
```

```python
import concourse.bass as bass
from concourse import mybir
from contextlib import ExitStack, contextmanager

D = 1024
KD = D // 128
SEQ, CTX = 512, 256
DEPTH = 2
WB = 512
CB = WB // 128
NH, NKV, HD = 8, 2, 64
FEMB, FHID = 33, 64
EPS = 1e-6
SCALE = HD ** -0.5

UW = 512
RAW, RING, LEAD = 3, 9, 5
U_AHZ, U_Q, U_G, U_O = 4 * 18, 12, 8 * 9, 16
U_LAYER = U_AHZ + U_Q + U_G + U_O
U_MOD = DEPTH * 48

V_NG, V_BM, V_CONV, V_HB, V_QG, V_KG, V_FIL = 0, 8, 32, 80, 88, 89, 90
NV = 94

C1, C2 = 6.28125, 0.0019350051879882812
C3 = 6.283185307179586 - C1 - C2
MAGIC = 12582912.0
PI_IN = 3.1415925


def build(nc, d_stream, d_mod, d_cc, d_x, d_ctx, d_vec, d_fw1, d_fw2, d_w3, d_feats, d_dec, d_tab, d_rope,
          d_x1, d_ctx1, d_out):
    f32, f32r = mybir.dt.float32, mybir.dt.float32r
    ACT, ALU, AX = mybir.ActivationFunctionType, mybir.AluOpType, mybir.AxisListType
    K = 1024
    BASE = 16512

    def at(name, shape, kb, dt=f32):
        return nc.alloc_sbuf_tensor_at(name, shape, dt, offset=BASE + int(kb * K))

    raw = at("raw", [128, RAW, UW], 0)
    w_hi = at("w_hi", [128, RING, UW], 6, f32r)
    w_lo = at("w_lo", [128, RING, UW], 24, f32r)
    ones = at("ones", [128, 128], 42)
    ident = at("ident", [128, 128], 42.5)
    heads2 = at("heads2", [128, 2], 43)
    vec = at("vec", [128, DEPTH, NV], 43.0625)
    modv = at("modv", [128, DEPTH, 24, 2], 43.8125)
    gain = at("gain", [128, DEPTH, KD, 2], 44.25)
    mraw = at("mraw", [128, DEPTH * 24, 4], 44.375)
    cc = at("cc", [128, KD, 2], 45.125)
    cs = at("cs", [128, KD, 2], 45.1875)
    c4 = at("c4", [128, KD, 4], 45.25, f32r)
    ms = at("ms", [128, 10 * 4], 45.375)
    rs = at("rs", [128, 10 * 4], 45.5625)
    nu = at("nu", [128, 10 * 4], 45.75)
    den = at("den", [128, 32], 45.9375)
    rden = at("rden", [128, 32], 46.0625)
    nmx = at("nmx", [128, 32], 46.1875)
    mx = at("mx", [128, 32], 46.3125)
    knorm = at("knorm", [128, 2], 46.4375)
    kx = at("kx", [128, SEQ + CTX], 47)
    vx = at("vx", [128, SEQ + CTX], 50)
    h_hi = at("h_hi", [128, KD, SEQ], 53, f32r)
    h_lo = at("h_lo", [128, KD, SEQ], 69, f32r)
    ya = at("ya", [128, CB, SEQ], 85)
    vb = at("vb", [128, CB, SEQ], 93)
    zs = at("zs", [128, CB, SEQ], 101)
    traw = at("traw", [128, 4096], 109)
    feats = at("feats", [FEMB, SEQ], 85)
    arg = at("arg", [FHID, SEQ], 87)
    turn = at("turn", [FHID, SEQ], 89)
    h1 = at("h1", [FHID, SEQ], 91)
    fw1 = at("fw1", [FEMB, FHID], 93)
    fw2 = at("fw2", [FHID, FHID], 93.5)
    xb = at("xb", [128, KD, SEQ], 171)
    sq = at("sq", [128, 2, SEQ], 187)
    xt = at("xt", [128, 2, SEQ], 191)
    x12 = at("x12", [128, 2, CB, SEQ], 109)
    tab_hi = at("tab_hi", [128, 4096], 125, f32r)
    tab_lo = at("tab_lo", [128, 4096], 141, f32r)
    dec = at("dec", [128, 4, WB], 157)
    w3s = at("w3s", [FHID + 1, 2, 512], 165)
    h2 = at("h2", [FHID + 1, SEQ], 169)
    pads = at("pads", [128, 4, SEQ + 8], 171)
    ca_s = at("ca_s", [128, SEQ], 180)
    sza = at("sza", [128, SEQ], 182)
    szh = at("szh", [128, SEQ], 184)
    y1 = at("y1", [128, SEQ], 186)
    y2 = at("y2", [128, SEQ], 188)
    kspec = at("kspec", [128, 2, 2, 2, 256], 171)
    kp_hi = at("kp_hi", [128, 4, 512], 179, f32r)
    kp_lo = at("kp_lo", [128, 4, 512], 187, f32r)
    u_hi = at("u_hi", [128, 4, 256], 179, f32r)
    u_lo = at("u_lo", [128, 4, 256], 183, f32r)
    y_hi = at("y_hi", [128, 2, 2, 256], 187, f32r)
    y_lo = at("y_lo", [128, 2, 2, 256], 191, f32r)
    uu = at("uu", [128, 2, 2, 256], 195)
    p1 = at("p1", [128, 2, 2, 256], 199)
    p2 = at("p2", [128, 2, 2, 256], 203)
    kg = at("kg", [128, 2, 512], 195)
    kt = at("kt", [128, 2, 512], 199)
    kab = at("kab", [128, 2, 512], 203)
    zt = at("zt", [128, 512], 195)
    e_sb = at("e_sb", [128, 512], 47)
    q_hl = at("q_hl", [128, NH, SEQ], 109, f32r)
    k_hi = at("k_hi", [128, NKV, SEQ + CTX], 125, f32r)
    k_lo = at("k_lo", [128, NKV, SEQ + CTX], 131, f32r)
    v_hi = at("v_hi", [128, 6, 128], 137, f32r)
    v_lo = at("v_lo", [128, 6, 128], 140, f32r)
    ropes = at("ropes", [128, 2, SEQ], 143)
    oT = at("oT", [128, CB, SEQ], 149)
    pt_hi = at("pt_hi", [128, 2, 6, 256], 157, f32r)
    pt_lo = at("pt_lo", [128, 2, 6, 256], 169, f32r)
    pb = at("pb", [128, 2, SEQ + CTX], 181)
    rb = at("rb", [128, 2, 256], 187)
    qraw = at("qraw", [128, 5, SEQ], 157)
    qsq = at("qsq", [128, 5, SEQ], 167)
    rsx = at("rsx", [128, 10 * 4, HD], 167)
    qn = at("qn", [128, 5, SEQ], 177)
    qsh = at("qsh", [128, 5, SEQ], 187)
    qr = at("qr", [128, CB, SEQ], 197)
    b_hi = at("b_hi", [128, 3, CB, SEQ], 109, f32r)
    b_lo = at("b_lo", [128, 3, CB, SEQ], 133, f32r)
    mg = at("mg", [128, KD, SEQ], 157)
    xr = at("xr", [128, KD, SEQ], 173)
    sg = at("sg", [128, 3, SEQ], 189)
    tg = at("tg", [128, 2, SEQ], 195)

    ctx = ExitStack()
    with ctx:
        ps = ctx.enter_context(nc.psum_tensor("ps", [128, 8, 512], f32))

        def sem(name):
            return ctx.enter_context(nc.semaphore(name))

        s_raw = [sem(f"s_raw{b}") for b in range(RAW)]
        s_hi = sem("s_hi")
        s_lo = sem("s_lo")
        s_used = sem("s_used")
        s_act = sem("s_act")
        s_dve = sem("s_dve")
        s_const = sem("s_const")
        s_cdma = sem("s_cdma")
        s_c4 = sem("s_c4")
        s_mraw = sem("s_mraw")

        sems, counts = {}, {}

        class Job:

            def __init__(self, name, layer, who, full, first_unit):
                self.name, self.layer, self.who, self.full, self.u0 = name, layer, who, full, first_unit
                self.L = SEQ if who == 0 else CTX
                self.T = self.L // 128
                self.Lh = self.L // 2
                self.FT = self.Lh // 128
                self.TW = 2 * self.L * self.L // 128
                self.nk = SEQ + CTX if who == 0 else CTX
                self.k0 = 0 if who == 0 else SEQ
                self.kt = self.nk // 128
                L, T, FT, full = self.L, self.T, self.FT, self.full
                steps, nt = NH * T, 6 if full else 2
                self.total = dict(xin=16, sq=8, msq=7, msd=2, ms=2, rt=2, rs=2, rbc=1, xt=8, hh=8, hl=8,
                                  qraw=nt, rsx=1, qsq=nt - 1, qn=nt - 1, qbc=nt - 1, done=1)
                if full:
                    self.total.update(
                        fil=48, tab=16, dec=16, w3=32, rope=16 * (who == 0), xr=16, stored=16 * KD,
                        tabh=1, tabl=1, fm=2, fa=2, fs=2, eva=1 + 7 * CB, evd=1 + 2 * CB, ya=1 + CB, cv=1 + 3 * CB,
                        kgen=4 * T, kd=4 * T, kt=4 * T, kh=4 * T, kl=4 * T, kab=4 * T, ksum=4 * T, kn=4, kf=4 * FT, ke=4 * FT, kuse=4 * FT,
                        ut=2 * T, uh=2 * T, ul=2 * T, uf=4 * FT, ue=4 * FT, uuse=4 * FT, eo=4 * FT, yh=4 * FT, yl=4 * FT,
                        yi=4 * FT, fin=4, qr=1, ksp=6, ksl=6, vt=1, vh=1, vl=1,
                        qk=steps, mx=steps, ex=steps, rd=steps, tp=steps, ph=steps, pl=steps,
                        rt2=steps // 2, rb=steps // 2, pv=steps // 2, oout=steps // 2, yc=1, bh=3, bl=3,
                        sg=3 + 3 * KD, pm=3 + 3 * KD, mg=KD, gh=KD, gl=KD, xo=KD)
                for n in self.total:
                    if n not in sems:
                        sems[n] = sem(f"s_{n}")
                self.base = dict(counts)
                for n, v in self.total.items():
                    counts[n] = counts.get(n, 0) + v

            def s(self, name):
                assert name in self.total, name
                return sems[name]

            def at(self, name, value):
                return self.s(name), value + self.base.get(name, 0)

        u = U_MOD
        jobs = []
        for name, layer, who, full in (("c0", 0, 1, True), ("x0", 0, 0, True), ("c1", 1, 1, False), ("x1", 1, 0, True)):
            jobs.append(Job(name, layer, who, full, u))
            u += U_LAYER if full else 4
        N_UNITS = u
        before = {j: (jobs[n - 1] if n else None) for n, j in enumerate(jobs)}

        class Chain:

            def __init__(self, eng, s):
                self.eng, self.sem, self.n, self.at = eng, s, 0, 0

            def __call__(self, ins):
                self.n += 1
                ins.then_inc(self.sem, 1)
                self.eng.wait_ge(self.sem, self.at + self.n)

            @contextmanager
            def loop(self, count, steps):
                start = self.n
                with self.eng.Fori(0, count, 1) as i:
                    self.at = i * steps
                    yield i
                    assert self.n - start == steps, (self.n - start, steps)
                self.at = 0
                self.n = start + steps * count

        def mm3(out, hi, lo, m_hi, m_lo, start, stop):
            nc.tensor.matmul(out, hi, m_hi, start=start, stop=False)
            nc.tensor.matmul(out, hi, m_lo, start=False, stop=False)
            return nc.tensor.matmul(out, lo, m_hi, start=False, stop=stop)

        block = ctx.enter_context(nc.Block())

        @block.sync
        def _(sp):
            def unit(src, index, n, i=0, per=0):
                b = n % RAW
                if n >= RAW:
                    sp.wait_ge(s_lo, n - RAW + 1 + i * per)
                sp.dma_start(raw[:, b, :], src[bass.ds(index, 1)].rearrange("o p c -> p (o c)")).then_inc(s_raw[b], 16)

            def segment(src, first, n, count):
                done = 0
                if n == 0:
                    for p in range(RING):
                        unit(src, first + p, n + p)
                    done = RING
                loops = (count - done) // RING
                if loops > 1:
                    with sp.Fori(0, loops, 1) as i:
                        for p in range(RING):
                            unit(src, i * RING + (first + done + p), n + done + p, i, RING)
                    done += loops * RING
                for p in range(done, count):
                    unit(src, first + p, n + p)

            segment(d_mod, 0, 0, U_MOD)
            for j in jobs:
                if j.full:
                    segment(d_stream[j.layer], 0, j.u0, U_LAYER)
                else:
                    segment(d_stream[j.layer], U_AHZ, j.u0, 4)
            for j in jobs:
                if j.full:
                    sp.wait_ge(*j.at("stored", 16 * KD))

        @block.gpsimd
        def _(pool):
            nc.gpsimd.memset(ident[:, :], 0.0).then_inc(s_const, 1)
            nc.gpsimd.memset(ones[:, :], 1.0).then_inc(s_const, 1)
            nc.gpsimd.memset(heads2[:, :], 0.0).then_inc(s_const, 1)
            pool.wait_ge(s_const, 3)
            nc.gpsimd.affine_select(out=ident[:, :], in_=ident[:, :], compare_op=ALU.not_equal, fill=1.0, base=0,
                                    pattern=[[-1, 128]], channel_multiplier=1).then_inc(s_const, 1)
            pool.wait_ge(s_const, 4)
            nc.gpsimd.memset(heads2[0:HD, 0:1], 1.0).then_inc(s_const, 1)
            pool.wait_ge(s_const, 5)
            nc.gpsimd.memset(heads2[HD:128, 1:2], 1.0).then_inc(s_const, 1)
            pool.dma_start(cc[:, :, :], d_cc).then_inc(s_cdma, 16)
            pool.dma_start(vec[:, :, :], d_vec).then_inc(s_cdma, 16)
            for j in jobs:
                L, T, ly = j.L, j.T, j.layer
                prev = before[j]
                if prev is not None:
                    pool.wait_ge(*prev.at("done", 1))
                if j.full:
                    pool.dma_start(feats[:, 0:L], d_feats[j.who]).then_inc(j.s("fil"), 16)
                    pool.dma_start(fw1[:, :], d_fw1[ly]).then_inc(j.s("fil"), 16)
                    pool.dma_start(fw2[:, :], d_fw2[ly]).then_inc(j.s("fil"), 16)
                    pool.dma_start(traw[:, 0:j.TW], d_tab[j.who]).then_inc(j.s("tab"), 16)
                    pool.dma_start(dec[:, 0:T, :], d_dec[j.who]).then_inc(j.s("dec"), 16)
                if ly == 0:
                    src = (d_x, d_ctx)[j.who]
                else:
                    src = (d_x1, d_ctx1)[j.who]
                    pool.wait_ge(*[q for q in jobs if q.layer == 0 and q.who == j.who][0].at("stored", 16 * KD))
                pool.dma_start(xb[:, :, 0:L], src).then_inc(j.s("xin"), 16)
                if not j.full:
                    continue
                for o in range(2):
                    if o:
                        pool.wait_ge(*j.at("kgen", 2 * T))
                    pool.dma_start(w3s[:, :, :], d_w3[ly, o]).then_inc(j.s("w3"), 16)
                if j.who == 0:
                    pool.wait_ge(*j.at("fin", 4))
                    pool.dma_start(ropes[:, :, :], d_rope).then_inc(j.s("rope"), 16)
                pool.wait_ge(*j.at("oout", NH * T // 2))
                pool.dma_start(xr[:, :, 0:L], src).then_inc(j.s("xr"), 16)
                dst = d_out if (ly == 1) else (d_x1, d_ctx1)[j.who]
                for d in range(KD):
                    pool.wait_ge(*j.at("xo", d + 1))
                    pool.dma_start(dst[:, d, :], xr[:, d, 0:L]).then_inc(j.s("stored"), 16)

        @block.scalar
        def _(act):
            chain = Chain(act, s_act)

            def split_hi(n, i=0, per=0):
                n += LEAD
                if n >= N_UNITS:
                    return
                act.wait_ge(s_raw[n % RAW], 16 * (n // RAW + 1) + i * (16 * per // RAW))
                if n >= RING:
                    act.wait_ge(s_used, n - RING + 1 + i * per)
                nc.scalar.activation(w_hi[:, n % RING, :], raw[:, n % RAW, :], ACT.Copy).then_inc(s_hi, 1)

            def used(n, i=0, per=0):
                act.wait_ge(s_used, n + 1 + i * per)

            act.wait_ge(s_cdma, 32)
            nc.scalar.activation(cs[:, :, :], cc[:, :, :], ACT.Silu).then_inc(s_act, 1)
            act.wait_ge(s_act, 1)
            chain.n = 1
            chain(nc.scalar.activation(c4[:, :, 0:2], cs[:, :, :], ACT.Copy))
            for n in range(LEAD):
                split_hi(n - LEAD)
            for n in range(RING - LEAD):
                split_hi(n)
            first = RING - LEAD
            loops = (U_MOD - first) // RING
            with act.Fori(0, loops, 1) as i:
                for p in range(RING):
                    split_hi(first + p, i, RING)
            for n in range(first + loops * RING, U_MOD):
                split_hi(n)
            used(U_MOD - 1)
            nc.scalar.activation(mraw[:, :, :].rearrange("p a b -> p (a b)"), ps[:, 7, 0:DEPTH * 96], ACT.Copy).then_inc(s_mraw, 1)

            for j in jobs:
                L, T, Lh, FT, ly, who = j.L, j.T, j.Lh, j.FT, j.layer, j.who
                if j.full:
                    act.wait_ge(*j.at("tab", 16))
                    nc.scalar.activation(tab_hi[:, 0:j.TW], traw[:, 0:j.TW], ACT.Copy).then_inc(j.s("tabh"), 1)
                    act.wait_ge(*j.at("fa", 1))
                    nc.scalar.activation(h1[:, 0:L], arg[:, 0:L], ACT.Sin).then_inc(j.s("fs"), 1)
                    act.wait_ge(*j.at("fa", 2))
                    nc.scalar.activation(h2[0:FHID, 0:L], arg[:, 0:L], ACT.Sin).then_inc(j.s("fs"), 1)
                act.wait_ge(*j.at("xin", 16))
                for k in range(KD):
                    if k >= 2:
                        act.wait_ge(*j.at("msq", k - 1))
                    nc.scalar.activation(sq[:, k % 2, 0:L], xb[:, k, 0:L], ACT.Square).then_inc(j.s("sq"), 1)
                act.wait_ge(*j.at("ms", 1))
                nc.scalar.activation(rs[:, 0:T], ms[:, 0:T], ACT.Sqrt).then_inc(j.s("rt"), 1)
                for k in range(KD):
                    act.wait_ge(*j.at("xt", k + 1))
                    nc.scalar.activation(h_hi[:, k, 0:L], xt[:, k % 2, 0:L], ACT.Identity,
                                         bias=modv[:, ly, k, who:who + 1]).then_inc(j.s("hh"), 1)

                if j.full:
                    act.sem_inc(j.s("eva"), 1)
                    per = 18
                    with act.Fori(0, CB, 1) as i:
                        for ti in range(9):
                            for half in range(2):
                                split_hi(j.u0 + 2 * ti + half, i, per)
                            n = j.u0 + 2 * ti + 1
                            bank = ps[:, 1 if ti == 8 else ti, 0:L]
                            if ti == 0:
                                used(n, i, per)
                                act.wait_ge(*j.at("evd", 2 * i + 1))
                                nc.scalar.activation(ca_s[:, 0:L], bank, ACT.Copy).then_inc(j.s("eva"), 1)
                            elif ti == 3:
                                used(n, i, per)
                                act.wait_ge(*j.at("ya", i + 1))
                                nc.scalar.activation(sza[:, 0:L], bank, ACT.Silu).then_inc(j.s("eva"), 1)
                            elif ti in (4, 5, 6):
                                used(n, i, per)
                                act.wait_ge(*j.at("cv", 3 * i + 1))
                                nc.scalar.activation(pads[:, ti - 3, 1:L + 1], bank, ACT.Copy).then_inc(j.s("eva"), 1)
                            elif ti == 7:
                                used(n, i, per)
                                nc.scalar.activation(szh[:, 0:L], bank, ACT.Silu).then_inc(j.s("eva"), 1)
                            elif ti == 8:
                                used(n, i, per)
                                nc.scalar.activation(zs[:, bass.ds(i, 1), 0:L].rearrange("p o l -> p (o l)"), bank, ACT.Silu)\
                                  .then_inc(j.s("eva"), 1)
                    for r in range(4):
                        for tt in range(T):
                            act.wait_ge(*j.at("kt", r * T + tt + 1))
                            nc.scalar.activation(kp_hi[:, tt, :], kt[:, tt % 2, :], ACT.Copy).then_inc(j.s("kh"), 1)
                            if r * T + tt >= 2:
                                act.wait_ge(*j.at("ksum", r * T + tt - 1))
                            nc.scalar.activation(kab[:, tt % 2, :], kg[:, tt % 2, :], ACT.Abs).then_inc(j.s("kab"), 1)
                        for ft in range(FT):
                            act.wait_ge(*j.at("kf", r * FT + ft + 1))
                            if ft or r:
                                act.wait_ge(*j.at("kuse", r * FT + ft))
                            nc.scalar.activation(e_sb[:, :], ps[:, 2 * ft, :], ACT.Copy).then_inc(j.s("ke"), 1)
                        act.wait_ge(*j.at("kf", (r + 1) * FT))
                        for b in range((T + 1) // 2):
                            act.wait_ge(*j.at("ut", r * (T // 2) + b + 1))
                            nc.scalar.activation(u_hi[:, 2 * b:2 * b + 2, :].rearrange("p a c -> p (a c)"), ps[:, 4 + b, :], ACT.Copy)\
                              .then_inc(j.s("uh"), 1)
                        for ft in range(FT):
                            act.wait_ge(*j.at("uf", r * FT + ft + 1))
                            act.wait_ge(*j.at("kuse", (r + 1) * FT))
                            if ft:
                                act.wait_ge(*j.at("uuse", r * FT + ft))
                            nc.scalar.activation(e_sb[:, :], ps[:, 2 * ft, :], ACT.Copy).then_inc(j.s("ue"), 1)
                            act.wait_ge(*j.at("eo", r * FT + ft + 1))
                            if ft:
                                act.wait_ge(*j.at("yi", r * FT + ft))
                            nc.scalar.activation(y_hi[:, :, :, :].rearrange("p a b c -> p (a b c)"),
                                                 p1[:, :, :, :].rearrange("p a b c -> p (a b c)"), ACT.Copy).then_inc(j.s("yh"), 1)

                uq = j.u0 + (U_AHZ if j.full else 0)
                nt = 6 if j.full else 2
                for ti in range(nt):
                    for half in range(2):
                        split_hi(uq + 2 * ti + half)
                    used(uq + 2 * ti + 1)
                    if ti == 1:
                        nc.scalar.activation(vx[:, j.k0:j.k0 + L], ps[:, 1, 0:L], ACT.Copy).then_inc(j.s("qraw"), 1)
                    else:
                        m = 0 if ti == 0 else ti - 1
                        nc.scalar.activation(qraw[:, m, 0:L], ps[:, ti, 0:L], ACT.Copy).then_inc(j.s("qraw"), 1)
                        act.wait_ge(*j.at("qraw", ti + 1))
                        nc.scalar.activation(qsq[:, m, 0:L], qraw[:, m, 0:L], ACT.Square).then_inc(j.s("qsq"), 1)
                nm = nt - 1
                act.wait_ge(*j.at("ms", 2))
                nc.scalar.activation(rs[:, 0:2 * nm * T], ms[:, 0:2 * nm * T], ACT.Sqrt).then_inc(j.s("rt"), 1)
                act.wait_ge(*j.at("rs", 2))
                nc.scalar.activation(rsx[:, 0:2 * nm * T, :], rs[:, 0:2 * nm * T].rearrange("p (a o) -> p a o", o=1)
                                     .to_broadcast([128, 2 * nm * T, HD]), ACT.Copy).then_inc(j.s("rsx"), 1)
                if not j.full:
                    continue
                act.wait_ge(*j.at("qr", 1))
                for g in range(NKV):
                    rows = slice(64 * g, 64 * g + 64)
                    for half in range(2):
                        nc.scalar.activation(k_hi[64 * half:64 * half + 64, g, 0:j.nk], kx[rows, j.k0:j.k0 + j.nk], ACT.Copy)\
                          .then_inc(j.s("ksp"), 1)
                src = qr if who == 0 else qn[:, 1:5, :]
                for e in range(2):
                    rows = slice(64 * e, 64 * e + 64)
                    nc.scalar.activation(q_hl[rows, e:NH:2, 0:L], src[rows, :, 0:L], ACT.Copy).then_inc(j.s("ksp"), 1)
                act.wait_ge(*j.at("vt", 1))
                nc.scalar.activation(v_hi[:, 0:j.kt, :].rearrange("p a c -> p (a c)"),
                                     ps[:, 0:2, :].rearrange("p a c -> p (a c)")[:, 0:j.nk], ACT.Copy).then_inc(j.s("vh"), 1)

                steps = NH * T

                def exps(s):
                    act.wait_ge(*j.at("mx", s + 1))
                    if s >= 2:
                        act.wait_ge(*j.at("tp", s - 1))
                    b = 2 * (s % 2)
                    nc.scalar.activation(pb[:, s % 2, 0:j.nk], ps[:, b:b + 2, :].rearrange("p a c -> p (a c)")[:, 0:j.nk],
                                         ACT.Exp, bias=nmx[:, s:s + 1], scale=SCALE, accum_out=den[:, s:s + 1])\
                      .then_inc(j.s("ex"), 1)

                def hi_of_p(s):
                    grp, q = s // 2, s % 2
                    act.wait_ge(*j.at("tp", s + 1))
                    if grp >= 2:
                        act.wait_ge(*j.at("pv", grp - 1))
                    nc.scalar.activation(pt_hi[:, grp % 2, 0:j.kt, 128 * q:128 * q + 128],
                                         ps[:, 4:6, :].rearrange("p a c -> p (a c)")[:, 0:j.nk].rearrange("p (a c) -> p a c", c=128),
                                         ACT.Copy).then_inc(j.s("ph"), 1)

                def spread(grp):
                    act.wait_ge(*j.at("rt2", grp + 1))
                    if grp >= 2:
                        act.wait_ge(*j.at("oout", grp - 1))
                    b = 6 + grp % 2
                    nc.scalar.activation(rb[:, grp % 2, :], ps[:, b, 256:512], ACT.Copy).then_inc(j.s("rb"), 1)

                exps(0)
                for s in range(steps):
                    if s + 1 < steps:
                        exps(s + 1)
                    hi_of_p(s)
                    if s % 2 == 1 and s >= 3:
                        spread(s // 2 - 1)
                spread(steps // 2 - 1)

                for n, src in enumerate((ya, vb, zs)):
                    if n == 2:
                        act.wait_ge(*j.at("yc", 1))
                    nc.scalar.activation(b_hi[:, n, :, 0:L], src[:, :, 0:L], ACT.Copy).then_inc(j.s("bh"), 1)
                ug = j.u0 + U_AHZ + U_Q
                act.sem_inc(j.s("sg"), 3)
                with act.Fori(0, KD, 1) as i:
                    for n in range(3):
                        for half in range(2):
                            split_hi(ug + 3 * n + half, i, 9)
                        used(ug + 3 * n + 1, i, 9)
                        act.wait_ge(*j.at("pm", 3 * i + (n + 1)))
                        nc.scalar.activation(sg[:, n, 0:L], ps[:, n, 0:L], ACT.Sigmoid).then_inc(j.s("sg"), 1)
                        split_hi(ug + 3 * n + 2, i, 9)
                for k in range(KD):
                    act.wait_ge(*j.at("mg", k + 1))
                    nc.scalar.activation(h_hi[:, k, 0:L], mg[:, k, 0:L], ACT.Copy).then_inc(j.s("gh"), 1)
                for d in range(KD):
                    for half in range(2):
                        split_hi(ug + U_G + 2 * d + half)

        @block.vector
        def _(dve):
            chain = Chain(dve, s_dve)
            V = nc.vector

            def split_lo(n, i=0, per=0):
                n += LEAD
                if n >= N_UNITS:
                    return
                dve.wait_ge(s_hi, n + 1 + i * per)
                V.tensor_tensor(w_lo[:, n % RING, :], raw[:, n % RAW, :], w_hi[:, n % RING, :].bitcast(f32), ALU.subtract)\
                 .then_inc(s_lo, 1)

            def used(n, i=0, per=0):
                dve.wait_ge(s_used, n + 1 + i * per)

            def rsqrt(n, j, which):
                dve.wait_ge(*j.at("rt", which))
                chain(V.reciprocal(rs[:, 0:n], rs[:, 0:n]))
                chain(V.scalar_tensor_tensor(out=nu[:, 0:n], in0=rs[:, 0:n], scalar=-0.5, in1=ms[:, 0:n], op0=ALU.mult, op1=ALU.mult))
                chain(V.tensor_tensor(nu[:, 0:n], nu[:, 0:n], rs[:, 0:n], ALU.mult))
                V.scalar_tensor_tensor(out=rs[:, 0:n], in0=nu[:, 0:n], scalar=1.5, in1=rs[:, 0:n], op0=ALU.add, op1=ALU.mult)\
                 .then_inc(j.s("rs"), 1)
                dve.wait_ge(*j.at("rs", which))

            dve.wait_ge(s_act, 2)
            V.tensor_tensor(c4[:, :, 2:4], cs[:, :, :], c4[:, :, 0:2].bitcast(f32), ALU.subtract).then_inc(s_c4, 1)
            for n in range(LEAD):
                split_lo(n - LEAD)
            loops = U_MOD // RING
            with dve.Fori(0, loops, 1) as i:
                for p in range(RING):
                    split_lo(p, i, RING)
            for n in range(loops * RING, U_MOD):
                split_lo(n)
            dve.wait_ge(s_mraw, 1)
            mv = modv[:, :, :, :].rearrange("p l t w -> p (l t) w")
            chain(V.tensor_tensor(mv, mraw[:, :, 0:2], mraw[:, :, 2:4], ALU.add))
            for ly in range(DEPTH):
                for w in range(2):
                    chain(V.tensor_tensor(modv[:, ly, :, w], modv[:, ly, :, w], vec[:, ly, V_BM:V_BM + 24], ALU.add))
                    chain(V.scalar_tensor_tensor(out=gain[:, ly, :, w], in0=modv[:, ly, KD:2 * KD, w], scalar=1.0,
                                                 in1=vec[:, ly, V_NG:V_NG + KD], op0=ALU.add, op1=ALU.mult))

            for j in jobs:
                L, T, Lh, FT, ly, who = j.L, j.T, j.Lh, j.FT, j.layer, j.who

                def col(c, rows=slice(0, 128)):
                    return vec[rows, ly, c:c + 1]

                if j.full:
                    dve.wait_ge(*j.at("tabh", 1))
                    V.tensor_tensor(tab_lo[:, 0:j.TW], traw[:, 0:j.TW], tab_hi[:, 0:j.TW].bitcast(f32), ALU.subtract)\
                     .then_inc(j.s("tabl"), 1)
                    for layer in range(2):
                        dve.wait_ge(*j.at("fm", layer + 1))
                        hid = slice(0, FHID)
                        if layer == 1:
                            dve.wait_ge(*j.at("fs", 1))
                        chain(V.tensor_scalar(arg[:, 0:L], ps[hid, 6, 0:L], col(V_FIL + 2 * layer, hid), col(V_FIL + 2 * layer + 1, hid),
                                              ALU.add, ALU.mult))
                        chain(V.tensor_scalar(turn[:, 0:L], arg[:, 0:L], 1.0 / 6.283185307179586, MAGIC, ALU.mult, ALU.add))
                        chain(V.tensor_scalar(turn[:, 0:L], turn[:, 0:L], -MAGIC, None, ALU.add))
                        for part in (C1, C2, C3):
                            chain(V.scalar_tensor_tensor(out=arg[:, 0:L], in0=turn[:, 0:L], scalar=-part, in1=arg[:, 0:L],
                                                         op0=ALU.mult, op1=ALU.add))
                        V.tensor_scalar(arg[:, 0:L], arg[:, 0:L], PI_IN, -PI_IN, ALU.min, ALU.max).then_inc(j.s("fa"), 1)
                        dve.wait_ge(*j.at("fa", layer + 1))
                    chain(V.memset(h2[FHID:FHID + 1, 0:L], 1.0))
                dve.wait_ge(*j.at("msd", 1))
                V.tensor_scalar(ms[:, 0:T], ps[:, 5, 0:T], 1.0 / D, EPS, ALU.mult, ALU.add).then_inc(j.s("ms"), 1)
                dve.wait_ge(*j.at("ms", 1))
                rsqrt(T, j, 1)
                dve.wait_ge(*j.at("rbc", 1))
                dve.wait_ge(*j.at("xin", 16))
                for k in range(KD):
                    if k >= 2:
                        dve.wait_ge(*j.at("hl", k - 1))
                    V.scalar_tensor_tensor(out=xt[:, k % 2, 0:L], in0=xb[:, k, 0:L], scalar=gain[:, ly, k, who:who + 1],
                                           in1=ps[:, 4, 0:L], op0=ALU.mult, op1=ALU.mult).then_inc(j.s("xt"), 1)
                    dve.wait_ge(*j.at("hh", k + 1))
                    V.scalar_tensor_tensor(out=h_lo[:, k, 0:L], in0=xt[:, k % 2, 0:L], scalar=modv[:, ly, k, who:who + 1],
                                           in1=h_hi[:, k, 0:L].bitcast(f32), op0=ALU.add, op1=ALU.subtract).then_inc(j.s("hl"), 1)

                if j.full:
                    dve.wait_ge(*j.at("hl", KD))
                    chain(V.memset(pads[:, :, 0:1], 0.0))
                    chain(V.memset(pads[:, :, L + 1:L + 2], 0.0))
                    for name, n in (("evd", 1), ("ya", 1), ("cv", 1)):
                        dve.sem_inc(j.s(name), n)
                    per = 18

                    def taps(kind, i):
                        return [vec[:, ly, bass.ds(i + (V_CONV + (3 * kind + t) * CB), 1)] for t in range(3)]

                    def short_conv(kind, i, y, last=None):
                        w0, w1, w2 = taps(kind, i)
                        row = pads[:, kind]
                        chain(V.tensor_scalar(y, row[:, 0:L], w0, None, ALU.mult))
                        chain(V.scalar_tensor_tensor(out=y, in0=row[:, 1:L + 1], scalar=w1, in1=y, op0=ALU.mult, op1=ALU.add))
                        ins = V.scalar_tensor_tensor(out=y, in0=row[:, 2:L + 2], scalar=w2, in1=y, op0=ALU.mult, op1=ALU.add)
                        if last is None:
                            chain(ins)
                        else:
                            ins.then_inc(last, 1)

                    def eva(k, i):
                        dve.wait_ge(*j.at("eva", 7 * i + (k + 1)))

                    with chain.loop(CB, 3 + 2 + 2 + 3) as i:
                        row_of = lambda a: a[:, bass.ds(i, 1), 0:L].rearrange("p o l -> p (o l)")
                        for ti in range(9):
                            for half in range(2):
                                split_lo(j.u0 + 2 * ti + half, i, per)
                            n = j.u0 + 2 * ti + 1
                            if ti == 1:
                                used(n, i, per)
                                eva(1, i)
                                V.tensor_tensor(pads[:, 0, 1:L + 1], ca_s[:, 0:L], ps[:, 1, 0:L], ALU.mult).then_inc(j.s("evd"), 1)
                                dve.wait_ge(*j.at("evd", 2 * i + 2))
                                short_conv(0, i, y1[:, 0:L])
                            elif ti == 2:
                                used(n, i, per)
                                V.tensor_tensor(y1[:, 0:L], y1[:, 0:L], ps[:, 2, 0:L], ALU.mult).then_inc(j.s("evd"), 1)
                                dve.wait_ge(*j.at("evd", 2 * i + 3))
                            elif ti == 3:
                                eva(2, i)
                                V.tensor_tensor(row_of(ya), y1[:, 0:L], sza[:, 0:L], ALU.mult).then_inc(j.s("ya"), 1)
                            elif ti == 4:
                                eva(3, i)
                                short_conv(1, i, row_of(vb), j.s("cv"))
                            elif ti == 5:
                                eva(4, i)
                                short_conv(2, i, x12[:, 0, bass.ds(i, 1), 0:L].rearrange("p o l -> p (o l)"), j.s("cv"))
                            elif ti == 6:
                                eva(5, i)
                                short_conv(3, i, y2[:, 0:L])
                            elif ti == 7:
                                eva(6, i)
                                V.tensor_tensor(x12[:, 1, bass.ds(i, 1), 0:L].rearrange("p o l -> p (o l)"), y2[:, 0:L], szh[:, 0:L],
                                                ALU.mult).then_inc(j.s("cv"), 1)
                    dve.wait_ge(*j.at("cv", 1 + 3 * CB))
                    dve.wait_ge(*j.at("ya", 1 + CB))

                    dve.wait_ge(*j.at("dec", 16))
                    for r in range(4):
                        o, ch = r // 2, r % 2
                        cw = slice(256 * ch, 256 * ch + 256)

                        def kp_low(tt):
                            dve.wait_ge(*j.at("kh", r * T + tt + 1))
                            V.tensor_tensor(kp_lo[:, tt, :], kt[:, tt % 2, :], kp_hi[:, tt, :].bitcast(f32), ALU.subtract)\
                             .then_inc(j.s("kl"), 1)
                            dve.wait_ge(*j.at("kl", r * T + tt + 1))

                        for tt in range(T):
                            dve.wait_ge(*j.at("kgen", r * T + tt + 1))
                            g = kg[:, tt % 2, :]
                            if r * T + tt >= 2:
                                dve.wait_ge(*j.at("kab", r * T + tt - 1))
                            V.tensor_tensor(g.rearrange("p (d c) -> p d c", d=2), ps[:, 6 + tt % 2, :].rearrange("p (d c) -> p d c", d=2),
                                            dec[:, tt:tt + 1, cw].to_broadcast([128, 2, 256]), ALU.mult).then_inc(j.s("kd"), 1)
                            dve.wait_ge(*j.at("kd", r * T + tt + 1))
                            if tt == 0:
                                chain(V.memset(kg[0:1, 0, 256:512], 0.0))
                            chain(V.tensor_tensor(kt[:, tt % 2, 0:256], g[:, 0:256], g[:, 256:512], ALU.add))
                            V.tensor_tensor(kt[:, tt % 2, 256:512], g[:, 0:256], g[:, 256:512], ALU.subtract).then_inc(j.s("kt"), 1)
                            dve.wait_ge(*j.at("kt", r * T + tt + 1))
                            if tt:
                                kp_low(tt - 1)
                        kp_low(T - 1)
                        dve.wait_ge(*j.at("ksum", (r + 1) * T))
                        V.reciprocal(knorm[:, :], ps[:, 5, 0:2]).then_inc(j.s("kn"), 1)
                        dve.wait_ge(*j.at("kn", r + 1))
                        for ft in range(FT):
                            dve.wait_ge(*j.at("ke", r * FT + ft + 1))
                            for sgn, op in enumerate((ALU.add, ALU.subtract)):
                                ins = V.tensor_tensor(kspec[:, ft, sgn, :, :].rearrange("p a c -> p (a c)"), e_sb[:, :],
                                                      ps[:, 2 * ft + 1, :], op)
                                if sgn == 0:
                                    chain(ins)
                                else:
                                    ins.then_inc(j.s("kuse"), 1)
                                    dve.wait_ge(*j.at("kuse", r * FT + ft + 1))
                        for b in range((T + 1) // 2):
                            dve.wait_ge(*j.at("uh", r * (T // 2) + b + 1))
                            V.tensor_tensor(u_lo[:, 2 * b:2 * b + 2, :].rearrange("p a c -> p (a c)"), ps[:, 4 + b, :],
                                            u_hi[:, 2 * b:2 * b + 2, :].rearrange("p a c -> p (a c)").bitcast(f32), ALU.subtract)\
                             .then_inc(j.s("ul"), 1)
                        for ft in range(FT):
                            k = kspec[:, ft]
                            dve.wait_ge(*j.at("ue", r * FT + ft + 1))
                            chain(V.tensor_tensor(uu[:, 0, :, :].rearrange("p a c -> p (a c)"), e_sb[:, :], ps[:, 2 * ft + 1, :], ALU.add))
                            V.tensor_tensor(uu[:, 1, :, :].rearrange("p a c -> p (a c)"), e_sb[:, :], ps[:, 2 * ft + 1, :], ALU.subtract)\
                             .then_inc(j.s("uuse"), 1)
                            dve.wait_ge(*j.at("uuse", r * FT + ft + 1))
                            chain(V.tensor_tensor(p1[:, :, :, :], uu[:, :, :, :], k, ALU.mult))
                            chain(V.tensor_tensor(p2[:, :, 0, :], uu[:, :, 0, :], k[:, :, 1, :], ALU.mult))
                            chain(V.tensor_tensor(p2[:, :, 1, :], uu[:, :, 1, :], k[:, :, 0, :], ALU.mult))
                            chain(V.tensor_tensor(uu[:, :, 0, :], p1[:, :, 0, :], p1[:, :, 1, :], ALU.subtract))
                            chain(V.tensor_tensor(uu[:, :, 1, :], p2[:, :, 0, :], p2[:, :, 1, :], ALU.add))
                            chain(V.tensor_tensor(p1[:, 0, :, :], uu[:, 0, :, :], uu[:, 1, :, :], ALU.add))
                            V.tensor_tensor(p1[:, 1, :, :], uu[:, 0, :, :], uu[:, 1, :, :], ALU.subtract).then_inc(j.s("eo"), 1)
                            dve.wait_ge(*j.at("yh", r * FT + ft + 1))
                            V.tensor_tensor(y_lo[:, :, :, :].rearrange("p a b c -> p (a b c)"),
                                            p1[:, :, :, :].rearrange("p a b c -> p (a b c)"),
                                            y_hi[:, :, :, :].rearrange("p a b c -> p (a b c)").bitcast(f32), ALU.subtract)\
                             .then_inc(j.s("yl"), 1)
                            dve.wait_ge(*j.at("yl", r * FT + ft + 1))
                        dve.wait_ge(*j.at("yi", (r + 1) * FT))
                        for ct in range(2):
                            c = 2 * ch + ct
                            by_parity = lambda a: a.rearrange("p (i two) -> p two i", two=2)
                            z = zt[:, 0:L].rearrange("p (two i) -> p two i", two=2)
                            u_row = by_parity(vb[:, c, 0:L])
                            chain(V.tensor_scalar(z, u_row, col(V_HB + CB * o + c), None, ALU.mult))
                            chain(V.scalar_tensor_tensor(out=z, in0=ps[:, 2 * ct + 4:2 * ct + 6, 0:Lh], scalar=knorm[:, ct:ct + 1],
                                                         in1=z, op0=ALU.mult, op1=ALU.add))
                            ins = V.tensor_tensor(u_row, z, by_parity(x12[:, o, c, 0:L]), ALU.mult)
                            if ct == 0:
                                chain(ins)
                            else:
                                ins.then_inc(j.s("fin"), 1)
                                dve.wait_ge(*j.at("fin", r + 1))

                uq = j.u0 + (U_AHZ if j.full else 0)
                nt = 6 if j.full else 2
                nm = nt - 1
                for n in range(2 * nt):
                    split_lo(uq + n)
                dve.wait_ge(*j.at("msd", 2))
                V.tensor_scalar(ms[:, 0:2 * nm * T], ps[:, 6, 0:2 * nm * T], 1.0 / HD, EPS, ALU.mult, ALU.add).then_inc(j.s("ms"), 1)
                dve.wait_ge(*j.at("ms", 2))
                rsqrt(2 * nm * T, j, 2)
                for m in range(nm):
                    dve.wait_ge(*j.at("qbc", m + 1))
                    dst = kx[:, SEQ:SEQ + L] if (m == 0 and who == 1) else qn[:, m, 0:L]
                    ins = V.scalar_tensor_tensor(out=dst, in0=qraw[:, m, 0:L], scalar=col(V_KG if m == 0 else V_QG),
                                                 in1=ps[:, m % 2, 0:L], op0=ALU.mult, op1=ALU.mult)
                    ins.then_inc(j.s("qn"), 1)
                    dve.wait_ge(*j.at("qn", m + 1))
                if not j.full:
                    dve.sem_inc(j.s("done"), 1)
                    continue
                if who == 0:
                    dve.wait_ge(*j.at("rope", 16))
                    mask = [(p + 16) % 32 for p in range(32)]
                    chain(V.stream_shuffle(qsh[:, :, :], qn[:, :, :], mask))
                    chain(V.tensor_tensor(qn[:, :, :], qn[:, :, :], ropes[:, 0:1, :].to_broadcast([128, 5, SEQ]), ALU.mult))
                    chain(V.tensor_tensor(qsh[:, :, :], qsh[:, :, :], ropes[:, 1:2, :].to_broadcast([128, 5, SEQ]), ALU.mult))
                    chain(V.tensor_tensor(kx[:, 0:SEQ], qn[:, 0, :], qsh[:, 0, :], ALU.add))
                    V.tensor_tensor(qr[:, :, :], qn[:, 1:5, :], qsh[:, 1:5, :], ALU.add).then_inc(j.s("qr"), 1)
                else:
                    V.memset(nu[:, 0:1], 0.0).then_inc(j.s("qr"), 1)
                dve.wait_ge(*j.at("qr", 1))
                for g in range(NKV):
                    rows = slice(64 * g, 64 * g + 64)
                    dve.wait_ge(*j.at("ksp", 2 * g + 2))
                    for half in range(2):
                        V.tensor_tensor(k_lo[64 * half:64 * half + 64, g, 0:j.nk], kx[rows, j.k0:j.k0 + j.nk],
                                        k_hi[rows, g, 0:j.nk].bitcast(f32), ALU.subtract).then_inc(j.s("ksl"), 1)
                src = qr if who == 0 else qn[:, 1:5, :]
                for e in range(2):
                    rows = slice(64 * e, 64 * e + 64)
                    other = slice(64 - 64 * e, 128 - 64 * e)
                    dve.wait_ge(*j.at("ksp", 5 + e))
                    V.tensor_tensor(q_hl[other, e:NH:2, 0:L], src[rows, :, 0:L], q_hl[rows, e:NH:2, 0:L].bitcast(f32), ALU.subtract)\
                     .then_inc(j.s("ksl"), 1)
                dve.wait_ge(*j.at("vh", 1))
                V.tensor_tensor(v_lo[:, 0:j.kt, :].rearrange("p a c -> p (a c)"),
                                ps[:, 0:2, :].rearrange("p a c -> p (a c)")[:, 0:j.nk],
                                v_hi[:, 0:j.kt, :].rearrange("p a c -> p (a c)").bitcast(f32), ALU.subtract).then_inc(j.s("vl"), 1)
                dve.wait_ge(*j.at("vl", 1))

                steps = NH * T

                def maxima(s):
                    dve.wait_ge(*j.at("qk", s + 1))
                    b = 2 * (s % 2)
                    chain(V.tensor_reduce(mx[:, s:s + 1], ps[:, b:b + 2, :].rearrange("p a c -> p (a c)")[:, 0:j.nk], AX.X, ALU.max))
                    V.tensor_scalar(nmx[:, s:s + 1], mx[:, s:s + 1], -SCALE, None, ALU.mult).then_inc(j.s("mx"), 1)

                def lo_of_p(s):
                    grp, q = s // 2, s % 2
                    dve.wait_ge(*j.at("ph", s + 1))
                    V.tensor_tensor(pt_lo[:, grp % 2, 0:j.kt, 128 * q:128 * q + 128],
                                    ps[:, 4:6, :].rearrange("p a c -> p (a c)")[:, 0:j.nk].rearrange("p (a c) -> p a c", c=128),
                                    pt_hi[:, grp % 2, 0:j.kt, 128 * q:128 * q + 128].bitcast(f32), ALU.subtract).then_inc(j.s("pl"), 1)

                def recip(s):
                    dve.wait_ge(*j.at("ex", s + 1))
                    V.reciprocal(rden[:, s:s + 1], den[:, s:s + 1]).then_inc(j.s("rd"), 1)

                def out_of(grp):
                    h, q = grp // (T // 2), grp % (T // 2)
                    g = h // (NH // NKV)
                    rows = slice(64 * g, 64 * g + 64)
                    to = slice(64 * (h % 2), 64 * (h % 2) + 64)
                    dve.wait_ge(*j.at("pv", grp + 1))
                    dve.wait_ge(*j.at("rb", grp + 1))
                    V.tensor_tensor(oT[to, h // 2, 256 * q:256 * q + 256], ps[rows, 6 + grp % 2, 0:256], rb[rows, grp % 2, :], ALU.mult)\
                     .then_inc(j.s("oout"), 1)

                maxima(0)
                for s in range(steps):
                    if s + 1 < steps:
                        maxima(s + 1)
                    recip(s)
                    lo_of_p(s)
                    if s % 2 == 1 and s >= 3:
                        out_of(s // 2 - 1)
                out_of(steps // 2 - 1)
                dve.wait_ge(*j.at("oout", steps // 2))

                V.tensor_tensor(zs[:, :, 0:L], oT[:, :, 0:L], zs[:, :, 0:L], ALU.mult).then_inc(j.s("yc"), 1)
                dve.wait_ge(*j.at("yc", 1))
                for n, src in enumerate((ya, vb, zs)):
                    dve.wait_ge(*j.at("bh", n + 1))
                    V.tensor_tensor(b_lo[:, n, :, 0:L], src[:, :, 0:L], b_hi[:, n, :, 0:L].bitcast(f32), ALU.subtract).then_inc(j.s("bl"), 1)
                ug = j.u0 + U_AHZ + U_Q
                dve.sem_inc(j.s("pm"), 3)
                dve.wait_ge(*j.at("bl", 3))
                with chain.loop(KD, 1) as i:
                    row = mg[:, bass.ds(i, 1), 0:L].rearrange("p o l -> p (o l)")
                    for n in range(3):
                        for q in range(3):
                            split_lo(ug + 3 * n + q, i, 9)
                        used(ug + 3 * n + 2, i, 9)
                        dve.wait_ge(*j.at("sg", 3 * i + (n + 4)))
                        dst = row if n == 0 else tg[:, n - 1, 0:L]
                        V.tensor_tensor(dst, sg[:, n, 0:L], ps[:, 3 + n, 0:L], ALU.mult).then_inc(j.s("pm"), 1)
                        dve.wait_ge(*j.at("pm", 3 * i + (n + 4)))
                        if n == 1:
                            chain(V.tensor_tensor(row, row, tg[:, 0, 0:L], ALU.add))
                        if n == 2:
                            V.tensor_tensor(row, row, tg[:, 1, 0:L], ALU.add).then_inc(j.s("mg"), 1)
                            dve.wait_ge(*j.at("mg", i + 1))
                for k in range(KD):
                    dve.wait_ge(*j.at("gh", k + 1))
                    V.tensor_tensor(h_lo[:, k, 0:L], mg[:, k, 0:L], h_hi[:, k, 0:L].bitcast(f32), ALU.subtract).then_inc(j.s("gl"), 1)
                dve.wait_ge(*j.at("xr", 16))
                for d in range(KD):
                    for half in range(2):
                        split_lo(ug + U_G + 2 * d + half)
                    used(ug + U_G + 2 * d + 1)
                    V.scalar_tensor_tensor(out=xr[:, d, 0:L], in0=ps[:, d % 4, 0:L], scalar=modv[:, ly, 2 * KD + d, who:who + 1],
                                           in1=xr[:, d, 0:L], op0=ALU.mult, op1=ALU.add).then_inc(j.s("xo"), 1)
                dve.wait_ge(*j.at("xo", KD))
                dve.wait_ge(*j.at("stored", 16 * KD))
                dve.sem_inc(j.s("done"), 1)

        @block.tensor
        def _(pe):
            MM = nc.tensor.matmul

            def w_ready(n, i=0, per=0):
                pe.wait_ge(s_lo, n + 1 + i * per)

            def unit(n, out, m_hi, m_lo, first, last, i=0, per=0):
                w_ready(n, i, per)
                for k in range(4):
                    hi = w_hi[:, n % RING, 128 * k:128 * k + 128]
                    lo = w_lo[:, n % RING, 128 * k:128 * k + 128]
                    ins = mm3(out, hi, lo, m_hi(k), m_lo(k), first and k == 0, last and k == 3)
                ins.then_inc(s_used, 1)

            def tile(n, out, a_hi, a_lo, i=0, per=0):
                for half in range(2):
                    unit(n + half, out, lambda k: a_hi(4 * half + k), lambda k: a_lo(4 * half + k), half == 0, half == 1, i, per)

            pe.wait_ge(s_const, 6)
            pe.wait_ge(s_c4, 1)

            def mod_unit(n, col, i=0, per=0):
                w_ready(n, i, per)
                for k in range(4):
                    kk = 4 * (n % 2) + k
                    for part in (w_hi, w_lo):
                        ins = MM(ps[:, 7, col:col + 4], part[:, n % RING, 128 * k:128 * k + 128], c4[:, kk, :],
                                 start=(kk == 0 and part is w_hi), stop=(kk == 7 and part is w_lo))
                ins.then_inc(s_used, 1)

            for n in range(U_MOD):
                mod_unit(n, 4 * (n // 2))

            for j in jobs:
                L, T, Lh, FT, ly, who = j.L, j.T, j.Lh, j.FT, j.layer, j.who
                prev = before[j]
                if prev is not None:
                    pe.wait_ge(*prev.at("done", 1))
                if j.full:
                    pe.wait_ge(*j.at("fil", 48))
                    MM(ps[0:FHID, 6, 0:L], fw1[:, :], feats[:, 0:L], start=True, stop=True).then_inc(j.s("fm"), 1)
                    pe.wait_ge(*j.at("fs", 1))
                    MM(ps[0:FHID, 6, 0:L], fw2[:, :], h1[:, 0:L], start=True, stop=True).then_inc(j.s("fm"), 1)
                for k in range(KD):
                    pe.wait_ge(*j.at("sq", k + 1))
                    for tt in range(T):
                        ins = MM(ps[:, 5, tt:tt + 1], sq[:, k % 2, 128 * tt:128 * tt + 128], ones[:, 0:1], start=(k == 0 and tt == 0),
                                 stop=(k == KD - 1), skip_group_check=True)
                    ins.then_inc(j.s("msd") if k == KD - 1 else j.s("msq"), 1)
                pe.wait_ge(*j.at("rs", 1))
                for tt in range(T):
                    ins = nc.tensor.transpose(ps[:, 4, 128 * tt:128 * tt + 128], rs[:, tt:tt + 1].to_broadcast([128, 128]), ident[:, :])
                ins.then_inc(j.s("rbc"), 1)
                H = lambda k: h_hi[:, k, 0:L]
                Hl = lambda k: h_lo[:, k, 0:L]
                pe.wait_ge(*j.at("hl", KD))

                if j.full:
                    per = 18
                    with pe.Fori(0, CB, 1) as i:
                        for ti in range(9):
                            if ti == 8:
                                pe.wait_ge(*j.at("evd", 2 * i + 2))
                            else:
                                if ti in (1, 2):
                                    pe.wait_ge(*j.at("evd", 2 * i + 1))
                                pe.wait_ge(*j.at("eva", 7 * i + 1 if ti else 7 * i + 1))
                            tile(j.u0 + 2 * ti, ps[:, 1 if ti == 8 else ti, 0:L], H, Hl, i, per)
                    pe.wait_ge(*j.at("eva", 7 * CB + 1))

                    pe.wait_ge(*j.at("tabl", 1))
                    fwd = lambda t, cs_, tt, ft: t[:, cs_ * T * Lh + tt * Lh + 128 * ft:cs_ * T * Lh + tt * Lh + 128 * ft + 128]
                    inv = lambda t, cs_, ft, par: t[:, j.TW // 2 + (cs_ * FT + ft) * L + par * Lh:j.TW // 2 + (cs_ * FT + ft) * L + par * Lh + Lh]

                    def transform(ft, m_hi, m_lo, name):
                        for par in range(2):
                            for cs_ in range(2):
                                out = ps[:, 2 * ft + par, 256 * cs_:256 * cs_ + 256]
                                for a in range(T // 2):
                                    tt = par * (T // 2) + a
                                    ins = mm3(out, fwd(tab_hi, cs_, tt, ft), fwd(tab_lo, cs_, tt, ft), m_hi(tt, cs_), m_lo(tt, cs_),
                                              a == 0, a == T // 2 - 1)
                        ins.then_inc(j.s(name), 1)

                    def magnitudes(r, tt):
                        pe.wait_ge(*j.at("kab", r * T + tt + 1))
                        for d in range(2):
                            for ct in range(2):
                                ins = MM(ps[:, 5, ct:ct + 1], kab[:, tt % 2, 256 * d + 128 * ct:256 * d + 128 * ct + 128], ones[:, 0:1],
                                         start=(tt == 0 and d == 0 and ct == 0), stop=(tt == T - 1 and d == 1), skip_group_check=True)
                        ins.then_inc(j.s("ksum"), 1)

                    pe.wait_ge(*j.at("fs", 2))
                    for r in range(4):
                        o, ch = r // 2, r % 2
                        pe.wait_ge(*j.at("w3", 16 * (o + 1)))
                        for tt in range(T):
                            if r * T + tt >= 2:
                                pe.wait_ge(*j.at("kd", r * T + tt - 1))
                            if r:
                                pe.wait_ge(*j.at("fin", r))
                            MM(ps[:, 6 + tt % 2, :], h2[:, 128 * tt:128 * tt + 128], w3s[:, ch, :], start=True, stop=True)\
                              .then_inc(j.s("kgen"), 1)
                            if tt:
                                magnitudes(r, tt - 1)
                        magnitudes(r, T - 1)
                        pe.wait_ge(*j.at("kl", (r + 1) * T))
                        for ft in range(FT):
                            transform(ft, lambda tt, c: kp_hi[:, tt, 256 * c:256 * c + 256],
                                      lambda tt, c: kp_lo[:, tt, 256 * c:256 * c + 256], "kf")
                        pe.wait_ge(*j.at("kn", r + 1))
                        for b in range((T + 1) // 2):
                            for q in range(2):
                                tt = 2 * b + q
                                par, a = tt // (T // 2), tt % (T // 2)
                                t0 = 256 * a + par
                                for ct in range(2):
                                    ins = nc.tensor.transpose(ps[:, 4 + b, 256 * q + 128 * ct:256 * q + 128 * ct + 128],
                                                              vb[:, 2 * ch + ct, t0:t0 + 255:2], ident[:, :])
                            ins.then_inc(j.s("ut"), 1)
                        pe.wait_ge(*j.at("kuse", (r + 1) * FT))
                        pe.wait_ge(*j.at("ul", (r + 1) * (T // 2)))
                        for ft in range(FT):
                            transform(ft, lambda tt, c: u_hi[:, tt, :], lambda tt, c: u_lo[:, tt, :], "uf")
                        for ft in range(FT):
                            pe.wait_ge(*j.at("yl", r * FT + ft + 1))
                            for ct in range(2):
                                for par in range(2):
                                    for cs_ in range(2):
                                        ins = mm3(ps[:, 4 + 2 * ct + par, 0:Lh], y_hi[:, par, cs_, 128 * ct:128 * ct + 128],
                                                  y_lo[:, par, cs_, 128 * ct:128 * ct + 128], inv(tab_hi, cs_, ft, par),
                                                  inv(tab_lo, cs_, ft, par), ft == 0 and cs_ == 0, ft == FT - 1 and cs_ == 1)
                            ins.then_inc(j.s("yi"), 1)
                    pe.wait_ge(*j.at("fin", 4))

                uq = j.u0 + (U_AHZ if j.full else 0)
                nt = 6 if j.full else 2
                for ti in range(nt):
                    tile(uq + 2 * ti, ps[:, ti, 0:L], H, Hl)
                nm = nt - 1
                for m in range(nm):
                    pe.wait_ge(*j.at("qsq", m + 1))
                    for tt in range(T):
                        c = 2 * (m * T + tt)
                        ins = MM(ps[:, 6, c:c + 2], qsq[:, m, 128 * tt:128 * tt + 128], heads2[:, :], start=True, stop=True)
                ins.then_inc(j.s("msd"), 1)
                pe.wait_ge(*j.at("rsx", 1))
                pe.wait_ge(*j.at("qraw", nt))
                for m in range(nm):
                    if m >= 2:
                        pe.wait_ge(*j.at("qn", m - 1))
                    for tt in range(T):
                        c = 2 * (m * T + tt)
                        ins = nc.tensor.transpose(ps[:, m % 2, 128 * tt:128 * tt + 128],
                                                  rsx[:, c:c + 2, :].rearrange("p a c -> p (a c)"), ident[:, :])
                    ins.then_inc(j.s("qbc"), 1)
                if not j.full:
                    continue
                pe.wait_ge(*j.at("qn", nm))
                for t in range(j.kt):
                    ins = nc.tensor.transpose(ps[:, t // 4, 128 * (t % 4):128 * (t % 4) + 128],
                                              vx[:, j.k0 + 128 * t:j.k0 + 128 * t + 128], ident[:, :])
                ins.then_inc(j.s("vt"), 1)
                pe.wait_ge(*j.at("vl", 1))
                pe.wait_ge(*j.at("ksl", 6))

                steps = NH * T

                def scores(s):
                    h, q = s // T, s % T
                    g = h // (NH // NKV)
                    if s >= 2:
                        pe.wait_ge(*j.at("ex", s - 1))
                    lhs = q_hl[:, h, 128 * q:128 * q + 128]
                    for b, (k0, k1) in enumerate(((0, min(512, j.nk)), (512, j.nk))):
                        if k1 <= k0:
                            continue
                        out = ps[:, 2 * (s % 2) + b, 0:k1 - k0]
                        MM(out, lhs, k_hi[:, g, k0:k1], start=True, stop=False)
                        ins = MM(out, lhs, k_lo[:, g, k0:k1], start=False, stop=True)
                    ins.then_inc(j.s("qk"), 1)

                def transposes(s):
                    pe.wait_ge(*j.at("ex", s + 1))
                    if s >= 1:
                        pe.wait_ge(*j.at("pl", s))
                    for t in range(j.kt):
                        ins = nc.tensor.transpose(ps[:, 4 + t // 4, 128 * (t % 4):128 * (t % 4) + 128],
                                                  pb[:, s % 2, 128 * t:128 * t + 128], ident[:, :])
                    ins.then_inc(j.s("tp"), 1)

                def values(grp):
                    bank = 6 + grp % 2
                    if grp >= 2:
                        pe.wait_ge(*j.at("oout", grp - 1))
                    pe.wait_ge(*j.at("pl", 2 * grp + 2))
                    pe.wait_ge(*j.at("rd", 2 * grp + 2))
                    for q in range(2):
                        s = 2 * grp + q
                        ins = nc.tensor.transpose(ps[:, bank, 256 + 128 * q:256 + 128 * q + 128],
                                                  rden[:, s:s + 1].to_broadcast([128, 128]), ident[:, :])
                    ins.then_inc(j.s("rt2"), 1)
                    pe.wait_ge(*j.at("rb", grp + 1))
                    for t in range(j.kt):
                        ins = mm3(ps[:, bank, 0:256], v_hi[:, t, :], v_lo[:, t, :], pt_hi[:, grp % 2, t, :], pt_lo[:, grp % 2, t, :],
                                  t == 0, t == j.kt - 1)
                    ins.then_inc(j.s("pv"), 1)

                scores(0)
                for s in range(steps):
                    if s + 1 < steps:
                        scores(s + 1)
                    transposes(s)
                    if s % 2 == 1 and s >= 3:
                        values(s // 2 - 1)
                values(steps // 2 - 1)

                ug = j.u0 + U_AHZ + U_Q
                pe.wait_ge(*j.at("bl", 3))
                with pe.Fori(0, KD, 1) as i:
                    for n in range(3):
                        pe.wait_ge(*j.at("sg", 3 * i + (n + 1)))
                        tile(ug + 3 * n, ps[:, n, 0:L], H, Hl, i, 9)
                        pe.wait_ge(*j.at("pm", 3 * i + (n + 1)))
                        unit(ug + 3 * n + 2, ps[:, 3 + n, 0:L], lambda k: b_hi[:, n, k, 0:L], lambda k: b_lo[:, n, k, 0:L], True, True, i, 9)
                pe.wait_ge(*j.at("gl", KD))
                for d in range(KD):
                    if d >= 4:
                        pe.wait_ge(*j.at("xo", d - 3))
                    tile(ug + U_G + 2 * d, ps[:, d % 4, 0:L], H, Hl)


def _tables(L):
    import math
    import numpy as np
    f = np.float32
    order = np.concatenate([np.arange(0, L, 2), np.arange(1, L, 2)])
    T, Lh = L // 128, L // 2
    FT = Lh // 128

    def linspace(a, b, n):
        s = np.arange(n, dtype=f) / f(n - 1)
        out = f(a) * (f(1) - s) + f(b) * s
        out[-1] = f(b)
        return out

    t = linspace(0.0, 1.0, L)
    bands = linspace(1e-4, 15, 16)
    w = f(2.0 * math.pi / L) * np.arange(L, dtype=f)[:, None]
    wb = (w * bands).astype(f).astype(np.float64)
    feats = np.concatenate([t[:, None], np.cos(wb), np.sin(wb)], axis=1).astype(f)
    lo, hi = math.log(1e-2) / 1.5, math.log(1e-2) / 0.3
    deltas = np.abs(linspace(lo, hi, WB))
    dec = np.exp((-t[:, None] * deltas).astype(f).astype(np.float64)).astype(f)
    theta = 2 * np.pi * (np.arange(Lh) + 0.5) / (2 * L)
    ang = order[:, None] * theta[None, :]
    fwd = np.stack([np.cos(ang), np.sin(ang)])
    fwd = fwd.reshape(2, T, 128, Lh).transpose(2, 0, 1, 3).reshape(128, 2 * T * Lh)
    inv = np.stack([np.cos(ang.T), np.sin(ang.T)]) / L
    inv = inv.reshape(2, FT, 128, L).transpose(2, 0, 1, 3).reshape(128, 2 * FT * L)
    tab = np.concatenate([fwd, inv], axis=1).astype(f)
    return (np.ascontiguousarray(feats[order].T), np.ascontiguousarray(dec[order].reshape(T, 128, WB).transpose(1, 0, 2)), tab)


def _rope():
    import numpy as np
    f = np.float32
    inv = (f(10000.0) ** (-(np.arange(16, dtype=f) / f(16)))).astype(f)
    pos = np.stack([np.repeat(np.arange(SEQ // 64), 64), np.tile(np.arange(64), SEQ // 64)]).astype(f)
    ang = (pos[:, :, None] * inv).astype(f).astype(np.float64)
    out = np.zeros((2, 2, 2, 16, SEQ))
    for a in range(2):
        for half in range(2):
            out[0, a, half] = np.cos(ang[a]).T
            out[1, a, half] = np.sin(ang[a]).T * (1 if half else -1)
    out = out.reshape(2, HD, SEQ)
    return np.ascontiguousarray(np.concatenate([out, out], axis=1).transpose(1, 0, 2)).astype(f)


def kernel(x, c, ctx, c_ctx, norm_g, w_mod, b_mod, w_in, conv_a, conv_h, filt_w1, filt_b1, filt_w2, filt_b2, filt_w3, filt_b3,
           filt_freq, hyena_bias, q_norm_g, k_norm_g, w_branch, w_out):
    import numpy as np
    import concourse.bacc as bacc
    from concourse.bass_utils import run_bass_kernel_spmd as run
    A = np.asarray

    def rows(v):
        return A(v).reshape(-1, 128).T

    def tile_units(w, c0):
        t = A(w)[:, c0:c0 + 128].reshape(-1, 4, 128, 128)
        return list(t.transpose(0, 2, 1, 3).reshape(-1, 128, UW))

    def chunks(v):
        return np.ascontiguousarray(A(v)[0].T.reshape(KD, 128, -1).transpose(1, 0, 2))

    XA, BA, CA, ZA, HV, HX1, HX2, HZ = (512 * n for n in range(8))
    QO, KO, VO, ZO, GO = 4096, 4608, 4736, 4864, 5376
    stream, mod, vec, w3 = [], [], [], []
    for l in range(DEPTH):
        units = []
        for n in range(CB):
            for c0 in (CA, XA, BA, ZA, HV, HX1, HX2, HZ, ZO):
                units += tile_units(w_in[l], c0 + 128 * n)
        for c0 in (KO, VO, QO, QO + 128, QO + 256, QO + 384):
            units += tile_units(w_in[l], c0)
        for d in range(KD):
            for n in range(3):
                units += tile_units(w_in[l], GO + 1024 * n + 128 * d)
                units += tile_units(w_branch[l, n], 128 * d)
        for d in range(KD):
            units += tile_units(w_out[l], 128 * d)
        stream.append(np.stack(units))
        for t in range(24):
            mod += tile_units(w_mod[l], 128 * t)
        v = np.zeros((128, NV), np.float32)
        v[:, V_NG:V_NG + 8] = rows(norm_g[l])
        v[:, V_BM:V_BM + 24] = rows(b_mod[l])
        for kind in range(4):
            for t in range(3):
                taps = A(conv_a)[l, t] if kind == 0 else A(conv_h)[l, t, WB * (kind - 1):WB * kind]
                v[:, V_CONV + (3 * kind + t) * CB:V_CONV + (3 * kind + t + 1) * CB] = rows(taps)
        v[:, V_HB:V_HB + 8] = rows(A(hyena_bias)[l].reshape(-1))
        v[:, V_QG] = np.tile(A(q_norm_g)[l], 2)
        v[:, V_KG] = np.tile(A(k_norm_g)[l], 2)
        v[:FHID, V_FIL] = A(filt_b1)[l]
        v[:FHID, V_FIL + 1] = A(filt_freq)[l, 0]
        v[:FHID, V_FIL + 2] = A(filt_b2)[l]
        v[:FHID, V_FIL + 3] = A(filt_freq)[l, 1]
        vec.append(v)
        w = np.concatenate([A(filt_w3)[l], A(filt_b3)[l][None]]).reshape(FHID + 1, 2, 2, 2, 256)
        w3.append(w.transpose(1, 0, 3, 2, 4).reshape(2, FHID + 1, 2, 512))
    tx, tc = _tables(SEQ), _tables(CTX)
    arrays = dict(
        stream=np.stack(stream), mod=np.stack(mod),
        cc=np.ascontiguousarray(np.stack([rows(A(c)[0]), rows(c_ctx)], axis=2)),
        x=chunks(x), ctx=chunks(A(ctx)), vec=np.ascontiguousarray(np.stack(vec, axis=1)),
        fw1=A(filt_w1), fw2=A(filt_w2), w3=np.ascontiguousarray(np.stack(w3)),
        feats_x=tx[0], feats_c=tc[0], dec_x=tx[1], dec_c=tc[1], tab_x=tx[2], tab_c=tc[2], rope=_rope())
    nc = bacc.Bacc("TRN2", target_bir_lowering=False, num_devices=1)
    f32 = mybir.dt.float32
    a = {k: nc.dram_tensor(f"in_{k}", v.shape, f32, kind="ExternalInput").ap() for k, v in arrays.items()}
    x1 = nc.dram_tensor("x1", (128, KD, SEQ), f32).ap()
    ctx1 = nc.dram_tensor("ctx1", (128, KD, CTX), f32).ap()
    out = nc.dram_tensor("out", (128, KD, SEQ), f32, kind="ExternalOutput").ap()
    build(nc, a["stream"], a["mod"], a["cc"], a["x"], a["ctx"], a["vec"], a["fw1"], a["fw2"], a["w3"],
          (a["feats_x"], a["feats_c"]), (a["dec_x"], a["dec_c"]), (a["tab_x"], a["tab_c"]), a["rope"], x1, ctx1, out)
    r = run(nc, [{f"in_{k}": np.ascontiguousarray(v) for k, v in arrays.items()}], core_ids=[0])
    y = r.results[0]["out"]
    return np.ascontiguousarray(y.transpose(2, 1, 0).reshape(1, SEQ, D))
```

```python
import concourse.bass as bass
from concourse import mybir
from contextlib import ExitStack, contextmanager

D = 1024
KD = D // 128
SEQ, CTX = 512, 256
DEPTH = 2
WB = 512
CB = WB // 128
NH, NKV, HD = 8, 2, 64
FEMB, FHID = 33, 64
EPS = 1e-6
SCALE = HD ** -0.5

UW = 512
RAW, RING, LEAD = 6, 6, 4
U_H, U_A, U_Q, U_Z, U_E, U_G, U_O = 2 * 18, 4 * 8, 12, 4, 8 * 3, 8 * 6, 16
U_QKV = U_H + U_A
U_FIRST = U_QKV + U_Q + U_Z
U_GATES = U_FIRST + U_E
E_EARLY = 2
U_LAYER = U_GATES + U_G + U_O
LOOP = 18
MODS = 6

V_NG, V_BM, V_CONV, V_HB, V_QG, V_KG, V_FIL = 0, 8, 32, 80, 88, 89, 90
NV = 94

C1, C2 = 6.28125, 0.0019350051879882812
C3 = 6.283185307179586 - C1 - C2
MAGIC = 12582912.0
PI_IN = 3.1415925


def build(nc, d_stream, d_mod, d_cc, d_x, d_ctx, d_vec, d_fw1, d_fw2, d_w3, d_feats, d_dec, d_tab, d_rope,
          d_x1, d_ctx1, d_out):
    f32, f32r = mybir.dt.float32, mybir.dt.float32r
    ACT, ALU, AX = mybir.ActivationFunctionType, mybir.AluOpType, mybir.AxisListType
    K = 1024
    BASE = 16512

    def at(name, shape, kb, dt=f32):
        return nc.alloc_sbuf_tensor_at(name, shape, dt, offset=BASE + int(kb * K))

    raw = at("raw", [128, RAW, UW], 0)
    w_hi = at("w_hi", [128, RING, UW], 18, f32r)
    w_lo = at("w_lo", [128, RING, UW], 30, f32r)
    ones = at("ones", [128, 128], 42)
    ident = at("ident", [128, 128], 42.5)
    heads2 = at("heads2", [128, 2], 43)
    vec = at("vec", [128, DEPTH, NV], 43.0625)
    modv = at("modv", [128, DEPTH, 24, 2], 43.8125)
    gain = at("gain", [128, DEPTH, KD, 2], 44.25)
    cc = at("cc", [128, KD, 2], 45.125)
    cs = at("cs", [128, KD, 2], 45.1875)
    ms = at("ms", [128, 10 * 4], 45.375)
    rs = at("rs", [128, 10 * 4], 45.5625)
    nu = at("nu", [128, 10 * 4], 45.75)
    den = at("den", [128, 32], 45.9375)
    rden = at("rden", [128, 32], 46.0625)
    nmx = at("nmx", [128, 32], 46.1875)
    mx = at("mx", [128, 32], 46.3125)
    knorm = at("knorm", [128, 2], 46.4375)
    nms = at("nms", [128, 2, 4], 46.5)
    nrs = at("nrs", [128, 2, 4], 46.53125)
    nnu = at("nnu", [128, 2, 4], 46.5625)
    kx = at("kx", [128, SEQ + CTX], 47)
    vx = at("vx", [128, SEQ + CTX], 50)
    ya_hi = [at(f"ya_hi{n}", [128, SEQ], kb, f32r) for n, kb in enumerate((12, 14, 16, 147))]
    h_hi = at("h_hi", [128, KD, SEQ], 53, f32r)
    h_lo = at("h_lo", [128, KD, SEQ], 69, f32r)
    ya = at("ya", [128, CB, SEQ], 85)
    ya_lo = at("ya_lo", [128, CB, SEQ], 85, f32r)
    vb = at("vb", [128, CB, SEQ], 93)
    zs = at("zs", [128, CB, SEQ], 101)
    mw = [at(f"mw{n}", [128, 3 * D], kb) for n, kb in enumerate((53, 65, 97, 145, 157, 195))]
    mrow = at("mrow", [2, 6, 512], 171)
    traw = at("traw", [128, 4096], 191)
    feats = at("feats", [FEMB, SEQ], 85)
    arg = at("arg", [FHID, SEQ], 87)
    turn = at("turn", [FHID, SEQ], 89)
    h1 = at("h1", [FHID, SEQ], 91)
    fw1 = at("fw1", [FEMB, FHID], 93)
    fw2 = at("fw2", [FHID, FHID], 93.5)
    xb = at("xb", [128, KD, SEQ], 125)
    sq = at("sq", [128, 2, 2, SEQ], 109)
    xt = at("xt", [128, 2, 2, SEQ], 117)
    hc_hi = at("hc_hi", [128, KD, CTX], 141, f32r)
    hc_lo = at("hc_lo", [128, KD, CTX], 149, f32r)
    qraw_c = at("qraw_c", [128, 1, CTX], 102)
    qsq_c = at("qsq_c", [128, 1, CTX], 103)
    rsx_c = at("rsx_c", [128, 4, HD], 104)
    x12 = at("x12", [128, 2, CB, SEQ], 109)
    tab_hi = at("tab_hi", [128, 4096], 125, f32r)
    tab_lo = at("tab_lo", [128, 4096], 141, f32r)
    dec = at("dec", [128, 4, WB], 157)
    w3s = at("w3s", [FHID + 1, 2, 512], 165)
    h2 = at("h2", [FHID + 1, SEQ], 169)
    pads = at("pads", [128, 4, SEQ + 8], 171)
    szh = at("szh", [128, SEQ], 184)
    y2 = at("y2", [128, SEQ], 188)
    kspec = at("kspec", [128, 2, 2, 2, 256], 171)
    kp_hi = at("kp_hi", [128, 4, 512], 179, f32r)
    kp_lo = at("kp_lo", [128, 4, 512], 187, f32r)
    u_hi = at("u_hi", [128, 4, 256], 179, f32r)
    u_lo = at("u_lo", [128, 4, 256], 183, f32r)
    y_hi = at("y_hi", [128, 2, 2, 256], 187, f32r)
    y_lo = at("y_lo", [128, 2, 2, 256], 191, f32r)
    uu = at("uu", [128, 2, 2, 256], 195)
    p1 = at("p1", [128, 2, 2, 256], 199)
    p2 = at("p2", [128, 2, 2, 256], 203)
    kg = at("kg", [128, 2, 512], 195)
    kt = at("kt", [128, 2, 512], 199)
    kab = at("kab", [128, 2, 512], 203)
    zt = at("zt", [128, 512], 195)
    e_sb = at("e_sb", [128, 512], 47)
    pa = at("pa", [128, SEQ], 50)
    q_hl = at("q_hl", [128, NH, SEQ], 109, f32r)
    k_hi = at("k_hi", [128, NKV, SEQ + CTX], 125, f32r)
    k_lo = at("k_lo", [128, NKV, SEQ + CTX], 131, f32r)
    v_hi = at("v_hi", [128, 6, 128], 137, f32r)
    v_lo = at("v_lo", [128, 6, 128], 140, f32r)
    ropes = at("ropes", [128, 2, SEQ], 143)
    oT = at("oT", [128, CB, SEQ], 149)
    pt_hi = at("pt_hi", [128, 2, 6, 256], 157, f32r)
    pt_lo = at("pt_lo", [128, 2, 6, 256], 169, f32r)
    pb = at("pb", [128, 2, SEQ + CTX], 181)
    rb = at("rb", [128, 2, 256], 187)
    qraw = at("qraw", [128, 5, SEQ], 157)
    qsq = at("qsq", [128, 5, SEQ], 167)
    rsx = at("rsx", [128, 10 * 4, HD], 167)
    qn = [at(f"qn{m}", [128, SEQ], kb) for m, kb in enumerate((177, 179, 199, 201, 203))]
    qsh = at("qsh", [128, SEQ], 50)
    b_hi = at("b_hi", [128, 2, CB, SEQ], 109, f32r)
    b_lo = at("b_lo", [128, 2, CB, SEQ], 125, f32r)
    mg = at("mg", [128, KD, SEQ], 189)
    te = at("te", [128, SEQ], 205)
    xr = at("xr", [128, KD, SEQ], 173)
    sg = at("sg", [128, 2, SEQ], 157)
    tg = at("tg", [128, 2, SEQ], 161)

    ctx = ExitStack()
    with ctx:
        ps = ctx.enter_context(nc.psum_tensor("ps", [128, 8, 512], f32))

        def sem(name):
            return ctx.enter_context(nc.semaphore(name))

        s_raw = [sem(f"s_raw{b}") for b in range(RAW)]
        s_hi = sem("s_hi")
        s_lo = sem("s_lo")
        s_used = sem("s_used")
        s_cs = sem("s_cs")
        s_act = sem("s_act")
        s_dve = sem("s_dve")
        s_const = sem("s_const")
        s_cdma = sem("s_cdma")
        s_mw = [sem(f"s_mw{b}") for b in range(MODS)]
        s_mused = sem("s_mused")
        s_mrow = sem("s_mrow")
        s_mcol = sem("s_mcol")

        sems, counts = {}, {}

        class Job:

            def __init__(self, name, layer, who, full, first_unit):
                self.name, self.layer, self.who, self.full, self.u0 = name, layer, who, full, first_unit
                self.L = SEQ if who == 0 else CTX
                self.T = self.L // 128
                self.Lh = self.L // 2
                self.FT = self.Lh // 128
                self.TW = 2 * self.L * self.L // 128
                self.nk = SEQ + CTX if who == 0 else CTX
                self.k0 = 0 if who == 0 else SEQ
                self.kt = self.nk // 128
                L, T, FT, full = self.L, self.T, self.FT, self.full
                steps, nt = NH * T, 6 if full else 2
                self.total = dict(xin=16 * (layer == 0 or who == 1), sq=8, msq=7, msd=1, ms=1, nmsd=1, nms=1, rt=1, rs=1, nrt=1, nrs=1, rbc=1, xt=8,  hh=8, hl=8,
                                  qraw=nt, rsx=1, qsq=nt - 1, qn=nt - 1, qbc=nt - 1)
                if full:
                    self.total.update(
                        fil=48, tab=16, dec=16, w3=32, rope=16 * (who == 0), xr=16, stored=16 * KD,
                        tabh=CB, tabl=CB, fm=2, fa=2, fs=2, eva=9 + 18, ze=2, cv=1 + 3 * CB, fva=2 * CB, fvd=2 * CB, pa=CB, ya=CB,
                        kgen=4 * T, kd=4 * T, kt=4 * T, kh=4 * T, kl=4 * T, kab=4 * T, ksum=4 * T, kn=4, kf=4 * FT, ke=4 * FT, kuse=4 * FT,
                        ut=2 * T, uh=2 * T, ul=2 * T, uf=4 * FT, ue=4 * FT, uuse=4 * FT, eo=4 * FT, yh=4 * FT, yl=4 * FT,
                        yi=4 * FT, fin=4, qr=5 * (who == 0), ksp=12, ksl=12, vt=1, vh=1, vl=1,
                        qk=steps, mx=steps, ex=steps, rd=steps, tp=steps, ph=steps, pl=steps,
                        rt2=steps // 2, rb=steps // 2, pv=steps // 2, oout=steps // 2, yc=1, bh=CB + 2, bl=CB + 2, et=KD, em=KD,
                        sg=2 + 2 * KD, pm=2 + 2 * KD, mg=KD, gh=KD, gl=KD, xo=KD)
                self.prefix = "" if full else f"{name}_"
                self.base = {}
                for n, v in self.total.items():
                    key = self.prefix + n
                    if key not in sems:
                        sems[key] = sem(f"s_{key}")
                    self.base[n] = counts.get(key, 0)
                    counts[key] = self.base[n] + v

            def s(self, name):
                assert name in self.total, name
                return sems[self.prefix + name]

            def at(self, name, value):
                return self.s(name), value + self.base[name]

        u = 0
        jobs = []
        for name, layer, who, full in (("c0", 0, 1, True), ("x0", 0, 0, True), ("c1", 1, 1, False), ("x1", 1, 0, True)):
            jobs.append(Job(name, layer, who, full, u))
            u += U_LAYER if full else 4
        N_UNITS = u
        c0, x0, c1, x1_ = jobs
        full_jobs = (c0, x0, x1_)
        before = {c0: None, x0: c0, c1: x0, x1_: x0}
        after = {c0: (x0,), x0: (c1, x1_), x1_: ()}
        x_of = lambda j: xr if j is x1_ else xb
        h_of = lambda j: (hc_hi, hc_lo) if j is c1 else (h_hi, h_lo)

        def scores_at(j, s, k0, k1):
            b = 2 * (s % 2)
            return ps[:, b:b + 2, :].rearrange("p a c -> p (a c)")[:, k0:k1]

        def first_units(j, s):
            weight = [2 if q == 1 else (q + 1) % 2 for q in range(NH * j.T)] if j.who == 0 else [2, 2] + [1] * (NH * j.T - 2)
            assert sum(weight) == U_E - 3 * E_EARLY
            first = 3 * E_EARLY + sum(weight[:s])
            return range(first, first + weight[s])

        def queries_at(j, s):
            m, left = divmod(s - (j.T - 1), 2 * j.T)
            return m + 2 if left == 0 and 0 <= m < 3 else None

        class Chain:

            def __init__(self, eng, s):
                self.eng, self.sem, self.n, self.at = eng, s, 0, 0

            def __call__(self, ins):
                self.n += 1
                ins.then_inc(self.sem, 1)
                self.eng.wait_ge(self.sem, self.at + self.n)

            @contextmanager
            def loop(self, count, steps):
                start = self.n
                with self.eng.Fori(0, count, 1) as i:
                    self.at = i * steps
                    yield i
                    assert self.n - start == steps, (self.n - start, steps)
                self.at = 0
                self.n = start + steps * count

        def mm3(out, hi, lo, m_hi, m_lo, start, stop, shared=False):
            nc.tensor.matmul(out, hi, m_hi, start=start, stop=False, skip_group_check=shared)
            nc.tensor.matmul(out, hi, m_lo, start=False, stop=False, skip_group_check=shared)
            return nc.tensor.matmul(out, lo, m_hi, start=False, stop=stop, skip_group_check=shared)

        block = ctx.enter_context(nc.Block())

        @block.sync
        def _(sp):
            def unit(src, index, n, i=0, per=0):
                b = n % RAW
                if n >= RAW:
                    sp.wait_ge(s_lo, n - RAW + 1 + i * per)
                sp.dma_start(raw[:, b, :], src[bass.ds(index, 1)].rearrange("o p c -> p (o c)")).then_inc(s_raw[b], 16)

            def segment(src, first, n, count):
                done = 0
                if n == 0:
                    for p in range(LOOP):
                        unit(src, first + p, n + p)
                    done = LOOP
                loops = (count - done) // LOOP
                if loops > 1:
                    with sp.Fori(0, loops, 1) as i:
                        for p in range(LOOP):
                            unit(src, i * LOOP + (first + done + p), n + done + p, i, LOOP)
                    done += loops * LOOP
                for p in range(done, count):
                    unit(src, first + p, n + p)

            sp.dma_start(cc[:, :, :], d_cc).then_inc(s_cdma, 16)
            sp.dma_start(vec[:, :, :], d_vec).then_inc(s_cdma, 16)
            for n in range(DEPTH * KD):
                if n >= MODS:
                    sp.wait_ge(s_mused, n - MODS + 1)
                sp.dma_start(mw[n % MODS][:, :], d_mod[n]).then_inc(s_mw[n % MODS], 16)
            for j in jobs:
                if j.full:
                    segment(d_stream[j.layer], 0, j.u0, U_LAYER)
                else:
                    segment(d_stream[j.layer], U_QKV, j.u0, 4)
            for j in full_jobs:
                sp.wait_ge(*j.at("stored", 16 * KD))

        @block.gpsimd
        def _(pool):
            nc.gpsimd.memset(ident[:, :], 0.0).then_inc(s_const, 1)
            nc.gpsimd.memset(ones[:, :], 1.0).then_inc(s_const, 1)
            nc.gpsimd.memset(heads2[:, :], 0.0).then_inc(s_const, 1)
            pool.wait_ge(s_const, 3)
            nc.gpsimd.affine_select(out=ident[:, :], in_=ident[:, :], compare_op=ALU.not_equal, fill=1.0, base=0,
                                    pattern=[[-1, 128]], channel_multiplier=1).then_inc(s_const, 1)
            pool.wait_ge(s_const, 4)
            nc.gpsimd.memset(heads2[0:HD, 0:1], 1.0).then_inc(s_const, 1)
            pool.wait_ge(s_const, 5)
            nc.gpsimd.memset(heads2[HD:128, 1:2], 1.0).then_inc(s_const, 1)

            def source(j):
                return ((d_x, d_ctx), (d_x1, d_ctx1))[j.layer][j.who]

            def start(j):
                L, T, ly, prev = j.L, j.T, j.layer, before[j]
                if prev is not None:
                    pool.wait_ge(*prev.at("mg", KD))
                if j is not x1_:
                    if j is c1:
                        pool.wait_ge(*c0.at("stored", 16 * KD))
                    pool.dma_start(xb[:, :, 0:L], source(j)).then_inc(j.s("xin"), 16)
                if not j.full:
                    return
                pool.dma_start(feats[:, 0:L], d_feats[j.who]).then_inc(j.s("fil"), 16)
                pool.dma_start(fw1[:, :], d_fw1[ly]).then_inc(j.s("fil"), 16)
                pool.dma_start(fw2[:, :], d_fw2[ly]).then_inc(j.s("fil"), 16)
                if prev is not None:
                    pool.wait_ge(*prev.at("gl", KD))
                else:
                    pool.wait_ge(s_mused, DEPTH * KD)
                pool.dma_start(traw[:, 0:j.TW], d_tab[j.who]).then_inc(j.s("tab"), 16)
                pool.dma_start(dec[:, 0:T, :], d_dec[j.who]).then_inc(j.s("dec"), 16)
                pool.dma_start(w3s[:, :, :], d_w3[ly, 0]).then_inc(j.s("w3"), 16)

            start(c0)
            for j in full_jobs:
                L, T, ly = j.L, j.T, j.layer
                pool.wait_ge(*j.at("kgen", 2 * T))
                pool.dma_start(w3s[:, :, :], d_w3[ly, 1]).then_inc(j.s("w3"), 16)
                if j.who == 0:
                    pool.wait_ge(*j.at("fin", 4))
                    pool.dma_start(ropes[:, :, :], d_rope).then_inc(j.s("rope"), 16)
                pool.wait_ge(*j.at("oout", NH * T // 2))
                if j is x1_:
                    pool.wait_ge(*x0.at("stored", 16 * KD))
                pool.dma_start(xr[:, :, 0:L], source(j)).then_inc(j.s("xr"), 16)
                for nx in after[j]:
                    start(nx)
                dst = d_out if (ly == 1) else (d_x1, d_ctx1)[j.who]
                for d in range(KD):
                    pool.wait_ge(*j.at("xo", d + 1))
                    pool.dma_start(dst[:, d, :], xr[:, d, 0:L]).then_inc(j.s("stored"), 16)

        @block.scalar
        def _(act):
            chain = Chain(act, s_act)

            def split_hi(n, i=0, per=0):
                n += LEAD
                if n >= N_UNITS:
                    return
                act.wait_ge(s_raw[n % RAW], 16 * (n // RAW + 1) + i * (16 * per // RAW))
                if n >= RING:
                    act.wait_ge(s_used, n - RING + 1 + i * per)
                nc.scalar.activation(w_hi[:, n % RING, :], raw[:, n % RAW, :], ACT.Copy).then_inc(s_hi, 1)

            def used(n, i=0, per=0):
                act.wait_ge(s_used, n + 1 + i * per)

            def square(j, k):
                if j is x1_:
                    act.wait_ge(*x0.at("xo", k + 1))
                else:
                    act.wait_ge(*j.at("xin", 16))
                if k >= 2:
                    act.wait_ge(*j.at("msq", k - 1))
                nc.scalar.activation(sq[:, j.who, k % 2, 0:j.L], x_of(j)[:, k, 0:j.L], ACT.Square).then_inc(j.s("sq"), 1)

            def sine(j, layer):
                if layer == 1 and before[j] is not None:
                    act.wait_ge(*before[j].at("gl", KD))
                act.wait_ge(*j.at("fa", layer + 1))
                to = h1[:, 0:j.L] if layer == 0 else h2[0:FHID, 0:j.L]
                nc.scalar.activation(to, arg[:, 0:j.L], ACT.Sin).then_inc(j.s("fs"), 1)

            def root(j):
                act.wait_ge(*j.at("nms", 1))
                nc.scalar.activation(nrs[:, j.who, 0:j.T], nms[:, j.who, 0:j.T], ACT.Sqrt).then_inc(j.s("nrt"), 1)

            def modulate(j, k):
                if k == 0 and before[j] is not None and j is not c1:
                    used(before[j].u0 + U_LAYER - 1)
                act.wait_ge(*j.at("xt", k + 1))
                nc.scalar.activation(h_of(j)[0][:, k, 0:j.L], xt[:, j.who, k % 2, 0:j.L], ACT.Identity,
                                     bias=modv[:, j.layer, k, j.who:j.who + 1]).then_inc(j.s("hh"), 1)

            def out_of_psum(j, ti, u, raw_rows, squares):
                L = j.L
                for half in range(2):
                    split_hi(u + 2 * ti + half)
                used(u + 2 * ti + 1)
                if ti == 1:
                    nc.scalar.activation(vx[:, j.k0:j.k0 + L], ps[:, 1, 0:L], ACT.Copy).then_inc(j.s("qraw"), 1)
                else:
                    m = 0 if ti == 0 else ti - 1
                    nc.scalar.activation(raw_rows[:, m, 0:L], ps[:, ti, 0:L], ACT.Copy).then_inc(j.s("qraw"), 1)
                    act.wait_ge(*j.at("qraw", ti + 1))
                    nc.scalar.activation(squares[:, m, 0:L], raw_rows[:, m, 0:L], ACT.Square).then_inc(j.s("qsq"), 1)

            def head_roots(j, n, spread_rows):
                act.wait_ge(*j.at("ms", 1))
                nc.scalar.activation(rs[:, 0:n], ms[:, 0:n], ACT.Sqrt).then_inc(j.s("rt"), 1)
                act.wait_ge(*j.at("rs", 1))
                nc.scalar.activation(spread_rows[:, 0:n, :], rs[:, 0:n].rearrange("p (a o) -> p a o", o=1)
                                     .to_broadcast([128, n, HD]), ACT.Copy).then_inc(j.s("rsx"), 1)

            act.wait_ge(s_cdma, 32)
            nc.scalar.activation(cs[:, :, :], cc[:, :, :], ACT.Silu).then_inc(s_cs, 1)
            sine(c0, 0)
            sine(c0, 1)
            for ly in range(DEPTH):
                if ly == 1:
                    for k in range(KD):
                        square(c0, k)
                    root(c0)
                act.wait_ge(s_mused, KD * (ly + 1))
                if ly:
                    act.wait_ge(s_mcol, ly)
                nc.scalar.activation(mrow[:, :, :], ps[0:2, 0:6, :], ACT.Copy).then_inc(s_mrow, 1)
            for n in range(LEAD):
                split_hi(n - LEAD)

            for j in full_jobs:
                L, T, Lh, FT, ly, who = j.L, j.T, j.Lh, j.FT, j.layer, j.who
                if j is x1_:
                    for k in range(KD):
                        modulate(c1, k)
                for k in range(KD):
                    if j is x1_ and k == KD // 2:
                        for ti in range(2):
                            out_of_psum(c1, ti, c1.u0, qraw_c, qsq_c)
                    modulate(j, k)

                act.sem_inc(j.s("eva"), 9)
                act.wait_ge(*j.at("tab", 16))
                if before[j] is not None:
                    act.wait_ge(*before[j].at("stored", 16 * KD))
                tw = j.TW // CB
                with act.Fori(0, 2, 1) as i:
                    for ti in range(9):
                        sub = ti // 4
                        for half in range(2):
                            split_hi(j.u0 + 2 * ti + half, i, LOOP)
                        used(j.u0 + 2 * ti + 1, i, LOOP)
                        bank = ps[:, ti % 8, 0:L]
                        if ti == 8:
                            nc.scalar.activation(zs[:, bass.ds(i + 2, 1), 0:L].rearrange("p o l -> p (o l)"), bank, ACT.Silu)\
                              .then_inc(j.s("eva"), 1)
                        elif ti % 4 == 3:
                            nc.scalar.activation(szh[:, 0:L], bank, ACT.Silu).then_inc(j.s("eva"), 1)
                        else:
                            act.wait_ge(*j.at("cv", 6 * i + (3 * sub + 1)))
                            nc.scalar.activation(pads[:, 1 + ti % 4, 1:L + 1], bank, ACT.Copy).then_inc(j.s("eva"), 1)
                        if ti in (0, 4):
                            nc.scalar.activation(tab_hi[:, bass.ds(i * (2 * tw) + sub * tw, tw)], traw[:, bass.ds(i * (2 * tw) + sub * tw, tw)],
                                                 ACT.Copy).then_inc(j.s("tabh"), 1)

                if j is x1_:
                    head_roots(c1, 2 * c1.T, rsx_c)

                def gated(r, f):
                    n = j.u0 + U_H + 8 * r + 2 * f
                    for half in range(2):
                        split_hi(n + half)
                    if f == 0:
                        used(n + 1)
                        if r:
                            act.wait_ge(*j.at("ya", r))
                        nc.scalar.activation(pa[:, 0:L], ps[:, 6, 0:L], ACT.Copy).then_inc(j.s("fva"), 1)
                    if f == 3:
                        used(n + 1)
                        act.wait_ge(*j.at("fvd", 2 * r + 2))
                        nc.scalar.activation(pa[:, 0:L], ps[:, 7, 0:L], ACT.Silu).then_inc(j.s("fva"), 1)

                for r in range(4):
                    for tt in range(T):
                        act.wait_ge(*j.at("kt", r * T + tt + 1))
                        nc.scalar.activation(kp_hi[:, tt, :], kt[:, tt % 2, :], ACT.Copy).then_inc(j.s("kh"), 1)
                        if r * T + tt >= 2:
                            act.wait_ge(*j.at("ksum", r * T + tt - 1))
                        nc.scalar.activation(kab[:, tt % 2, :], kg[:, tt % 2, :], ACT.Abs).then_inc(j.s("kab"), 1)
                        if tt == 0:
                            gated(r, 0)
                        if tt == T // 2:
                            gated(r, 1)
                    for ft in range(FT):
                        act.wait_ge(*j.at("kf", r * FT + ft + 1))
                        if ft or r:
                            act.wait_ge(*j.at("kuse", r * FT + ft))
                        nc.scalar.activation(e_sb[:, :], ps[:, 2 * ft, :], ACT.Copy).then_inc(j.s("ke"), 1)
                    act.wait_ge(*j.at("kf", (r + 1) * FT))
                    for b in range((T + 1) // 2):
                        act.wait_ge(*j.at("ut", r * (T // 2) + b + 1))
                        nc.scalar.activation(u_hi[:, 2 * b:2 * b + 2, :].rearrange("p a c -> p (a c)"), ps[:, 4 + b, :], ACT.Copy)\
                          .then_inc(j.s("uh"), 1)
                    gated(r, 2)
                    for ft in range(FT):
                        act.wait_ge(*j.at("uf", r * FT + ft + 1))
                        act.wait_ge(*j.at("kuse", (r + 1) * FT))
                        if ft:
                            act.wait_ge(*j.at("uuse", r * FT + ft))
                        nc.scalar.activation(e_sb[:, :], ps[:, 2 * ft, :], ACT.Copy).then_inc(j.s("ue"), 1)
                        if ft == 0:
                            gated(r, 3)
                        act.wait_ge(*j.at("eo", r * FT + ft + 1))
                        if ft:
                            act.wait_ge(*j.at("yi", r * FT + ft))
                        nc.scalar.activation(y_hi[:, :, :, :].rearrange("p a b c -> p (a b c)"),
                                             p1[:, :, :, :].rearrange("p a b c -> p (a b c)"), ACT.Copy).then_inc(j.s("yh"), 1)

                uq = j.u0 + U_QKV
                nm = 5
                for ti in range(6):
                    out_of_psum(j, ti, uq, qraw, qsq)
                    if ti < CB:
                        act.wait_ge(*j.at("ya", ti + 1))
                        nc.scalar.activation(ya_hi[ti][:, 0:L], ya[:, ti, 0:L], ACT.Copy).then_inc(j.s("bh"), 1)

                def gate_of_attention(n):
                    for half in range(2):
                        split_hi(uq + U_Q + 2 * n + half)
                    used(uq + U_Q + 2 * n + 1)
                    nc.scalar.activation(zs[:, n, 0:L], ps[:, (7, 2)[n], 0:L], ACT.Silu).then_inc(j.s("ze"), 1)

                head_roots(j, 2 * nm * T, rsx)
                gate_of_attention(0)
                gate_of_attention(1)

                def first_branch(e):
                    d, q = e // 3, e % 3
                    split_hi(j.u0 + U_FIRST + e)
                    if q == 1:
                        used(j.u0 + U_FIRST + e)
                        if d:
                            act.wait_ge(*j.at("em", d))
                        nc.scalar.activation(te[:, 0:L], ps[:, 7, 0:L], ACT.Tanh, scale=0.5).then_inc(j.s("et"), 1)

                for e in range(3 * E_EARLY):
                    first_branch(e)
                act.wait_ge(*(j.at("qr", 1) if who == 0 else j.at("qn", 1)))
                for g in range(NKV):
                    rows = slice(64 * g, 64 * g + 64)
                    for half in range(2):
                        nc.scalar.activation(k_hi[64 * half:64 * half + 64, g, 0:j.nk], kx[rows, j.k0:j.k0 + j.nk], ACT.Copy)\
                          .then_inc(j.s("ksp"), 1)

                def queries(m):
                    act.wait_ge(*(j.at("qr", m + 1) if who == 0 else j.at("qn", m + 1)))
                    for e in range(2):
                        rows = slice(64 * e, 64 * e + 64)
                        nc.scalar.activation(q_hl[rows, 2 * (m - 1) + e, 0:L], qn[m][rows, 0:L], ACT.Copy).then_inc(j.s("ksp"), 1)

                queries(1)
                act.wait_ge(*j.at("vt", 1))
                nc.scalar.activation(v_hi[:, 0:j.kt, :].rearrange("p a c -> p (a c)"),
                                     ps[:, 0:2, :].rearrange("p a c -> p (a c)")[:, 0:j.nk], ACT.Copy).then_inc(j.s("vh"), 1)

                steps = NH * T

                def exps(s):
                    act.wait_ge(*j.at("mx", s + 1))
                    if s >= 2:
                        act.wait_ge(*j.at("tp", s - 1))
                    nc.scalar.activation(pb[:, s % 2, 0:j.nk], scores_at(j, s, 0, j.nk),
                                         ACT.Exp, bias=nmx[:, s:s + 1], scale=SCALE, accum_out=den[:, s:s + 1])\
                      .then_inc(j.s("ex"), 1)

                def hi_of_p(s):
                    grp, q = s // 2, s % 2
                    act.wait_ge(*j.at("tp", s + 1))
                    if grp >= 2:
                        act.wait_ge(*j.at("pv", grp - 1))
                    nc.scalar.activation(pt_hi[:, grp % 2, 0:j.kt, 128 * q:128 * q + 128],
                                         ps[:, 4:6, :].rearrange("p a c -> p (a c)")[:, 0:j.nk].rearrange("p (a c) -> p a c", c=128),
                                         ACT.Copy).then_inc(j.s("ph"), 1)

                def spread(grp):
                    act.wait_ge(*j.at("rt2", grp + 1))
                    if grp >= 2:
                        act.wait_ge(*j.at("oout", grp - 1))
                    nc.scalar.activation(rb[:, grp % 2, :], ps[:, 6, 256:512], ACT.Copy).then_inc(j.s("rb"), 1)

                exps(0)
                for s in range(steps):
                    if s % 2 == 1 and s >= 3:
                        spread(s // 2 - 1)
                    hi_of_p(s)
                    if s + 1 < steps:
                        exps(s + 1)
                    if queries_at(j, s - 1):
                        queries(queries_at(j, s - 1))
                    for e in first_units(j, s):
                        first_branch(e)
                spread(steps // 2 - 1)

                for n, src in enumerate((vb, zs)):
                    if n == 1:
                        act.wait_ge(*j.at("yc", 1))
                    nc.scalar.activation(b_hi[:, n, :, 0:L], src[:, :, 0:L], ACT.Copy).then_inc(j.s("bh"), 1)
                ug = j.u0 + U_GATES
                act.sem_inc(j.s("sg"), 2)
                with act.Fori(0, KD, 1) as i:
                    for n in range(2):
                        for half in range(2):
                            split_hi(ug + 3 * n + half, i, 6)
                        used(ug + 3 * n + 1, i, 6)
                        act.wait_ge(*j.at("pm", 2 * i + (n + 1)))
                        nc.scalar.activation(sg[:, n, 0:L], ps[:, n, 0:L], ACT.Tanh, scale=0.5).then_inc(j.s("sg"), 1)
                        split_hi(ug + 3 * n + 2, i, 6)
                for k in range(KD):
                    act.wait_ge(*j.at("mg", k + 1))
                    nc.scalar.activation(h_hi[:, k, 0:L], mg[:, k, 0:L], ACT.Copy, scale=0.5).then_inc(j.s("gh"), 1)
                for d in range(KD):
                    for half in range(2):
                        split_hi(ug + U_G + 2 * d + half)
                    for nx in after[j]:
                        if nx is not x1_:
                            square(nx, d)
                        elif d:
                            square(nx, d - 1)
                        if nx.full and d == 2:
                            sine(nx, 0)
                        if nx.full and d == 5:
                            sine(nx, 1)
                for nx in after[j]:
                    if nx is x1_:
                        square(nx, KD - 1)
                    root(nx)

        @block.vector
        def _(dve):
            chain = Chain(dve, s_dve)
            V = nc.vector

            def split_lo(n, i=0, per=0):
                n += LEAD
                if n >= N_UNITS:
                    return
                dve.wait_ge(s_hi, n + 1 + i * per)
                V.tensor_tensor(w_lo[:, n % RING, :], raw[:, n % RAW, :], w_hi[:, n % RING, :].bitcast(f32), ALU.subtract)\
                 .then_inc(s_lo, 1)

            def used(n, i=0, per=0):
                dve.wait_ge(s_used, n + 1 + i * per)

            def rsqrt(n, rs, ms, nu, ready, done):
                dve.wait_ge(*ready)
                chain(V.reciprocal(rs[:, 0:n], rs[:, 0:n]))
                chain(V.scalar_tensor_tensor(out=nu[:, 0:n], in0=rs[:, 0:n], scalar=-0.5, in1=ms[:, 0:n], op0=ALU.mult, op1=ALU.mult))
                chain(V.tensor_tensor(nu[:, 0:n], nu[:, 0:n], rs[:, 0:n], ALU.mult))
                V.scalar_tensor_tensor(out=rs[:, 0:n], in0=nu[:, 0:n], scalar=1.5, in1=rs[:, 0:n], op0=ALU.add, op1=ALU.mult)\
                 .then_inc(done[0], 1)
                dve.wait_ge(*done)

            def arguments(j, layer):
                L = j.L
                dve.wait_ge(*j.at("fm", layer + 1))
                col = lambda c: vec[0:FHID, j.layer, c:c + 1]
                if layer == 1:
                    dve.wait_ge(*j.at("fs", 1))
                chain(V.tensor_scalar(arg[:, 0:L], ps[0:FHID, 6, 0:L], col(V_FIL + 2 * layer), col(V_FIL + 2 * layer + 1), ALU.add, ALU.mult))
                chain(V.tensor_scalar(turn[:, 0:L], arg[:, 0:L], 1.0 / 6.283185307179586, MAGIC, ALU.mult, ALU.add))
                chain(V.tensor_scalar(turn[:, 0:L], turn[:, 0:L], -MAGIC, None, ALU.add))
                for part in (C1, C2, C3):
                    chain(V.scalar_tensor_tensor(out=arg[:, 0:L], in0=turn[:, 0:L], scalar=-part, in1=arg[:, 0:L],
                                                 op0=ALU.mult, op1=ALU.add))
                V.tensor_scalar(arg[:, 0:L], arg[:, 0:L], PI_IN, -PI_IN, ALU.min, ALU.max).then_inc(j.s("fa"), 1)
                dve.wait_ge(*j.at("fa", layer + 1))

            def norm(j):
                T, w = j.T, j.who
                dve.wait_ge(*j.at("nmsd", 1))
                V.tensor_scalar(nms[:, w, 0:T], ps[:, (5, 7)[w], 0:T], 1.0 / D, EPS, ALU.mult, ALU.add).then_inc(j.s("nms"), 1)
                dve.wait_ge(*j.at("nms", 1))
                rsqrt(T, nrs[:, w], nms[:, w], nnu[:, w], j.at("nrt", 1), j.at("nrs", 1))

            def modulate(j, k):
                L, w, ly = j.L, j.who, j.layer
                if k == 0:
                    dve.wait_ge(*j.at("rbc", 1))
                    if j is not x1_:
                        dve.wait_ge(*j.at("xin", 16))
                if k >= 2:
                    dve.wait_ge(*j.at("hl", k - 1))
                V.scalar_tensor_tensor(out=xt[:, w, k % 2, 0:L], in0=x_of(j)[:, k, 0:L], scalar=gain[:, ly, k, w:w + 1],
                                       in1=ps[:, (4, 7)[w], 0:L], op0=ALU.mult, op1=ALU.mult).then_inc(j.s("xt"), 1)
                if k:
                    modulate_low(j, k - 1)
                if k == KD - 1:
                    modulate_low(j, k)

            def modulate_low(j, k):
                L, w, ly = j.L, j.who, j.layer
                dve.wait_ge(*j.at("hh", k + 1))
                V.scalar_tensor_tensor(out=h_of(j)[1][:, k, 0:L], in0=xt[:, w, k % 2, 0:L], scalar=modv[:, ly, k, w:w + 1],
                                       in1=h_of(j)[0][:, k, 0:L].bitcast(f32), op0=ALU.add, op1=ALU.subtract).then_inc(j.s("hl"), 1)

            def head_norms(j, n):
                dve.wait_ge(*j.at("msd", 1))
                V.tensor_scalar(ms[:, 0:n], ps[:, 5 if j is c1 else 6, 0:n], 1.0 / HD, EPS, ALU.mult, ALU.add).then_inc(j.s("ms"), 1)
                dve.wait_ge(*j.at("ms", 1))
                rsqrt(n, rs, ms, nu, j.at("rt", 1), j.at("rs", 1))

            def head_normed(j, m, rows, bank):
                dve.wait_ge(*j.at("qbc", m + 1))
                L = j.L
                dst = kx[:, SEQ:SEQ + L] if (m == 0 and j.who == 1) else qn[m][:, 0:L]
                c = V_KG if m == 0 else V_QG
                V.scalar_tensor_tensor(out=dst, in0=rows[:, m, 0:L], scalar=vec[:, j.layer, c:c + 1],
                                       in1=ps[:, bank, 0:L], op0=ALU.mult, op1=ALU.mult).then_inc(j.s("qn"), 1)
                dve.wait_ge(*j.at("qn", m + 1))

            dve.wait_ge(s_cdma, 32)
            for layer in range(2):
                arguments(c0, layer)
            chain(V.memset(h2[FHID:FHID + 1, :], 1.0))
            for ly in range(DEPTH):
                if ly == 1:
                    norm(c0)
                dve.wait_ge(s_mcol, ly + 1)
                for w in range(2):
                    chain(V.tensor_tensor(modv[:, ly, :, w], ps[:, 6, 48 * ly + w:48 * ly + 48:2], vec[:, ly, V_BM:V_BM + 24], ALU.add))
                    chain(V.scalar_tensor_tensor(out=gain[:, ly, :, w], in0=modv[:, ly, KD:2 * KD, w], scalar=1.0,
                                                 in1=vec[:, ly, V_NG:V_NG + KD], op0=ALU.add, op1=ALU.mult))
            for n in range(LEAD):
                split_lo(n - LEAD)

            for j in full_jobs:
                L, T, Lh, FT, ly, who = j.L, j.T, j.Lh, j.FT, j.layer, j.who

                def col(c, rows=slice(0, 128)):
                    return vec[rows, ly, c:c + 1]

                if j is x1_:
                    for k in range(KD):
                        modulate(c1, k)
                for k in range(KD):
                    if j is x1_ and k == KD // 2:
                        for n in range(4):
                            split_lo(c1.u0 + n)
                    modulate(j, k)

                if j.full:
                    dve.wait_ge(*j.at("hl", KD))
                    if before[j] is not None:
                        dve.wait_ge(*before[j].at("stored", 16 * KD))
                    if j is x1_:
                        used(c1.u0 + 3)
                    chain(V.memset(pads[:, :, 0:1], 0.0))
                    chain(V.memset(pads[:, :, L + 1:L + 2], 0.0))
                    dve.sem_inc(j.s("cv"), 1)

                    def short_conv(kind, i, y, last=None):
                        w0, w1, w2 = [vec[:, ly, bass.ds(i + (V_CONV + (3 * kind + t) * CB), 1)] for t in range(3)]
                        row = pads[:, kind]
                        chain(V.tensor_scalar(y, row[:, 0:L], w0, None, ALU.mult))
                        chain(V.scalar_tensor_tensor(out=y, in0=row[:, 1:L + 1], scalar=w1, in1=y, op0=ALU.mult, op1=ALU.add))
                        ins = V.scalar_tensor_tensor(out=y, in0=row[:, 2:L + 2], scalar=w2, in1=y, op0=ALU.mult, op1=ALU.add)
                        if last is None:
                            chain(ins)
                        else:
                            ins.then_inc(last, 1)

                    tw = j.TW // CB
                    with chain.loop(2, 2 * (2 + 2 + 3)) as i:
                        for ti in range(9):
                            sub = ti // 4
                            c = i * 2 + sub
                            row_of = lambda a: a[:, bass.ds(c, 1), 0:L].rearrange("p o l -> p (o l)")
                            for half in range(2):
                                split_lo(j.u0 + 2 * ti + half, i, LOOP)
                            if ti in (0, 4):
                                dve.wait_ge(*j.at("tabh", i * 2 + (sub + 1)))
                                part = bass.ds(i * (2 * tw) + sub * tw, tw)
                                V.tensor_tensor(tab_lo[:, part], traw[:, part], tab_hi[:, part].bitcast(f32), ALU.subtract)\
                                 .then_inc(j.s("tabl"), 1)
                            if ti == 8:
                                continue
                            dve.wait_ge(*j.at("eva", 9 * i + (9 + ti + 1)))
                            if ti % 4 == 0:
                                short_conv(1, c, row_of(vb), j.s("cv"))
                            elif ti % 4 == 1:
                                short_conv(2, c, row_of(x12[:, 0]), j.s("cv"))
                            elif ti % 4 == 2:
                                short_conv(3, c, y2[:, 0:L])
                            else:
                                V.tensor_tensor(row_of(x12[:, 1]), y2[:, 0:L], szh[:, 0:L], ALU.mult).then_inc(j.s("cv"), 1)
                    dve.wait_ge(*j.at("cv", 1 + 3 * CB))
                    dve.wait_ge(*j.at("tabl", CB))
                    if j is x1_:
                        head_norms(c1, 2 * c1.T)

                    def gated(r, f):
                        n = j.u0 + U_H + 8 * r + 2 * f
                        for half in range(2):
                            split_lo(n + half)
                        y = ya[:, r, 0:L]
                        if f == 1:
                            used(n + 1)
                            dve.wait_ge(*j.at("fva", 2 * r + 1))
                            V.tensor_tensor(pa[:, 0:L], pa[:, 0:L], ps[:, 7, 0:L], ALU.mult).then_inc(j.s("fvd"), 1)
                            dve.wait_ge(*j.at("fvd", 2 * r + 1))
                            w0, w1, w2 = [col(V_CONV + t * CB + r) for t in range(3)]
                            chain(V.tensor_scalar(y, pa[:, 0:L], w1, None, ALU.mult))
                            chain(V.scalar_tensor_tensor(out=y[:, 1:L], in0=pa[:, 0:L - 1], scalar=w0, in1=y[:, 1:L], op0=ALU.mult, op1=ALU.add))
                            chain(V.scalar_tensor_tensor(out=y[:, 0:L - 1], in0=pa[:, 1:L], scalar=w2, in1=y[:, 0:L - 1], op0=ALU.mult, op1=ALU.add))
                        elif f == 2:
                            used(n + 1)
                            V.tensor_tensor(y, y, ps[:, 6, 0:L], ALU.mult).then_inc(j.s("fvd"), 1)
                            dve.wait_ge(*j.at("fvd", 2 * r + 2))
                        elif f == 3:
                            dve.wait_ge(*j.at("fva", 2 * r + 2))
                            V.tensor_tensor(y, y, pa[:, 0:L], ALU.mult).then_inc(j.s("ya"), 1)

                    dve.wait_ge(*j.at("dec", 16))
                    for r in range(4):
                        o, ch = r // 2, r % 2
                        cw = slice(256 * ch, 256 * ch + 256)

                        def kp_low(tt):
                            dve.wait_ge(*j.at("kh", r * T + tt + 1))
                            V.tensor_tensor(kp_lo[:, tt, :], kt[:, tt % 2, :], kp_hi[:, tt, :].bitcast(f32), ALU.subtract)\
                             .then_inc(j.s("kl"), 1)
                            dve.wait_ge(*j.at("kl", r * T + tt + 1))

                        for tt in range(T):
                            dve.wait_ge(*j.at("kgen", r * T + tt + 1))
                            g = kg[:, tt % 2, :]
                            if r * T + tt >= 2:
                                dve.wait_ge(*j.at("kab", r * T + tt - 1))
                            V.tensor_tensor(g.rearrange("p (d c) -> p d c", d=2), ps[:, tt, :].rearrange("p (d c) -> p d c", d=2),
                                            dec[:, tt:tt + 1, cw].to_broadcast([128, 2, 256]), ALU.mult).then_inc(j.s("kd"), 1)
                            dve.wait_ge(*j.at("kd", r * T + tt + 1))
                            if tt == 0:
                                chain(V.memset(kg[0:1, 0, 256:512], 0.0))
                            chain(V.tensor_tensor(kt[:, tt % 2, 0:256], g[:, 0:256], g[:, 256:512], ALU.add))
                            V.tensor_tensor(kt[:, tt % 2, 256:512], g[:, 0:256], g[:, 256:512], ALU.subtract).then_inc(j.s("kt"), 1)
                            dve.wait_ge(*j.at("kt", r * T + tt + 1))
                            if tt:
                                kp_low(tt - 1)
                            if tt == 0:
                                gated(r, 0)
                            if tt == T - 1:
                                gated(r, 1)
                        kp_low(T - 1)
                        if j is x1_ and r == 0:
                            head_normed(c1, 0, qraw_c, 4)
                        dve.wait_ge(*j.at("ksum", (r + 1) * T))
                        V.reciprocal(knorm[:, :], ps[:, 5, 0:2]).then_inc(j.s("kn"), 1)
                        dve.wait_ge(*j.at("kn", r + 1))
                        for ft in range(FT):
                            dve.wait_ge(*j.at("ke", r * FT + ft + 1))
                            for sgn, op in enumerate((ALU.add, ALU.subtract)):
                                ins = V.tensor_tensor(kspec[:, ft, sgn, :, :].rearrange("p a c -> p (a c)"), e_sb[:, :],
                                                      ps[:, 2 * ft + 1, :], op)
                                if sgn == 0:
                                    chain(ins)
                                else:
                                    ins.then_inc(j.s("kuse"), 1)
                                    dve.wait_ge(*j.at("kuse", r * FT + ft + 1))
                        for b in range((T + 1) // 2):
                            dve.wait_ge(*j.at("uh", r * (T // 2) + b + 1))
                            V.tensor_tensor(u_lo[:, 2 * b:2 * b + 2, :].rearrange("p a c -> p (a c)"), ps[:, 4 + b, :],
                                            u_hi[:, 2 * b:2 * b + 2, :].rearrange("p a c -> p (a c)").bitcast(f32), ALU.subtract)\
                             .then_inc(j.s("ul"), 1)
                        gated(r, 2)
                        for ft in range(FT):
                            k = kspec[:, ft]
                            dve.wait_ge(*j.at("ue", r * FT + ft + 1))
                            chain(V.tensor_tensor(uu[:, 0, :, :].rearrange("p a c -> p (a c)"), e_sb[:, :], ps[:, 2 * ft + 1, :], ALU.add))
                            V.tensor_tensor(uu[:, 1, :, :].rearrange("p a c -> p (a c)"), e_sb[:, :], ps[:, 2 * ft + 1, :], ALU.subtract)\
                             .then_inc(j.s("uuse"), 1)
                            dve.wait_ge(*j.at("uuse", r * FT + ft + 1))
                            chain(V.tensor_tensor(p1[:, :, :, :], uu[:, :, :, :], k, ALU.mult))
                            chain(V.tensor_tensor(p2[:, :, 0, :], uu[:, :, 0, :], k[:, :, 1, :], ALU.mult))
                            chain(V.tensor_tensor(p2[:, :, 1, :], uu[:, :, 1, :], k[:, :, 0, :], ALU.mult))
                            chain(V.tensor_tensor(uu[:, :, 0, :], p1[:, :, 0, :], p1[:, :, 1, :], ALU.subtract))
                            chain(V.tensor_tensor(uu[:, :, 1, :], p2[:, :, 0, :], p2[:, :, 1, :], ALU.add))
                            chain(V.tensor_tensor(p1[:, 0, :, :], uu[:, 0, :, :], uu[:, 1, :, :], ALU.add))
                            V.tensor_tensor(p1[:, 1, :, :], uu[:, 0, :, :], uu[:, 1, :, :], ALU.subtract).then_inc(j.s("eo"), 1)
                            if ft == 0:
                                gated(r, 3)
                            dve.wait_ge(*j.at("yh", r * FT + ft + 1))
                            V.tensor_tensor(y_lo[:, :, :, :].rearrange("p a b c -> p (a b c)"),
                                            p1[:, :, :, :].rearrange("p a b c -> p (a b c)"),
                                            y_hi[:, :, :, :].rearrange("p a b c -> p (a b c)").bitcast(f32), ALU.subtract)\
                             .then_inc(j.s("yl"), 1)
                            dve.wait_ge(*j.at("yl", r * FT + ft + 1))
                        dve.wait_ge(*j.at("yi", (r + 1) * FT))
                        for ct in range(2):
                            c = 2 * ch + ct
                            by_parity = lambda a: a.rearrange("p (i two) -> p two i", two=2)
                            z = zt[:, 0:L].rearrange("p (two i) -> p two i", two=2)
                            u_row = by_parity(vb[:, c, 0:L])
                            chain(V.tensor_scalar(z, u_row, col(V_HB + CB * o + c), None, ALU.mult))
                            chain(V.scalar_tensor_tensor(out=z, in0=ps[:, 4 + ct, 0:L].rearrange("p (two i) -> p two i", two=2), scalar=knorm[:, ct:ct + 1],
                                                         in1=z, op0=ALU.mult, op1=ALU.add))
                            ins = V.tensor_tensor(u_row, z, by_parity(x12[:, o, c, 0:L]), ALU.mult)
                            if ct == 0:
                                chain(ins)
                            else:
                                ins.then_inc(j.s("fin"), 1)
                                dve.wait_ge(*j.at("fin", r + 1))

                dve.wait_ge(*j.at("ya", CB))
                uq = j.u0 + U_QKV
                nm = 5
                for n in range(U_Q + U_Z):
                    split_lo(uq + n)
                    if n % 2 == 1 and n // 2 < CB:
                        k = n // 2
                        dve.wait_ge(*j.at("bh", k + 1))
                        V.tensor_tensor(ya_lo[:, k, 0:L], ya[:, k, 0:L], ya_hi[k][:, 0:L].bitcast(f32), ALU.subtract).then_inc(j.s("bl"), 1)
                    if n == U_Q - 1:
                        head_norms(j, 2 * nm * T)

                def first_product(d):
                    used(j.u0 + U_FIRST + 3 * d + 2)
                    dve.wait_ge(*j.at("et", d + 1))
                    V.scalar_tensor_tensor(out=mg[:, d, 0:L], in0=te[:, 0:L], scalar=1.0, in1=ps[:, 7, 0:L], op0=ALU.add, op1=ALU.mult)\
                     .then_inc(j.s("em"), 1)

                def first_branch(e):
                    split_lo(j.u0 + U_FIRST + e)
                    if e % 3 == 2:
                        first_product(e // 3)

                for m in range(2):
                    head_normed(j, m, qraw, m % 2)
                for e in range(3):
                    first_branch(e)
                for m in range(2, nm):
                    head_normed(j, m, qraw, m % 2)
                for e in range(3, 3 * E_EARLY):
                    first_branch(e)

                def rope(m):
                    if who == 1:
                        return
                    dve.wait_ge(*j.at("rope", 16))
                    mask = [(p + 16) % 32 for p in range(32)]
                    chain(V.stream_shuffle(qsh[:, :], qn[m][:, :], mask))
                    chain(V.tensor_tensor(qn[m][:, :], qn[m][:, :], ropes[:, 0, :], ALU.mult))
                    chain(V.tensor_tensor(qsh[:, :], qsh[:, :], ropes[:, 1, :], ALU.mult))
                    V.tensor_tensor(kx[:, 0:SEQ] if m == 0 else qn[m][:, :], qn[m][:, :], qsh[:, :], ALU.add).then_inc(j.s("qr"), 1)
                    dve.wait_ge(*j.at("qr", m + 1))

                def queries(m):
                    for e in range(2):
                        rows = slice(64 * e, 64 * e + 64)
                        other = slice(64 - 64 * e, 128 - 64 * e)
                        h = 2 * (m - 1) + e
                        dve.wait_ge(*j.at("ksp", 4 + h + 1))
                        V.tensor_tensor(q_hl[other, h, 0:L], qn[m][rows, 0:L], q_hl[rows, h, 0:L].bitcast(f32), ALU.subtract)\
                         .then_inc(j.s("ksl"), 1)

                if who == 0:
                    dve.wait_ge(*j.at("vt", 1))
                rope(0)
                rope(1)
                for g in range(NKV):
                    rows = slice(64 * g, 64 * g + 64)
                    dve.wait_ge(*j.at("ksp", 2 * g + 2))
                    for half in range(2):
                        V.tensor_tensor(k_lo[64 * half:64 * half + 64, g, 0:j.nk], kx[rows, j.k0:j.k0 + j.nk],
                                        k_hi[rows, g, 0:j.nk].bitcast(f32), ALU.subtract).then_inc(j.s("ksl"), 1)
                queries(1)
                dve.wait_ge(*j.at("vh", 1))
                V.tensor_tensor(v_lo[:, 0:j.kt, :].rearrange("p a c -> p (a c)"),
                                ps[:, 0:2, :].rearrange("p a c -> p (a c)")[:, 0:j.nk],
                                v_hi[:, 0:j.kt, :].rearrange("p a c -> p (a c)").bitcast(f32), ALU.subtract).then_inc(j.s("vl"), 1)
                dve.wait_ge(*j.at("vl", 1))

                steps = NH * T

                def maxima(s):
                    dve.wait_ge(*j.at("qk", s + 1))
                    chain(V.tensor_reduce(mx[:, s:s + 1], scores_at(j, s, 0, j.nk), AX.X, ALU.max))
                    V.tensor_scalar(nmx[:, s:s + 1], mx[:, s:s + 1], -SCALE, None, ALU.mult).then_inc(j.s("mx"), 1)

                def lo_of_p(s):
                    grp, q = s // 2, s % 2
                    dve.wait_ge(*j.at("ph", s + 1))
                    V.tensor_tensor(pt_lo[:, grp % 2, 0:j.kt, 128 * q:128 * q + 128],
                                    ps[:, 4:6, :].rearrange("p a c -> p (a c)")[:, 0:j.nk].rearrange("p (a c) -> p a c", c=128),
                                    pt_hi[:, grp % 2, 0:j.kt, 128 * q:128 * q + 128].bitcast(f32), ALU.subtract).then_inc(j.s("pl"), 1)

                def recip(s):
                    dve.wait_ge(*j.at("ex", s + 1))
                    V.reciprocal(rden[:, s:s + 1], den[:, s:s + 1]).then_inc(j.s("rd"), 1)

                def out_of(grp):
                    h, q = grp // (T // 2), grp % (T // 2)
                    g = h // (NH // NKV)
                    rows = slice(64 * g, 64 * g + 64)
                    to = slice(64 * (h % 2), 64 * (h % 2) + 64)
                    dve.wait_ge(*j.at("pv", grp + 1))
                    dve.wait_ge(*j.at("rb", grp + 1))
                    V.tensor_tensor(oT[to, h // 2, 256 * q:256 * q + 256], ps[rows, 6, 0:256], rb[rows, grp % 2, :], ALU.mult)\
                     .then_inc(j.s("oout"), 1)

                maxima(0)
                for s in range(steps):
                    if s + 1 < steps:
                        maxima(s + 1)
                    recip(s)
                    lo_of_p(s)
                    if s % 2 == 1 and s >= 3:
                        out_of(s // 2 - 1)
                    if queries_at(j, s):
                        rope(queries_at(j, s))
                    if queries_at(j, s - 1):
                        queries(queries_at(j, s - 1))
                    for e in first_units(j, s):
                        first_branch(e)
                out_of(steps // 2 - 1)
                dve.wait_ge(*j.at("oout", steps // 2))

                dve.wait_ge(*j.at("em", KD))

                for n, src in enumerate((vb, zs)):
                    if n == 1:
                        dve.wait_ge(*j.at("ze", 2))
                        V.tensor_tensor(zs[:, :, 0:L], oT[:, :, 0:L], zs[:, :, 0:L], ALU.mult).then_inc(j.s("yc"), 1)
                        dve.wait_ge(*j.at("yc", 1))
                    dve.wait_ge(*j.at("bh", CB + n + 1))
                    V.tensor_tensor(b_lo[:, n, :, 0:L], src[:, :, 0:L], b_hi[:, n, :, 0:L].bitcast(f32), ALU.subtract).then_inc(j.s("bl"), 1)
                ug = j.u0 + U_GATES
                dve.sem_inc(j.s("pm"), 2)
                dve.wait_ge(*j.at("bl", CB + 2))
                with chain.loop(KD, 1) as i:
                    row = mg[:, bass.ds(i, 1), 0:L].rearrange("p o l -> p (o l)")
                    for n in range(2):
                        for q in range(3):
                            split_lo(ug + 3 * n + q, i, 6)
                        used(ug + 3 * n + 2, i, 6)
                        dve.wait_ge(*j.at("sg", 2 * i + (n + 3)))
                        V.scalar_tensor_tensor(out=tg[:, n, 0:L], in0=sg[:, n, 0:L], scalar=1.0, in1=ps[:, 4 + n, 0:L], op0=ALU.add, op1=ALU.mult)\
                         .then_inc(j.s("pm"), 1)
                        dve.wait_ge(*j.at("pm", 2 * i + (n + 3)))
                        ins = V.tensor_tensor(row, row, tg[:, n, 0:L], ALU.add)
                        if n == 0:
                            chain(ins)
                        else:
                            ins.then_inc(j.s("mg"), 1)
                            dve.wait_ge(*j.at("mg", i + 1))
                for k in range(KD):
                    dve.wait_ge(*j.at("gh", k + 1))
                    V.scalar_tensor_tensor(out=h_lo[:, k, 0:L], in0=mg[:, k, 0:L], scalar=0.5, in1=h_hi[:, k, 0:L].bitcast(f32),
                                           op0=ALU.mult, op1=ALU.subtract).then_inc(j.s("gl"), 1)
                dve.wait_ge(*j.at("xr", 16))
                for d in range(KD):
                    for half in range(2):
                        split_lo(ug + U_G + 2 * d + half)
                    used(ug + U_G + 2 * d + 1)
                    V.scalar_tensor_tensor(out=xr[:, d, 0:L], in0=ps[:, d % 4, 0:L], scalar=modv[:, ly, 2 * KD + d, who:who + 1],
                                           in1=xr[:, d, 0:L], op0=ALU.mult, op1=ALU.add).then_inc(j.s("xo"), 1)
                    for nx in after[j]:
                        if nx.full and d == 1:
                            dve.wait_ge(*j.at("gl", KD))
                            chain(V.memset(h2[FHID:FHID + 1, :], 1.0))
                            arguments(nx, 0)
                        if nx.full and d == 4:
                            arguments(nx, 1)
                for nx in after[j]:
                    norm(nx)

        @block.tensor
        def _(pe):
            MM = nc.tensor.matmul

            def w_ready(n, i=0, per=0):
                pe.wait_ge(s_lo, n + 1 + i * per)

            def unit(n, out, m_hi, m_lo, first, last, i=0, per=0):
                w_ready(n, i, per)
                for k in range(4):
                    hi = w_hi[:, n % RING, 128 * k:128 * k + 128]
                    lo = w_lo[:, n % RING, 128 * k:128 * k + 128]
                    ins = mm3(out, hi, lo, m_hi(k), m_lo(k), first and k == 0, last and k == 3)
                ins.then_inc(s_used, 1)

            def tile(n, out, a_hi, a_lo, i=0, per=0):
                for half in range(2):
                    unit(n + half, out, lambda k: a_hi(4 * half + k), lambda k: a_lo(4 * half + k), half == 0, half == 1, i, per)

            def hidden(j, layer):
                if layer == 0:
                    pe.wait_ge(*j.at("fil", 48))
                    MM(ps[0:FHID, 6, 0:j.L], fw1[:, :], feats[:, 0:j.L], start=True, stop=True).then_inc(j.s("fm"), 1)
                else:
                    pe.wait_ge(*j.at("fs", 1))
                    MM(ps[0:FHID, 6, 0:j.L], fw2[:, :], h1[:, 0:j.L], start=True, stop=True).then_inc(j.s("fm"), 1)

            def squares(j, k):
                pe.wait_ge(*j.at("sq", k + 1))
                for tt in range(j.T):
                    ins = MM(ps[:, (5, 7)[j.who], tt:tt + 1], sq[:, j.who, k % 2, 128 * tt:128 * tt + 128], ones[:, 0:1],
                             start=(k == 0 and tt == 0), stop=(k == KD - 1), skip_group_check=True)
                ins.then_inc(j.s("nmsd") if k == KD - 1 else j.s("msq"), 1)

            def norm_rows(j):
                pe.wait_ge(*j.at("nrs", 1))
                for tt in range(j.T):
                    ins = nc.tensor.transpose(ps[:, (4, 7)[j.who], 128 * tt:128 * tt + 128],
                                              nrs[:, j.who, tt:tt + 1].to_broadcast([128, 128]), ident[:, :])
                ins.then_inc(j.s("rbc"), 1)

            def head_squares(j, nm, squares, bank):
                for m in range(nm):
                    pe.wait_ge(*j.at("qsq", m + 1))
                    for tt in range(j.T):
                        c = 2 * (m * j.T + tt)
                        ins = MM(ps[:, bank, c:c + 2], squares[:, m, 128 * tt:128 * tt + 128], heads2[:, :], start=True, stop=True)
                ins.then_inc(j.s("msd"), 1)

            def head_rows(j, m, rows, bank):
                for tt in range(j.T):
                    c = 2 * (m * j.T + tt)
                    ins = nc.tensor.transpose(ps[:, bank, 128 * tt:128 * tt + 128],
                                              rows[:, c:c + 2, :].rearrange("p a c -> p (a c)"), ident[:, :])
                ins.then_inc(j.s("qbc"), 1)

            pe.wait_ge(s_const, 6)
            pe.wait_ge(s_cs, 1)
            for n in range(DEPTH * KD):
                ly, k = n // KD, n % KD
                pe.wait_ge(s_mw[n % MODS], 16 * (n // MODS + 1))
                if n == KD:
                    pe.wait_ge(s_mrow, 1)
                for b in range(6):
                    ins = MM(ps[0:2, b, :], cs[:, k, :], mw[n % MODS][:, 512 * b:512 * b + 512], start=(k == 0), stop=(k == KD - 1))
                ins.then_inc(s_mused, 1)
                if k == KD - 1:
                    if ly == 0:
                        pe.wait_ge(*c0.at("fa", 2))
                    else:
                        squares(c0, KD - 1)
                        norm_rows(c0)
                    pe.wait_ge(s_mrow, ly + 1)
                    for t in range(24):
                        ins = nc.tensor.transpose(ps[:, 6, 48 * ly + 2 * t:48 * ly + 2 * t + 2],
                                                  mrow[:, t // 4, 128 * (t % 4):128 * (t % 4) + 128], ident[0:2, 0:2])
                    ins.then_inc(s_mcol, 1)
                if n == 2:
                    hidden(c0, 0)
                if n == 5:
                    hidden(c0, 1)
                if KD <= n < 2 * KD - 1:
                    squares(c0, n - KD)

            for j in full_jobs:
                L, T, Lh, FT, ly, who = j.L, j.T, j.Lh, j.FT, j.layer, j.who
                H = lambda k: h_hi[:, k, 0:L]
                Hl = lambda k: h_lo[:, k, 0:L]
                if j is x1_:
                    pe.wait_ge(*c1.at("hl", KD))
                    for ti in range(2):
                        tile(c1.u0 + 2 * ti, ps[:, ti, 0:CTX], lambda k: hc_hi[:, k, 0:CTX], lambda k: hc_lo[:, k, 0:CTX])
                    pe.wait_ge(*c1.at("qraw", 2))
                pe.wait_ge(*j.at("fs", 2))
                pe.wait_ge(*j.at("hl", KD // 2))

                if j.full:
                    with pe.Fori(0, 2, 1) as i:
                        for ti in range(9):
                            pe.wait_ge(*j.at("eva", 9 * i + (9, 2, 3, 4, 5, 6, 7, 8, 10)[ti]))
                            for half in range(2):
                                if ti == 0 and half == 1:
                                    pe.wait_ge(*j.at("hl", KD))
                                unit(j.u0 + 2 * ti + half, ps[:, ti % 8, 0:L], lambda k: H(4 * half + k), lambda k: Hl(4 * half + k),
                                     half == 0, half == 1, i, LOOP)
                    pe.wait_ge(*j.at("eva", 9 + 18))
                    if j is x1_:
                        head_squares(c1, 1, qsq_c, 5)
                        pe.wait_ge(*c1.at("ms", 1))

                    def gated(r, f):
                        if f in (0, 1) and r:
                            pe.wait_ge(*j.at("fvd" if f == 0 else "fva", 2 * r))
                        if f in (2, 3):
                            pe.wait_ge(*j.at("fva" if f == 2 else "fvd", 2 * r + 1))
                        tile(j.u0 + U_H + 8 * r + 2 * f, ps[:, 6 + f % 2, 0:L], H, Hl)

                    pe.wait_ge(*j.at("tabl", CB))
                    fwd = lambda t, cs_, tt, ft: t[:, cs_ * T * Lh + tt * Lh + 128 * ft:cs_ * T * Lh + tt * Lh + 128 * ft + 128]
                    inv = lambda t, cs_, ft, par: t[:, j.TW // 2 + (cs_ * FT + ft) * L + par * Lh:j.TW // 2 + (cs_ * FT + ft) * L + par * Lh + Lh]

                    def transform(ft, m_hi, m_lo, name):
                        for par in range(2):
                            for cs_ in range(2):
                                out = ps[:, 2 * ft + par, 256 * cs_:256 * cs_ + 256]
                                for a in range(T // 2):
                                    tt = par * (T // 2) + a
                                    ins = mm3(out, fwd(tab_hi, cs_, tt, ft), fwd(tab_lo, cs_, tt, ft), m_hi(tt, cs_), m_lo(tt, cs_),
                                              a == 0, a == T // 2 - 1)
                        ins.then_inc(j.s(name), 1)

                    def magnitudes(r, tt):
                        pe.wait_ge(*j.at("kab", r * T + tt + 1))
                        for d in range(2):
                            for ct in range(2):
                                ins = MM(ps[:, 5, ct:ct + 1], kab[:, tt % 2, 256 * d + 128 * ct:256 * d + 128 * ct + 128], ones[:, 0:1],
                                         start=(tt == 0 and d == 0 and ct == 0), stop=(tt == T - 1 and d == 1), skip_group_check=True)
                        ins.then_inc(j.s("ksum"), 1)

                    for r in range(4):
                        o, ch = r // 2, r % 2
                        pe.wait_ge(*j.at("w3", 16 * (o + 1)))
                        if r:
                            pe.wait_ge(*j.at("uuse", r * FT))
                        for tt in range(T):
                            MM(ps[:, tt, :], h2[:, 128 * tt:128 * tt + 128], w3s[:, ch, :], start=True, stop=True)\
                              .then_inc(j.s("kgen"), 1)
                        gated(r, 0)
                        if r:
                            pe.wait_ge(*j.at("fin", r))
                        for tt in range(T):
                            if tt == T // 2:
                                gated(r, 1)
                            magnitudes(r, tt)
                        if j is x1_ and r == 0:
                            pe.wait_ge(*c1.at("rsx", 1))
                            head_rows(c1, 0, rsx_c, 4)
                            pe.wait_ge(*c1.at("qn", 1))
                        pe.wait_ge(*j.at("kl", (r + 1) * T))
                        for ft in range(FT):
                            transform(ft, lambda tt, c: kp_hi[:, tt, 256 * c:256 * c + 256],
                                      lambda tt, c: kp_lo[:, tt, 256 * c:256 * c + 256], "kf")
                        pe.wait_ge(*j.at("kn", r + 1))
                        for b in range((T + 1) // 2):
                            for q in range(2):
                                tt = 2 * b + q
                                par, a = tt // (T // 2), tt % (T // 2)
                                t0 = 256 * a + par
                                for ct in range(2):
                                    ins = nc.tensor.transpose(ps[:, 4 + b, 256 * q + 128 * ct:256 * q + 128 * ct + 128],
                                                              vb[:, 2 * ch + ct, t0:t0 + 255:2], ident[:, :])
                            ins.then_inc(j.s("ut"), 1)
                        gated(r, 2)
                        pe.wait_ge(*j.at("kuse", (r + 1) * FT))
                        pe.wait_ge(*j.at("ul", (r + 1) * (T // 2)))
                        for ft in range(FT):
                            transform(ft, lambda tt, c: u_hi[:, tt, :], lambda tt, c: u_lo[:, tt, :], "uf")
                        gated(r, 3)
                        for ft in range(FT):
                            pe.wait_ge(*j.at("yl", r * FT + ft + 1))
                            for ct in range(2):
                                for par in range(2):
                                    for cs_ in range(2):
                                        ins = mm3(ps[:, 4 + ct, par * Lh:par * Lh + Lh], y_hi[:, par, cs_, 128 * ct:128 * ct + 128],
                                                  y_lo[:, par, cs_, 128 * ct:128 * ct + 128], inv(tab_hi, cs_, ft, par),
                                                  inv(tab_lo, cs_, ft, par), ft == 0 and cs_ == 0 and par == 0,
                                                  ft == FT - 1 and cs_ == 1, shared=True)
                            ins.then_inc(j.s("yi"), 1)
                    pe.wait_ge(*j.at("fin", 4))

                uq = j.u0 + U_QKV
                nm = 5
                for ti in range(6):
                    tile(uq + 2 * ti, ps[:, ti, 0:L], H, Hl)
                pe.wait_ge(*j.at("fvd", 2 * CB))
                head_squares(j, nm, qsq, 6)
                pe.wait_ge(*j.at("fva", 2 * CB))
                tile(uq + U_Q, ps[:, 7, 0:L], H, Hl)
                pe.wait_ge(*j.at("qraw", 6))
                tile(uq + U_Q + 2, ps[:, 2, 0:L], H, Hl)
                pe.wait_ge(*j.at("ze", 1))

                def first_branch(e):
                    d, q = e // 3, e % 3
                    n = j.u0 + U_FIRST + e
                    if q == 2:
                        pe.wait_ge(*j.at("bl", CB))
                        pe.wait_ge(*j.at("et", d + 1))
                        unit(n, ps[:, 7, 0:L], lambda k: ya_hi[k][:, 0:L], lambda k: ya_lo[:, k, 0:L], True, True)
                    else:
                        if d and q == 0:
                            pe.wait_ge(*j.at("em", d))
                        unit(n, ps[:, 7, 0:L], lambda k: H(4 * q + k), lambda k: Hl(4 * q + k), q == 0, q == 1)

                for e in range(2):
                    first_branch(e)
                pe.wait_ge(*j.at("rsx", 1))
                for m in range(nm):
                    if m >= 2:
                        pe.wait_ge(*j.at("qn", m - 1))
                    head_rows(j, m, rsx, m % 2)
                    if m == 1:
                        first_branch(2)
                pe.wait_ge(*j.at("qn", nm))
                for t in range(j.kt):
                    ins = nc.tensor.transpose(ps[:, t // 4, 128 * (t % 4):128 * (t % 4) + 128],
                                              vx[:, j.k0 + 128 * t:j.k0 + 128 * t + 128], ident[:, :])
                ins.then_inc(j.s("vt"), 1)
                for e in range(3, 3 * E_EARLY):
                    first_branch(e)
                pe.wait_ge(*j.at("vl", 1))
                pe.wait_ge(*j.at("ksl", 4))

                pe.wait_ge(*j.at("ze", 2))
                steps = NH * T

                def scores(s):
                    h, q = s // T, s % T
                    g = h // (NH // NKV)
                    if s >= 2:
                        pe.wait_ge(*j.at("ex", s - 1))
                    if q == 0:
                        pe.wait_ge(*j.at("ksl", 4 + h + 1 + (h + 1) % 2))
                    lhs = q_hl[:, h, 128 * q:128 * q + 128]
                    for k0, k1 in ((0, min(512, j.nk)), (512, j.nk)):
                        if k1 <= k0:
                            continue
                        out = scores_at(j, s, k0, k1)
                        MM(out, lhs, k_hi[:, g, k0:k1], start=True, stop=False)
                        ins = MM(out, lhs, k_lo[:, g, k0:k1], start=False, stop=True)
                    ins.then_inc(j.s("qk"), 1)

                def transposes(s):
                    pe.wait_ge(*j.at("ex", s + 1))
                    if s >= 1:
                        pe.wait_ge(*j.at("pl", s))
                    for t in range(j.kt):
                        ins = nc.tensor.transpose(ps[:, 4 + t // 4, 128 * (t % 4):128 * (t % 4) + 128],
                                                  pb[:, s % 2, 128 * t:128 * t + 128], ident[:, :])
                    ins.then_inc(j.s("tp"), 1)

                def denominators(grp):
                    if grp:
                        pe.wait_ge(*j.at("oout", grp))
                    pe.wait_ge(*j.at("rd", 2 * grp + 2))
                    for q in range(2):
                        s = 2 * grp + q
                        ins = nc.tensor.transpose(ps[:, 6, 256 + 128 * q:256 + 128 * q + 128],
                                                  rden[:, s:s + 1].to_broadcast([128, 128]), ident[:, :])
                    ins.then_inc(j.s("rt2"), 1)

                def values(grp):
                    pe.wait_ge(*j.at("pl", 2 * grp + 2))
                    pe.wait_ge(*j.at("rb", grp + 1))
                    for t in range(j.kt):
                        ins = mm3(ps[:, 6, 0:256], v_hi[:, t, :], v_lo[:, t, :], pt_hi[:, grp % 2, t, :], pt_lo[:, grp % 2, t, :],
                                  t == 0, t == j.kt - 1)
                    ins.then_inc(j.s("pv"), 1)

                scores(0)
                for s in range(steps):
                    if s % 2 == 1 and s >= 3:
                        denominators(s // 2 - 1)
                    if s + 1 < steps:
                        scores(s + 1)
                    transposes(s)
                    if s % 2 == 1 and s >= 3:
                        values(s // 2 - 1)
                    for e in first_units(j, s):
                        first_branch(e)
                denominators(steps // 2 - 1)
                values(steps // 2 - 1)

                ug = j.u0 + U_GATES
                with pe.Fori(0, KD, 1) as i:
                    for n in range(2):
                        pe.wait_ge(*j.at("sg", 2 * i + (n + 1)))
                        tile(ug + 3 * n, ps[:, n, 0:L], H, Hl, i, 6)
                        pe.wait_ge(*j.at("pm", 2 * i + (n + 1)))
                        pe.wait_ge(*j.at("bl", CB + n + 1))
                        unit(ug + 3 * n + 2, ps[:, 4 + n, 0:L], lambda k: b_hi[:, n, k, 0:L], lambda k: b_lo[:, n, k, 0:L], True, True, i, 6)
                pe.wait_ge(*j.at("mg", KD))
                for d in range(KD):
                    if d >= 4:
                        pe.wait_ge(*j.at("xo", d - 3))
                    for half in range(2):
                        if d == 0:
                            pe.wait_ge(*j.at("gl", 4 * half + 4))
                        unit(ug + U_G + 2 * d + half, ps[:, d % 4, 0:L], lambda k: H(4 * half + k), lambda k: Hl(4 * half + k),
                             half == 0, half == 1)
                    for nx in after[j]:
                        if nx.full and d == 0:
                            hidden(nx, 0)
                        if nx.full and d == 3:
                            hidden(nx, 1)
                        if nx is not x1_:
                            squares(nx, d)
                        elif d:
                            squares(nx, d - 1)
                for nx in after[j]:
                    if nx is x1_:
                        squares(nx, KD - 1)
                for nx in after[j]:
                    norm_rows(nx)


def _tables(L):
    import math
    import numpy as np
    f = np.float32
    order = np.concatenate([np.arange(0, L, 2), np.arange(1, L, 2)])
    T, Lh = L // 128, L // 2
    FT = Lh // 128

    def linspace(a, b, n):
        s = np.arange(n, dtype=f) / f(n - 1)
        out = f(a) * (f(1) - s) + f(b) * s
        out[-1] = f(b)
        return out

    t = linspace(0.0, 1.0, L)
    bands = linspace(1e-4, 15, 16)
    w = f(2.0 * math.pi / L) * np.arange(L, dtype=f)[:, None]
    wb = (w * bands).astype(f).astype(np.float64)
    feats = np.concatenate([t[:, None], np.cos(wb), np.sin(wb)], axis=1).astype(f)
    lo, hi = math.log(1e-2) / 1.5, math.log(1e-2) / 0.3
    deltas = np.abs(linspace(lo, hi, WB))
    dec = np.exp((-t[:, None] * deltas).astype(f).astype(np.float64)).astype(f)
    theta = 2 * np.pi * (np.arange(Lh) + 0.5) / (2 * L)
    ang = order[:, None] * theta[None, :]
    fwd = np.stack([np.cos(ang), np.sin(ang)])
    fwd = fwd.reshape(2, T, 128, Lh).transpose(2, 0, 1, 3).reshape(128, 2 * T * Lh)
    inv = np.stack([np.cos(ang.T), np.sin(ang.T)]) / L
    inv = inv.reshape(2, FT, 128, L).transpose(2, 0, 1, 3).reshape(128, 2 * FT * L)
    tab = np.concatenate([fwd, inv], axis=1).astype(f)
    return (np.ascontiguousarray(feats[order].T), np.ascontiguousarray(dec[order].reshape(T, 128, WB).transpose(1, 0, 2)), tab)


def _rope():
    import numpy as np
    f = np.float32
    inv = (f(10000.0) ** (-(np.arange(16, dtype=f) / f(16)))).astype(f)
    pos = np.stack([np.repeat(np.arange(SEQ // 64), 64), np.tile(np.arange(64), SEQ // 64)]).astype(f)
    ang = (pos[:, :, None] * inv).astype(f).astype(np.float64)
    out = np.zeros((2, 2, 2, 16, SEQ))
    for a in range(2):
        for half in range(2):
            out[0, a, half] = np.cos(ang[a]).T
            out[1, a, half] = np.sin(ang[a]).T * (1 if half else -1)
    out = out.reshape(2, HD, SEQ)
    return np.ascontiguousarray(np.concatenate([out, out], axis=1).transpose(1, 0, 2)).astype(f)


def kernel(x, c, ctx, c_ctx, norm_g, w_mod, b_mod, w_in, conv_a, conv_h, filt_w1, filt_b1, filt_w2, filt_b2, filt_w3, filt_b3,
           filt_freq, hyena_bias, q_norm_g, k_norm_g, w_branch, w_out):
    import numpy as np
    import concourse.bacc as bacc
    from concourse.bass_utils import run_bass_kernel_spmd as run
    A = np.asarray

    def rows(v):
        return A(v).reshape(-1, 128).T

    def tile_units(w, c0):
        t = A(w)[:, c0:c0 + 128].reshape(-1, 4, 128, 128)
        return list(t.transpose(0, 2, 1, 3).reshape(-1, 128, UW))

    def chunks(v):
        return np.ascontiguousarray(A(v)[0].T.reshape(KD, 128, -1).transpose(1, 0, 2))

    XA, BA, CA, ZA, HV, HX1, HX2, HZ = (512 * n for n in range(8))
    QO, KO, VO, ZO, GO = 4096, 4608, 4736, 4864, 5376
    stream, mod, vec, w3 = [], [], [], []
    for l in range(DEPTH):
        units = []
        for group in ((HV, HX1, HX2, HZ), (CA, XA, BA, ZA)):
            for n in range(CB):
                for c0 in group:
                    units += tile_units(w_in[l], c0 + 128 * n)
                if group[0] == HV and n % 2 == 1:
                    units += tile_units(w_in[l], ZO + 128 * (2 + n // 2))
        for c0 in (KO, VO, QO, QO + 128, QO + 256, QO + 384):
            units += tile_units(w_in[l], c0)
        for n in range(2):
            units += tile_units(w_in[l], ZO + 128 * n)
        for branches in ((0,), (1, 2)):
            for d in range(KD):
                for n in branches:
                    units += tile_units(w_in[l], GO + 1024 * n + 128 * d)
                    units += tile_units(w_branch[l, n], 128 * d)
        for d in range(KD):
            units += tile_units(w_out[l], 128 * d)
        stream.append(np.stack(units))
        mod += list(A(w_mod)[l].reshape(KD, 128, 3 * D))
        v = np.zeros((128, NV), np.float32)
        v[:, V_NG:V_NG + 8] = rows(norm_g[l])
        v[:, V_BM:V_BM + 24] = rows(b_mod[l])
        for kind in range(4):
            for t in range(3):
                taps = A(conv_a)[l, t] if kind == 0 else A(conv_h)[l, t, WB * (kind - 1):WB * kind]
                v[:, V_CONV + (3 * kind + t) * CB:V_CONV + (3 * kind + t + 1) * CB] = rows(taps)
        v[:, V_HB:V_HB + 8] = rows(A(hyena_bias)[l].reshape(-1))
        v[:, V_QG] = np.tile(A(q_norm_g)[l], 2)
        v[:, V_KG] = np.tile(A(k_norm_g)[l], 2)
        v[:FHID, V_FIL] = A(filt_b1)[l]
        v[:FHID, V_FIL + 1] = A(filt_freq)[l, 0]
        v[:FHID, V_FIL + 2] = A(filt_b2)[l]
        v[:FHID, V_FIL + 3] = A(filt_freq)[l, 1]
        vec.append(v)
        w = np.concatenate([A(filt_w3)[l], A(filt_b3)[l][None]]).reshape(FHID + 1, 2, 2, 2, 256)
        w3.append(w.transpose(1, 0, 3, 2, 4).reshape(2, FHID + 1, 2, 512))
    tx, tc = _tables(SEQ), _tables(CTX)
    arrays = dict(
        stream=np.stack(stream), mod=np.stack(mod),
        cc=np.ascontiguousarray(np.stack([rows(A(c)[0]), rows(c_ctx)], axis=2)),
        x=chunks(x), ctx=chunks(A(ctx)), vec=np.ascontiguousarray(np.stack(vec, axis=1)),
        fw1=A(filt_w1), fw2=A(filt_w2), w3=np.ascontiguousarray(np.stack(w3)),
        feats_x=tx[0], feats_c=tc[0], dec_x=tx[1], dec_c=tc[1], tab_x=tx[2], tab_c=tc[2], rope=_rope())
    nc = bacc.Bacc("TRN2", target_bir_lowering=False, num_devices=1)
    f32 = mybir.dt.float32
    a = {k: nc.dram_tensor(f"in_{k}", v.shape, f32, kind="ExternalInput").ap() for k, v in arrays.items()}
    x1 = nc.dram_tensor("x1", (128, KD, SEQ), f32).ap()
    ctx1 = nc.dram_tensor("ctx1", (128, KD, CTX), f32).ap()
    out = nc.dram_tensor("out", (128, KD, SEQ), f32, kind="ExternalOutput").ap()
    build(nc, a["stream"], a["mod"], a["cc"], a["x"], a["ctx"], a["vec"], a["fw1"], a["fw2"], a["w3"],
          (a["feats_x"], a["feats_c"]), (a["dec_x"], a["dec_c"]), (a["tab_x"], a["tab_c"]), a["rope"], x1, ctx1, out)
    r = run(nc, [{f"in_{k}": np.ascontiguousarray(v) for k, v in arrays.items()}], core_ids=[0])
    y = r.results[0]["out"]
    return np.ascontiguousarray(y.transpose(2, 1, 0).reshape(1, SEQ, D))
```

```python
import concourse.bass as bass
from concourse import mybir
from contextlib import ExitStack, contextmanager

D = 1024
KD = D // 128
SEQ, CTX = 512, 256
DEPTH = 2
WB = 512
CB = WB // 128
NH, NKV, HD = 8, 2, 64
FEMB, FHID = 33, 64
EPS = 1e-6
SCALE = HD ** -0.5

UW = 512
RAW, RING, LEAD = 6, 6, 3
U_H, U_A, U_Q, U_E, U_G, U_O = 2 * 18, 4 * 8 + 4, 12, 8 * 3, 8 * 6, 16
U_QKV = U_H + U_A
U_FIRST = U_QKV + U_Q
U_GATES = U_FIRST + U_E
E_EARLY = 3
U_LAYER = U_GATES + U_G + U_O
LOOP = 18
MODS = 6
LMODS = 5
P, TURN = "loads", "turn"
LMOD_STEPS = [(P, 0), None, (P, 2), (P, 4), None,
              (P, 6), (TURN, 0), (P, 8), (P, 10), None,
              (P, 12), None, (P, 14), None, (TURN, 1),
              (P, 16), None, (P, 18), (P, 20), (P, 22),
              (TURN, 2)]

V_NG, V_BM, V_CONV, V_HB, V_QG, V_KG, V_FIL = 0, 8, 32, 80, 88, 89, 90
NV = 94

C1, C2 = 6.28125, 0.0019350051879882812
C3 = 6.283185307179586 - C1 - C2
MAGIC = 12582912.0
PI_IN = 3.1415925


def build(nc, d_stream, d_mod, d_cc, d_x, d_ctx, d_vec, d_fw1, d_fw2, d_w3, d_feats, d_dec, d_tab, d_rope,
          d_x1, d_ctx1, d_out):
    f32, f32r = mybir.dt.float32, mybir.dt.float32r
    ACT, ALU, AX = mybir.ActivationFunctionType, mybir.AluOpType, mybir.AxisListType
    K = 1024
    BASE = 16512

    def at(name, shape, kb, dt=f32):
        return nc.alloc_sbuf_tensor_at(name, shape, dt, offset=BASE + int(kb * K))

    raw = at("raw", [128, RAW, UW], 0)
    w_hi = at("w_hi", [128, RING, UW], 18, f32r)
    w_lo = at("w_lo", [128, RING, UW], 30, f32r)
    ones = at("ones", [128, 128], 42)
    ident = at("ident", [128, 128], 42.5)
    heads2 = at("heads2", [128, 2], 43)
    vec = at("vec", [128, DEPTH, NV], 43.0625)
    modv = at("modv", [128, DEPTH, 24, 2], 43.8125)
    gain = at("gain", [128, DEPTH, KD, 2], 44.25)
    cc = at("cc", [128, KD, 2], 45.125)
    cs = at("cs", [128, KD, 2], 45.1875)
    ms = at("ms", [128, 10 * 4], 45.375)
    rs = at("rs", [128, 10 * 4], 45.5625)
    nu = at("nu", [128, 10 * 4], 45.75)
    den = at("den", [128, 32], 45.9375)
    rden = at("rden", [128, 32], 46.0625)
    nmx = at("nmx", [128, 32], 46.1875)
    mx = at("mx", [128, 32], 46.3125)
    knorm = at("knorm", [128, 2], 46.4375)
    nms = at("nms", [128, 2, 4], 46.5)
    nrs = at("nrs", [128, 2, 4], 46.53125)
    nnu = at("nnu", [128, 2, 4], 46.5625)
    kx = at("kx", [128, SEQ + CTX], 47)
    vx = at("vx", [128, SEQ + CTX], 50)
    ya_hi = [at(f"ya_hi{n}", [128, SEQ], kb, f32r) for n, kb in enumerate((12, 14, 16, 147))]
    h_hi = at("h_hi", [128, KD, SEQ], 53, f32r)
    h_lo = at("h_lo", [128, KD, SEQ], 69, f32r)
    ya = at("ya", [128, CB, SEQ], 85)
    ya_lo = at("ya_lo", [128, CB, SEQ], 85, f32r)
    vb = at("vb", [128, CB, SEQ], 93)
    zs = at("zs", [128, CB, SEQ], 101)
    mw = [at(f"mw{n}", [128, 3 * D], kb) for n, kb in enumerate((53, 65, 97, 145, 157, 195))]
    mrow = at("mrow", [2, 6, 512], 171)
    lmw = [at(f"lmw{n}", [128, D], kb) for n, kb in enumerate((129, 133, 137, 145, 149))]
    lmrow = at("lmrow", [2, 2, 512], 153)
    traw = at("traw", [128, 4096], 191)
    feats = at("feats", [FEMB, SEQ], 85)
    feats_x0 = at("feats_x0", [FEMB, SEQ], 95)
    arg = at("arg", [FHID, SEQ], 87)
    turn = at("turn", [FHID, SEQ], 89)
    h1 = at("h1", [FHID, SEQ], 91)
    fw1 = at("fw1", [FEMB, FHID], 93)
    fw2 = at("fw2", [FHID, FHID], 93.5)
    xb = at("xb", [128, KD, SEQ], 125)
    sq_x = at("sq_x", [128, 2, SEQ], 109)
    sq_c = at("sq_c", [128, 4, CTX], 113)
    xt = at("xt", [128, 2, 2, SEQ], 117)
    xb_c = at("xb_c", [128, KD, CTX], 94)
    hc_hi = at("hc_hi", [128, KD, CTX], 125, f32r)
    hc_lo = at("hc_lo", [128, KD, CTX], 133, f32r)
    qraw_c = at("qraw_c", [128, 1, CTX], 102)
    qsq_c = at("qsq_c", [128, 1, CTX], 103)
    rsx_c = at("rsx_c", [128, 4, HD], 104)
    x12 = at("x12", [128, 2, CB, SEQ], 109)
    tab_hi = at("tab_hi", [128, 4096], 125, f32r)
    tab_lo = at("tab_lo", [128, 4096], 141, f32r)
    dec = at("dec", [128, 4, WB], 157)
    w3s = at("w3s", [FHID + 1, 2, 512], 165)
    h2 = at("h2", [FHID + 1, SEQ], 169)
    pads = at("pads", [128, 4, SEQ + 8], 171)
    szh = at("szh", [128, SEQ], 184)
    y2 = at("y2", [128, SEQ], 188)
    kspec = at("kspec", [128, 2, 2, 2, 256], 171)
    kp_hi = at("kp_hi", [128, 4, 512], 179, f32r)
    kp_lo = at("kp_lo", [128, 4, 512], 187, f32r)
    u_hi = at("u_hi", [128, 4, 256], 179, f32r)
    u_lo = at("u_lo", [128, 4, 256], 183, f32r)
    y_hi = at("y_hi", [128, 2, 2, 256], 187, f32r)
    y_lo = at("y_lo", [128, 2, 2, 256], 191, f32r)
    uu = at("uu", [128, 2, 2, 256], 195)
    p1 = at("p1", [128, 2, 2, 256], 199)
    p2 = at("p2", [128, 2, 2, 256], 203)
    kg = at("kg", [128, 2, 512], 195)
    kt = at("kt", [128, 2, 512], 199)
    kab = at("kab", [128, 2, 512], 203)
    zt = at("zt", [128, 2, 512], 195)
    e_sb = at("e_sb", [128, 512], 47)
    pa = at("pa", [128, SEQ], 50)
    q_hl = at("q_hl", [128, NH, SEQ], 109, f32r)
    k_hi = at("k_hi", [128, NKV, SEQ + CTX], 125, f32r)
    k_lo = at("k_lo", [128, NKV, SEQ + CTX], 131, f32r)
    v_hi = at("v_hi", [128, 6, 128], 137, f32r)
    v_lo = at("v_lo", [128, 6, 128], 140, f32r)
    ropes = at("ropes", [128, 2, SEQ], 143)
    oT = at("oT", [128, CB, SEQ], 149)
    pt_hi = at("pt_hi", [128, 2, 6, 256], 157, f32r)
    pt_lo = at("pt_lo", [128, 2, 6, 256], 169, f32r)
    pb = at("pb", [128, 2, SEQ + CTX], 181)
    rb = at("rb", [128, 2, 256], 187)
    qraw = at("qraw", [128, 5, SEQ], 157)
    qsq = at("qsq", [128, 5, SEQ], 167)
    rsx = at("rsx", [128, 10 * 4, HD], 167)
    qn = [at(f"qn{m}", [128, SEQ], kb) for m, kb in enumerate((177, 179, 199, 201, 203))]
    qsh = at("qsh", [128, SEQ], 50)
    b_hi = at("b_hi", [128, 2, CB, SEQ], 109, f32r)
    b_lo = at("b_lo", [128, 2, CB, SEQ], 125, f32r)
    mg = at("mg", [128, KD, SEQ], 189)
    bc_hi = at("bc_hi", [128, 2, CB, CTX], 109, f32r)
    bc_lo = at("bc_lo", [128, 2, CB, CTX], 117, f32r)
    mg_hi = at("mg_hi", [128, KD, SEQ], 141, f32r)
    mg_lo = at("mg_lo", [128, KD, SEQ], 189, f32r)
    te = at("te", [128, SEQ], 205)
    xr = at("xr", [128, KD, SEQ], 173)
    sg = at("sg", [128, 2, SEQ], 157)
    tg = at("tg", [128, 2, SEQ], 161)

    ctx = ExitStack()
    with ctx:
        ps = ctx.enter_context(nc.psum_tensor("ps", [128, 8, 512], f32))

        def sem(name):
            return ctx.enter_context(nc.semaphore(name))

        s_raw = [sem(f"s_raw{b}") for b in range(RAW)]
        s_hi = sem("s_hi")
        s_lo = sem("s_lo")
        s_used = sem("s_used")
        s_fx0 = sem("s_fx0")
        s_fc0 = sem("s_fc0")
        s_xc0 = sem("s_xc0")
        s_cs = sem("s_cs")
        s_act = sem("s_act")
        s_dve = sem("s_dve")
        s_const = sem("s_const")
        s_cdma = sem("s_cdma")
        s_mw = [sem(f"s_mw{b}") for b in range(MODS)]
        s_mused = sem("s_mused")
        s_mrow = sem("s_mrow")
        s_mcol = sem("s_mcol")
        s_lmw = [sem(f"s_lmw{b}") for b in range(LMODS)]
        s_lmused = sem("s_lmused")
        s_lmrow = sem("s_lmrow")
        s_lmcol = sem("s_lmcol")
        s_lmv = sem("s_lmv")

        sems, counts = {}, {}

        class Job:

            def __init__(self, name, layer, who, full, first_unit):
                self.name, self.layer, self.who, self.full, self.u0 = name, layer, who, full, first_unit
                self.L = SEQ if who == 0 else CTX
                self.T = self.L // 128
                self.Lh = self.L // 2
                self.FT = self.Lh // 128
                self.TW = 2 * self.L * self.L // 128
                self.nk = SEQ + CTX if who == 0 else CTX
                self.k0 = 0 if who == 0 else SEQ
                self.kt = self.nk // 128
                L, T, FT, full = self.L, self.T, self.FT, self.full
                steps, nt = NH * T, 6 if full else 2
                self.total = dict(xin=16 * (name in ("x0", "c1")), sq=8, msq=7, msd=nt - 1, ms=1, nmsd=1, nms=1, rt=1, rs=1, nrt=1, nrs=1, rbc=1, xt=8,  hh=8, hl=8,
                                  qraw=nt, rsx=1, qsq=nt - 1, qn=nt - 1, qbc=nt - 1)
                if full:
                    self.total.update(
                        fil=48 * (name == "x1"), tab=16, dec=16, w3=32, rope=16 * (who == 0), xr=16, stored=16 * KD,
                        tabh=CB, tabl=CB, fm=2, fa=2, fs=2, h2=2 * (name == "x0"), eva=9 + 18, ze=2, cv=1 + 3 * CB, fva=2 * CB, fvd=2 * CB, ya=CB,
                        kgen=4 * T, kd=4 * T, kt=4 * T, kh=4 * T, kl=4 * T, kab=4 * T, ksum=4 * T, kn=4, kf=4 * FT, ke=4 * FT, kuse=4 * FT,
                        ut=2 * T, uh=2 * T, ul=2 * T, uf=4 * FT, ue=4 * FT, uuse=4 * FT, eo=4 * FT, yh=4 * FT, yl=4 * FT,
                        yi=4 * FT, cross=8 * FT, fin=4, qr=5 * (who == 0), ksp=12, ksl=12, vt=1, vh=1, vl=1,
                        qk=steps, mx=steps, ex=steps, rd=steps, tp=steps, ph=steps, pl=steps,
                        rt2=steps // 2, rb=steps // 2, pv=steps // 2, oout=steps // 2, yc=1, bh=CB + 2, bl=CB + 2, et=KD, em=KD,
                        sg=2 + 2 * KD, pm=2 + 2 * KD, mg=KD, gh=KD, gl=KD, xo=KD)
                self.prefix = "" if full else f"{name}_"
                self.base = {}
                for n, v in self.total.items():
                    key = self.prefix + n
                    if key not in sems:
                        sems[key] = sem(f"s_{key}")
                    self.base[n] = counts.get(key, 0)
                    counts[key] = self.base[n] + v

            def s(self, name):
                assert name in self.total, name
                return sems[self.prefix + name]

            def at(self, name, value):
                return self.s(name), value + self.base[name]

        u = 0
        jobs = []
        for name, layer, who, full in (("c0", 0, 1, True), ("x0", 0, 0, True), ("c1", 1, 1, False), ("x1", 1, 0, True)):
            jobs.append(Job(name, layer, who, full, u))
            u += U_LAYER if full else 4
        N_UNITS = u
        c0, x0, c1, x1_ = jobs
        full_jobs = (c0, x0, x1_)
        before = {c0: None, x0: c0, c1: x0, x1_: x0}
        after = {c0: (x0,), x0: (c1, x1_), x1_: ()}
        h2_early = lambda half: zs[0:FHID, half, CTX:SEQ]
        x_of = lambda j: xr if j is x1_ else xb_c if j is c1 else xb
        sq_of = lambda j, k: (sq_x[:, k % 2, :], sq_c[:, k % 4, :])[j.who]
        b_of = lambda j: ((b_hi, b_lo), (bc_hi, bc_lo))[j.who]
        h_of = lambda j: (hc_hi, hc_lo) if j is c1 else (h_hi, h_lo)

        def gated_unit(j, r, f):
            return j.u0 + U_H + 8 * r + 2 * min(r, 2) + 2 * f

        def scores_at(j, s, k0, k1):
            b = 2 * (s % 2)
            return ps[:, b:b + 2, :].rearrange("p a c -> p (a c)")[:, k0:k1]

        def first_units(j, s):
            steps = NH * j.T
            weight = [(q + 1) % 2 * (q < steps - 2) if j.who == 0 else int(q < steps - 1) for q in range(steps)]
            assert sum(weight) == U_E - 3 * E_EARLY
            first = 3 * E_EARLY + sum(weight[:s])
            return range(first, first + weight[s])

        def queries_at(j, s):
            m, left = divmod(s - (j.T - 1), 2 * j.T)
            return m + 2 if left == 0 and 0 <= m < 3 else None

        class Chain:

            def __init__(self, eng, s):
                self.eng, self.sem, self.n, self.at = eng, s, 0, 0

            def __call__(self, ins):
                self.n += 1
                ins.then_inc(self.sem, 1)
                self.eng.wait_ge(self.sem, self.at + self.n)

            @contextmanager
            def loop(self, count, steps):
                start = self.n
                with self.eng.Fori(0, count, 1) as i:
                    self.at = i * steps
                    yield i
                    assert self.n - start == steps, (self.n - start, steps)
                self.at = 0
                self.n = start + steps * count

        def mm3(out, hi, lo, m_hi, m_lo, start, stop, shared=False):
            nc.tensor.matmul(out, hi, m_hi, start=start, stop=False, skip_group_check=shared)
            nc.tensor.matmul(out, hi, m_lo, start=False, stop=False, skip_group_check=shared)
            return nc.tensor.matmul(out, lo, m_hi, start=False, stop=stop, skip_group_check=shared)

        block = ctx.enter_context(nc.Block())

        @block.sync
        def _(sp):
            def unit(src, index, n, i=0, per=0):
                b = n % RAW
                if n >= RAW:
                    sp.wait_ge(s_lo, n - RAW + 1 + i * per)
                sp.dma_start(raw[:, b, :], src[bass.ds(index, 1)].rearrange("o p c -> p (o c)")).then_inc(s_raw[b], 16)

            def segment(src, first, n, count):
                done = 0
                if n == 0:
                    for p in range(LOOP):
                        unit(src, first + p, n + p)
                    done = LOOP
                loops = (count - done) // LOOP
                if loops > 1:
                    with sp.Fori(0, loops, 1) as i:
                        for p in range(LOOP):
                            unit(src, i * LOOP + (first + done + p), n + done + p, i, LOOP)
                    done += loops * LOOP
                for p in range(done, count):
                    unit(src, first + p, n + p)

            sp.dma_start(cc[:, :, :], d_cc).then_inc(s_cdma, 16)
            sp.dma_start(vec[:, :, :], d_vec).then_inc(s_cdma, 16)
            for n in range(KD):
                if n == 2:
                    sp.dma_start(feats[:, 0:CTX], d_feats[1]).then_inc(s_fc0, 16)
                    sp.dma_start(fw1[:, :], d_fw1[0]).then_inc(s_fc0, 16)
                    sp.dma_start(fw2[:, :], d_fw2[0]).then_inc(s_fc0, 16)
                    sp.dma_start(xb[:, :, 0:CTX], d_ctx).then_inc(s_xc0, 16)
                    sp.dma_start(feats_x0[:, :], d_feats[0]).then_inc(s_fx0, 16)
                if n >= MODS:
                    sp.wait_ge(s_mused, n - MODS + 1)
                sp.dma_start(mw[n % MODS][:, :], d_mod[0, n]).then_inc(s_mw[n % MODS], 16)
            for j in jobs:
                if j.full:
                    segment(d_stream[j.layer], 0, j.u0, U_LAYER)
                else:
                    segment(d_stream[j.layer], U_QKV, j.u0, 4)
            for j in full_jobs:
                sp.wait_ge(*j.at("stored", 16 * KD))

        @block.gpsimd
        def _(pool):
            nc.gpsimd.memset(ident[:, :], 0.0).then_inc(s_const, 1)
            nc.gpsimd.memset(ones[:, :], 1.0).then_inc(s_const, 1)
            nc.gpsimd.memset(heads2[:, :], 0.0).then_inc(s_const, 1)
            pool.wait_ge(s_const, 3)
            nc.gpsimd.affine_select(out=ident[:, :], in_=ident[:, :], compare_op=ALU.not_equal, fill=1.0, base=0,
                                    pattern=[[-1, 128]], channel_multiplier=1).then_inc(s_const, 1)
            pool.wait_ge(s_const, 4)
            nc.gpsimd.memset(heads2[0:HD, 0:1], 1.0).then_inc(s_const, 1)
            pool.wait_ge(s_const, 5)
            nc.gpsimd.memset(heads2[HD:128, 1:2], 1.0).then_inc(s_const, 1)

            def source(j):
                return ((d_x, d_ctx), (d_x1, d_ctx1))[j.layer][j.who]

            def filter_inputs(j):
                pool.dma_start(feats[:, 0:j.L], d_feats[j.who]).then_inc(j.s("fil"), 16)
                pool.dma_start(fw1[:, :], d_fw1[j.layer]).then_inc(j.s("fil"), 16)
                pool.dma_start(fw2[:, :], d_fw2[j.layer]).then_inc(j.s("fil"), 16)

            def start(j):
                L, T, ly, prev = j.L, j.T, j.layer, before[j]
                if prev is not None:
                    pool.wait_ge(*prev.at("bl", CB + 2))
                if j is not x1_:
                    if j is c1:
                        pool.wait_ge(*c0.at("stored", 16 * KD))
                    pool.dma_start(x_of(j)[:, :, 0:L], source(j)).then_inc(j.s("xin"), 16)
                if j.full and j is not x0:
                    filter_inputs(j)

            def filter_tables(j):
                T, ly, prev = j.T, j.layer, before[j]
                if prev is not None:
                    pool.wait_ge(*prev.at("gl", KD))
                else:
                    pool.wait_ge(s_mused, KD)
                pool.dma_start(dec[:, 0:T, :], d_dec[j.who]).then_inc(j.s("dec"), 16)
                pool.dma_start(w3s[:, :, :], d_w3[ly, 0]).then_inc(j.s("w3"), 16)

            def tables(j):
                pool.dma_start(traw[:, 0:j.TW], d_tab[j.who]).then_inc(j.s("tab"), 16)

            filter_tables(c0)
            tables(c0)
            for j in full_jobs:
                L, T, ly = j.L, j.T, j.layer
                G = nc.gpsimd
                for r in range(4):
                    for tt in range(T):
                        pool.wait_ge(*j.at("kh", r * T + tt + 1))
                        G.tensor_tensor(kp_lo[:, tt, :], kt[:, tt % 2, :], kp_hi[:, tt, :].bitcast(f32), ALU.subtract).then_inc(j.s("kl"), 1)
                    if r == 1:
                        pool.wait_ge(*j.at("kgen", 2 * T))
                        pool.dma_start(w3s[:, :, :], d_w3[ly, 1]).then_inc(j.s("w3"), 16)
                    for ft in range(j.FT):
                        pool.wait_ge(*j.at("uuse", r * j.FT + ft + 1))
                        k = kspec[:, ft]
                        for part in range(2):
                            G.tensor_tensor(p2[:, :, part, :], uu[:, :, part, :], k[:, :, 1 - part, :], ALU.mult).then_inc(j.s("cross"), 1)
                if j.who == 0:
                    pool.wait_ge(*j.at("fin", 4))
                    pool.dma_start(ropes[:, :, :], d_rope).then_inc(j.s("rope"), 16)
                pool.wait_ge(*j.at("oout", NH * T // 2))
                if j is x1_:
                    pool.wait_ge(*x0.at("stored", 16 * KD))
                pool.dma_start(xr[:, :, 0:L], source(j)).then_inc(j.s("xr"), 16)
                for nx in after[j]:
                    start(nx)
                for nx in after[j]:
                    if nx.full:
                        filter_tables(nx)
                dst = d_out if (ly == 1) else (d_x1, d_ctx1)[j.who]
                for d in range(KD):
                    pool.wait_ge(*j.at("xo", d + 1))
                    pool.dma_start(dst[:, d, :], xr[:, d, 0:L]).then_inc(j.s("stored"), 16)
                for nx in after[j]:
                    if nx.full:
                        tables(nx)

        @block.scalar
        def _(act):
            chain = Chain(act, s_act)

            def split_hi(n, i=0, per=0):
                n += LEAD
                if n >= N_UNITS:
                    return
                act.wait_ge(s_raw[n % RAW], 16 * (n // RAW + 1) + i * (16 * per // RAW))
                if n >= RING:
                    act.wait_ge(s_used, n - RING + 1 + i * per)
                nc.scalar.activation(w_hi[:, n % RING, :], raw[:, n % RAW, :], ACT.Copy).then_inc(s_hi, 1)

            def used(n, i=0, per=0):
                act.wait_ge(s_used, n + 1 + i * per)

            def square(j, k):
                if j is x1_:
                    act.wait_ge(*x0.at("xo", k + 1))
                else:
                    act.wait_ge(*((s_xc0, 16) if j is c0 else j.at("xin", 16)))
                slots = (2, 4)[j.who]
                if k >= slots:
                    act.wait_ge(*j.at("msq", k - slots + 1))
                nc.scalar.activation(sq_of(j, k), x_of(j)[:, k, 0:j.L], ACT.Square).then_inc(j.s("sq"), 1)

            def sine(j, layer):
                if layer == 1 and j is x1_:
                    act.wait_ge(*before[j].at("gl", KD))
                act.wait_ge(*j.at("fa", layer + 1))
                if layer == 0:
                    nc.scalar.activation(h1[:, 0:j.L], arg[:, 0:j.L], ACT.Sin).then_inc(j.s("fs"), 1)
                elif j is x0:
                    nc.scalar.activation(h2_early(slice(0, 2)), arg[:, :].rearrange("p (a c) -> p a c", a=2), ACT.Sin).then_inc(j.s("fs"), 1)
                else:
                    nc.scalar.activation(h2[0:FHID, 0:j.L], arg[:, 0:j.L], ACT.Sin).then_inc(j.s("fs"), 1)

            def root(j):
                act.wait_ge(*j.at("nms", 1))
                nc.scalar.activation(nrs[:, j.who, 0:j.T], nms[:, j.who, 0:j.T], ACT.Sqrt).then_inc(j.s("nrt"), 1)

            def modulate(j, k):
                if k == 0 and before[j] is not None:
                    act.wait_ge(*before[j].at("mg", KD))
                act.wait_ge(*j.at("xt", k + 1))
                nc.scalar.activation(h_of(j)[0][:, k, 0:j.L], xt[:, j.who, k % 2, 0:j.L], ACT.Identity,
                                     bias=modv[:, j.layer, k, j.who:j.who + 1]).then_inc(j.s("hh"), 1)

            def out_of_psum(j, ti, u, raw_rows, squares):
                L = j.L
                for half in range(2):
                    split_hi(u + 2 * ti + half)
                used(u + 2 * ti + 1)
                if ti == 1:
                    nc.scalar.activation(vx[:, j.k0:j.k0 + L], ps[:, 1, 0:L], ACT.Copy).then_inc(j.s("qraw"), 1)
                else:
                    m = 0 if ti == 0 else ti - 1
                    nc.scalar.activation(raw_rows[:, m, 0:L], ps[:, ti, 0:L], ACT.Copy).then_inc(j.s("qraw"), 1)
                    act.wait_ge(*j.at("qraw", ti + 1))
                    nc.scalar.activation(squares[:, m, 0:L], raw_rows[:, m, 0:L], ACT.Square).then_inc(j.s("qsq"), 1)

            def head_roots(j, n, spread_rows):
                act.wait_ge(*j.at("ms", 1))
                nc.scalar.activation(rs[:, 0:n], ms[:, 0:n], ACT.Sqrt).then_inc(j.s("rt"), 1)
                act.wait_ge(*j.at("rs", 1))
                nc.scalar.activation(spread_rows[:, 0:n, :], rs[:, 0:n].rearrange("p (a o) -> p a o", o=1)
                                     .to_broadcast([128, n, HD]), ACT.Copy).then_inc(j.s("rsx"), 1)

            act.wait_ge(s_cdma, 32)
            nc.scalar.activation(cs[:, :, :], cc[:, :, :], ACT.Silu).then_inc(s_cs, 1)
            sine(c0, 0)
            sine(c0, 1)
            for k in range(KD):
                square(c0, k)
            root(c0)
            sine(x0, 0)
            sine(x0, 1)
            act.wait_ge(s_mused, KD)
            nc.scalar.activation(mrow[:, :, :], ps[0:2, 0:6, :], ACT.Copy).then_inc(s_mrow, 1)
            for n in range(LEAD):
                split_hi(n - LEAD)

            for j in full_jobs:
                L, T, Lh, FT, ly, who = j.L, j.T, j.Lh, j.FT, j.layer, j.who
                for k in range(KD):
                    if j is x1_ and k == KD // 2:
                        for ti in range(2):
                            out_of_psum(c1, ti, c1.u0, qraw_c, qsq_c)
                    if j is not x0:
                        modulate(j, k)

                act.sem_inc(j.s("eva"), 9)
                if before[j] is not None:
                    act.wait_ge(*before[j].at("stored", 16 * KD))
                tw = j.TW // CB
                with act.Fori(0, 2, 1) as i:
                    for ti in range(9):
                        sub = ti // 4
                        for half in range(2):
                            split_hi(j.u0 + 2 * ti + half, i, LOOP)
                        used(j.u0 + 2 * ti + 1, i, LOOP)
                        bank = ps[:, ti % 8, 0:L]
                        if ti == 8:
                            nc.scalar.activation(zs[:, bass.ds(i + 2, 1), 0:L].rearrange("p o l -> p (o l)"), bank, ACT.Silu)\
                              .then_inc(j.s("eva"), 1)
                        elif ti % 4 == 3:
                            nc.scalar.activation(szh[:, 0:L], bank, ACT.Silu).then_inc(j.s("eva"), 1)
                        else:
                            act.wait_ge(*j.at("cv", 6 * i + (3 * sub + 1)))
                            nc.scalar.activation(pads[:, 1 + ti % 4, 1:L + 1], bank, ACT.Copy).then_inc(j.s("eva"), 1)
                        if ti in (2, 6):
                            act.wait_ge(*j.at("tab", 16))
                            nc.scalar.activation(tab_hi[:, bass.ds(i * (2 * tw) + sub * tw, tw)], traw[:, bass.ds(i * (2 * tw) + sub * tw, tw)],
                                                 ACT.Copy).then_inc(j.s("tabh"), 1)

                if j is x1_:
                    head_roots(c1, 2 * c1.T, rsx_c)

                def gated_units(r, f):
                    for half in range(2):
                        split_hi(gated_unit(j, r, f) + half)

                def gated(r, f):
                    n = gated_unit(j, r, f)
                    if f == 4:
                        used(n + 1)
                        nc.scalar.activation(zs[:, r, 0:L], ps[:, 6, 0:L], ACT.Silu).then_inc(j.s("ze"), 1)
                    if f == 0:
                        used(n + 1)
                        if r:
                            act.wait_ge(*j.at("ya", r))
                        nc.scalar.activation(pa[:, 0:L], ps[:, 6, 0:L], ACT.Copy).then_inc(j.s("fva"), 1)
                    if f == 3:
                        used(n + 1)
                        act.wait_ge(*j.at("fvd", 2 * r + 2))
                        nc.scalar.activation(pa[:, 0:L], ps[:, 7, 0:L], ACT.Silu).then_inc(j.s("fva"), 1)

                def modulation_load(n):
                    if n >= LMODS:
                        act.wait_ge(s_lmused, n - LMODS + 1)
                    act.dma_start(lmw[n % LMODS][:, :], d_mod[1, n % KD][:, D * (n // KD):D * (n // KD) + D]).then_inc(s_lmw[n % LMODS], 16)

                def last_modulation(n):
                    if j is not c0 or LMOD_STEPS[n] is None:
                        return
                    kind, q = LMOD_STEPS[n]
                    if kind == P:
                        for m in (q + 3, q + 4):
                            if LMODS <= m < 3 * KD:
                                modulation_load(m)
                    else:
                        act.wait_ge(s_lmused, KD * (q + 1))
                        nc.scalar.activation(lmrow[:, :, :], ps[0:2, 2:4, :], ACT.Copy).then_inc(s_lmrow, 1)

                if j is c0:
                    for n in range(LMODS):
                        modulation_load(n)
                gated_units(0, 0)
                gated(0, 0)
                for r in range(4):
                    for tt in range(T):
                        act.wait_ge(*j.at("kt", r * T + tt + 1))
                        nc.scalar.activation(kp_hi[:, tt, :], kt[:, tt % 2, :], ACT.Copy).then_inc(j.s("kh"), 1)
                        if r * T + tt >= 2:
                            act.wait_ge(*j.at("ksum", r * T + tt - 1))
                        nc.scalar.activation(kab[:, tt % 2, :], kg[:, tt % 2, :], ACT.Abs).then_inc(j.s("kab"), 1)
                        if tt == 0:
                            gated_units(r, 1)
                    gated_units(r, 2)
                    last_modulation(5 * r)
                    last_modulation(5 * r + 1)
                    for ft in range(FT):
                        act.wait_ge(*j.at("kf", r * FT + ft + 1))
                        if ft or r:
                            act.wait_ge(*j.at("kuse", r * FT + ft))
                        nc.scalar.activation(e_sb[:, :], ps[:, 2 * ft, :], ACT.Copy).then_inc(j.s("ke"), 1)
                    act.wait_ge(*j.at("kf", (r + 1) * FT))
                    for b in range((T + 1) // 2):
                        act.wait_ge(*j.at("ut", r * (T // 2) + b + 1))
                        nc.scalar.activation(u_hi[:, 2 * b:2 * b + 2, :].rearrange("p a c -> p (a c)"), ps[:, 4 + b, :], ACT.Copy)\
                          .then_inc(j.s("uh"), 1)
                    for ft in range(FT):
                        act.wait_ge(*j.at("uf", r * FT + ft + 1))
                        act.wait_ge(*j.at("kuse", (r + 1) * FT))
                        if ft:
                            act.wait_ge(*j.at("uuse", r * FT + ft))
                        nc.scalar.activation(e_sb[:, :], ps[:, 2 * ft, :], ACT.Copy).then_inc(j.s("ue"), 1)
                        if ft == 0:
                            gated_units(r, 3)
                            if r < 2:
                                gated_units(r, 4)
                        if ft == FT - 1 and r < 3:
                            gated_units(r + 1, 0)
                        act.wait_ge(*j.at("eo", r * FT + ft + 1))
                        if ft:
                            act.wait_ge(*j.at("yi", r * FT + ft))
                        nc.scalar.activation(y_hi[:, :, :, :].rearrange("p a b c -> p (a b c)"),
                                             uu[:, :, :, :].rearrange("p a b c -> p (a b c)"), ACT.Copy).then_inc(j.s("yh"), 1)
                        if ft == 0:
                            gated(r, 3)
                            if r < 2:
                                gated(r, 4)
                            for n in (2, 3, 4):
                                last_modulation(5 * r + n)
                        if ft == FT - 1 and r < 3:
                            gated(r + 1, 0)

                last_modulation(20)
                uq = j.u0 + U_QKV
                nm = 5
                for ti in range(6):
                    out_of_psum(j, ti, uq, qraw, qsq)
                    if ti < CB:
                        act.wait_ge(*j.at("ya", ti + 1))
                        nc.scalar.activation(ya_hi[ti][:, 0:L], ya[:, ti, 0:L], ACT.Copy).then_inc(j.s("bh"), 1)

                head_roots(j, 2 * nm * T, rsx)

                def first_branch(e, split=True, tanh=True):
                    d, q = e // 3, e % 3
                    if split:
                        split_hi(j.u0 + U_FIRST + e)
                    if q == 1 and tanh:
                        used(j.u0 + U_FIRST + e)
                        if d:
                            act.wait_ge(*j.at("em", d))
                        nc.scalar.activation(te[:, 0:L], ps[:, 7, 0:L], ACT.Tanh, scale=0.5).then_inc(j.s("et"), 1)

                for e in range(6):
                    first_branch(e)
                first_branch(6)
                first_branch(7, tanh=False)
                act.wait_ge(*(j.at("qr", 1) if who == 0 else j.at("qn", 1)))
                for g in range(NKV):
                    rows = slice(64 * g, 64 * g + 64)
                    for half in range(2):
                        nc.scalar.activation(k_hi[64 * half:64 * half + 64, g, 0:j.nk], kx[rows, j.k0:j.k0 + j.nk], ACT.Copy)\
                          .then_inc(j.s("ksp"), 1)

                def queries(m):
                    act.wait_ge(*(j.at("qr", m + 1) if who == 0 else j.at("qn", m + 1)))
                    for e in range(2):
                        rows = slice(64 * e, 64 * e + 64)
                        nc.scalar.activation(q_hl[rows, 2 * (m - 1) + e, 0:L], qn[m][rows, 0:L], ACT.Copy).then_inc(j.s("ksp"), 1)

                queries(1)
                first_branch(7, split=False)
                first_branch(8)
                act.wait_ge(*j.at("vt", 1))
                nc.scalar.activation(v_hi[:, 0:j.kt, :].rearrange("p a c -> p (a c)"),
                                     ps[:, 0:2, :].rearrange("p a c -> p (a c)")[:, 0:j.nk], ACT.Copy).then_inc(j.s("vh"), 1)

                steps = NH * T

                def exps(s):
                    act.wait_ge(*j.at("mx", s + 1))
                    if s >= 2:
                        act.wait_ge(*j.at("tp", s - 1))
                    nc.scalar.activation(pb[:, s % 2, 0:j.nk], scores_at(j, s, 0, j.nk),
                                         ACT.Exp, bias=nmx[:, s:s + 1], scale=SCALE, accum_out=den[:, s:s + 1])\
                      .then_inc(j.s("ex"), 1)

                def hi_of_p(s):
                    grp, q = s // 2, s % 2
                    act.wait_ge(*j.at("tp", s + 1))
                    if grp >= 2:
                        act.wait_ge(*j.at("pv", grp - 1))
                    nc.scalar.activation(pt_hi[:, grp % 2, 0:j.kt, 128 * q:128 * q + 128],
                                         ps[:, 4:6, :].rearrange("p a c -> p (a c)")[:, 0:j.nk].rearrange("p (a c) -> p a c", c=128),
                                         ACT.Copy).then_inc(j.s("ph"), 1)

                def spread(grp):
                    act.wait_ge(*j.at("rt2", grp + 1))
                    if grp >= 2:
                        act.wait_ge(*j.at("oout", grp - 1))
                    nc.scalar.activation(rb[:, grp % 2, :], ps[:, 6, 256:512], ACT.Copy).then_inc(j.s("rb"), 1)

                exps(0)
                for s in range(steps):
                    if s % 2 == 1 and s >= 3:
                        spread(s // 2 - 1)
                    hi_of_p(s)
                    if s + 1 < steps:
                        exps(s + 1)
                    if queries_at(j, s - 1):
                        queries(queries_at(j, s - 1))
                    for e in first_units(j, s):
                        first_branch(e)
                spread(steps // 2 - 1)

                act.sem_inc(j.s("sg"), 2)
                for n, src in enumerate((vb, zs)):
                    if n == 1:
                        act.wait_ge(*j.at("yc", 1))
                    nc.scalar.activation(b_of(j)[0][:, n, :, 0:L], src[:, :, 0:L], ACT.Copy).then_inc(j.s("bh"), 1)
                ug = j.u0 + U_GATES
                with act.Fori(0, KD, 1) as i:
                    for n in range(2):
                        for half in range(2):
                            split_hi(ug + 3 * n + half, i, 6)
                        used(ug + 3 * n + 1, i, 6)
                        act.wait_ge(*j.at("pm", 2 * i + (n + 1)))
                        nc.scalar.activation(sg[:, n, 0:L], ps[:, n, 0:L], ACT.Tanh, scale=0.5).then_inc(j.s("sg"), 1)
                        split_hi(ug + 3 * n + 2, i, 6)
                    act.wait_ge(*j.at("mg", i + 1))
                    nc.scalar.activation(mg_hi[:, bass.ds(i, 1), 0:L].rearrange("p o l -> p (o l)"),
                                         mg[:, bass.ds(i, 1), 0:L].rearrange("p o l -> p (o l)"), ACT.Copy, scale=0.5).then_inc(j.s("gh"), 1)
                for nx in after[j]:
                    if nx is not x1_:
                        square(nx, 0)
                        square(nx, 1)
                for d in range(KD):
                    for half in range(2):
                        split_hi(ug + U_G + 2 * d + half)
                    for nx in after[j]:
                        if nx is not x1_:
                            for k in range(2 * d + 2, 2 * d + 4):
                                if k < KD:
                                    square(nx, k)
                            if d == 3:
                                root(nx)
                        elif d:
                            square(nx, d - 1)
                        if nx is x0 and d == 1:
                            act.wait_ge(*j.at("gl", KD))
                            for half in range(2):
                                nc.scalar.activation(h2[0:FHID, CTX * half:CTX * half + CTX], h2_early(half), ACT.Copy).then_inc(nx.s("h2"), 1)
                        if nx is x1_ and d == 1:
                            sine(nx, 0)
                        if nx is x1_ and d == 4:
                            sine(nx, 1)
                        if nx is not x1_ and d >= 5:
                            for k in (2 * d - 10, 2 * d - 9):
                                modulate(nx, k)
                if x1_ in after[j]:
                    square(x1_, KD - 1)
                for nx in after[j]:
                    if nx is not x1_:
                        for k in range(6, KD):
                            modulate(nx, k)
                    else:
                        root(x1_)

        @block.vector
        def _(dve):
            chain = Chain(dve, s_dve)
            V = nc.vector

            def split_lo(n, i=0, per=0):
                n += LEAD
                if n >= N_UNITS:
                    return
                dve.wait_ge(s_hi, n + 1 + i * per)
                V.tensor_tensor(w_lo[:, n % RING, :], raw[:, n % RAW, :], w_hi[:, n % RING, :].bitcast(f32), ALU.subtract)\
                 .then_inc(s_lo, 1)

            def used(n, i=0, per=0):
                dve.wait_ge(s_used, n + 1 + i * per)

            def rsqrt(n, rs, ms, nu, ready, done):
                dve.wait_ge(*ready)
                chain(V.reciprocal(rs[:, 0:n], rs[:, 0:n]))
                chain(V.scalar_tensor_tensor(out=nu[:, 0:n], in0=rs[:, 0:n], scalar=-0.5, in1=ms[:, 0:n], op0=ALU.mult, op1=ALU.mult))
                chain(V.tensor_tensor(nu[:, 0:n], nu[:, 0:n], rs[:, 0:n], ALU.mult))
                V.scalar_tensor_tensor(out=rs[:, 0:n], in0=nu[:, 0:n], scalar=1.5, in1=rs[:, 0:n], op0=ALU.add, op1=ALU.mult)\
                 .then_inc(done[0], 1)
                dve.wait_ge(*done)

            def arguments(j, layer):
                L = j.L
                dve.wait_ge(*j.at("fm", layer + 1))
                col = lambda c: vec[0:FHID, j.layer, c:c + 1]
                if layer == 1:
                    dve.wait_ge(*j.at("fs", 1))
                elif j is x0:
                    dve.wait_ge(*c0.at("fs", 2))
                chain(V.tensor_scalar(arg[:, 0:L], ps[0:FHID, 6, 0:L], col(V_FIL + 2 * layer), col(V_FIL + 2 * layer + 1), ALU.add, ALU.mult))
                chain(V.tensor_scalar(turn[:, 0:L], arg[:, 0:L], 1.0 / 6.283185307179586, MAGIC, ALU.mult, ALU.add))
                chain(V.tensor_scalar(turn[:, 0:L], turn[:, 0:L], -MAGIC, None, ALU.add))
                for part in (C1, C2, C3):
                    chain(V.scalar_tensor_tensor(out=arg[:, 0:L], in0=turn[:, 0:L], scalar=-part, in1=arg[:, 0:L],
                                                 op0=ALU.mult, op1=ALU.add))
                V.tensor_scalar(arg[:, 0:L], arg[:, 0:L], PI_IN, -PI_IN, ALU.min, ALU.max).then_inc(j.s("fa"), 1)
                dve.wait_ge(*j.at("fa", layer + 1))

            def norm(j):
                T, w = j.T, j.who
                dve.wait_ge(*j.at("nmsd", 1))
                V.tensor_scalar(nms[:, w, 0:T], ps[:, (5, 7)[w], 0:T], 1.0 / D, EPS, ALU.mult, ALU.add).then_inc(j.s("nms"), 1)
                dve.wait_ge(*j.at("nms", 1))
                rsqrt(T, nrs[:, w], nms[:, w], nnu[:, w], j.at("nrt", 1), j.at("nrs", 1))

            def modulate(j, k):
                L, w, ly = j.L, j.who, j.layer
                if k == 0:
                    dve.wait_ge(*j.at("rbc", 1))
                    if j is not x1_:
                        dve.wait_ge(*((s_xc0, 16) if j is c0 else j.at("xin", 16)))
                if k >= 2:
                    dve.wait_ge(*j.at("hl", k - 1))
                V.scalar_tensor_tensor(out=xt[:, w, k % 2, 0:L], in0=x_of(j)[:, k, 0:L], scalar=gain[:, ly, k, w:w + 1],
                                       in1=ps[:, (4, 7)[w], 0:L], op0=ALU.mult, op1=ALU.mult).then_inc(j.s("xt"), 1)
                if k:
                    modulate_low(j, k - 1)
                if k == KD - 1:
                    modulate_low(j, k)

            def modulate_low(j, k):
                L, w, ly = j.L, j.who, j.layer
                dve.wait_ge(*j.at("hh", k + 1))
                V.scalar_tensor_tensor(out=h_of(j)[1][:, k, 0:L], in0=xt[:, w, k % 2, 0:L], scalar=modv[:, ly, k, w:w + 1],
                                       in1=h_of(j)[0][:, k, 0:L].bitcast(f32), op0=ALU.add, op1=ALU.subtract).then_inc(j.s("hl"), 1)

            def head_norms(j, n):
                dve.wait_ge(*j.at("msd", 1 if j is c1 else 5))
                V.tensor_scalar(ms[:, 0:n], ps[:, 5 if j is c1 else 6, 0:n], 1.0 / HD, EPS, ALU.mult, ALU.add).then_inc(j.s("ms"), 1)
                dve.wait_ge(*j.at("ms", 1))
                rsqrt(n, rs, ms, nu, j.at("rt", 1), j.at("rs", 1))

            def head_normed(j, m, rows, bank):
                dve.wait_ge(*j.at("qbc", m + 1))
                L = j.L
                dst = kx[:, SEQ:SEQ + L] if (m == 0 and j.who == 1) else qn[m][:, 0:L]
                c = V_KG if m == 0 else V_QG
                V.scalar_tensor_tensor(out=dst, in0=rows[:, m, 0:L], scalar=vec[:, j.layer, c:c + 1],
                                       in1=ps[:, bank, 0:L], op0=ALU.mult, op1=ALU.mult).then_inc(j.s("qn"), 1)
                dve.wait_ge(*j.at("qn", m + 1))

            dve.wait_ge(s_cdma, 32)
            for layer in range(2):
                arguments(c0, layer)
            chain(V.memset(h2[FHID:FHID + 1, :], 1.0))
            norm(c0)
            for layer in range(2):
                arguments(x0, layer)

            def gains(ly):
                for w in range(2):
                    chain(V.scalar_tensor_tensor(out=gain[:, ly, :, w], in0=modv[:, ly, KD:2 * KD, w], scalar=1.0,
                                                 in1=vec[:, ly, V_NG:V_NG + KD], op0=ALU.add, op1=ALU.mult))

            for n in range(LEAD):
                split_lo(n - LEAD)
            dve.wait_ge(s_mcol, 1)
            for w in range(2):
                chain(V.tensor_tensor(modv[:, 0, :, w], ps[:, 6, w:48:2], vec[:, 0, V_BM:V_BM + 24], ALU.add))
            gains(0)

            for j in full_jobs:
                L, T, Lh, FT, ly, who = j.L, j.T, j.Lh, j.FT, j.layer, j.who

                def col(c, rows=slice(0, 128)):
                    return vec[rows, ly, c:c + 1]

                for k in range(KD):
                    if j is x1_ and k == KD // 2:
                        for n in range(4):
                            split_lo(c1.u0 + n)
                    if j is not x0:
                        modulate(j, k)

                if j.full:
                    dve.wait_ge(*j.at("hl", KD))
                    if before[j] is not None:
                        dve.wait_ge(*before[j].at("stored", 16 * KD))
                    if j is x1_:
                        used(c1.u0 + 3)
                    chain(V.memset(pads[:, :, 0:1], 0.0))
                    chain(V.memset(pads[:, :, L + 1:L + 2], 0.0))
                    dve.sem_inc(j.s("cv"), 1)

                    def short_conv(kind, i, y, last=None):
                        w0, w1, w2 = [vec[:, ly, bass.ds(i + (V_CONV + (3 * kind + t) * CB), 1)] for t in range(3)]
                        row = pads[:, kind]
                        chain(V.tensor_scalar(y, row[:, 0:L], w0, None, ALU.mult))
                        chain(V.scalar_tensor_tensor(out=y, in0=row[:, 1:L + 1], scalar=w1, in1=y, op0=ALU.mult, op1=ALU.add))
                        ins = V.scalar_tensor_tensor(out=y, in0=row[:, 2:L + 2], scalar=w2, in1=y, op0=ALU.mult, op1=ALU.add)
                        if last is None:
                            chain(ins)
                        else:
                            ins.then_inc(last, 1)

                    tw = j.TW // CB
                    with chain.loop(2, 2 * (2 + 2 + 3)) as i:
                        for ti in range(9):
                            sub = ti // 4
                            c = i * 2 + sub
                            row_of = lambda a: a[:, bass.ds(c, 1), 0:L].rearrange("p o l -> p (o l)")
                            for half in range(2):
                                split_lo(j.u0 + 2 * ti + half, i, LOOP)
                            if ti in (2, 6):
                                dve.wait_ge(*j.at("tabh", i * 2 + (sub + 1)))
                                part = bass.ds(i * (2 * tw) + sub * tw, tw)
                                V.tensor_tensor(tab_lo[:, part], traw[:, part], tab_hi[:, part].bitcast(f32), ALU.subtract)\
                                 .then_inc(j.s("tabl"), 1)
                            if ti == 8:
                                continue
                            dve.wait_ge(*j.at("eva", 9 * i + (9 + ti + 1)))
                            if ti % 4 == 0:
                                short_conv(1, c, row_of(vb), j.s("cv"))
                            elif ti % 4 == 1:
                                short_conv(2, c, row_of(x12[:, 0]), j.s("cv"))
                            elif ti % 4 == 2:
                                short_conv(3, c, y2[:, 0:L])
                            else:
                                V.tensor_tensor(row_of(x12[:, 1]), y2[:, 0:L], szh[:, 0:L], ALU.mult).then_inc(j.s("cv"), 1)
                    dve.wait_ge(*j.at("cv", 1 + 3 * CB))
                    dve.wait_ge(*j.at("tabl", CB))
                    if j is x1_:
                        head_norms(c1, 2 * c1.T)

                    def gated_units(r, f):
                        for half in range(2):
                            split_lo(gated_unit(j, r, f) + half)

                    def gated(r, f):
                        n = gated_unit(j, r, f)
                        y = ya[:, r, 0:L]
                        if f == 1:
                            used(n + 1)
                            dve.wait_ge(*j.at("fva", 2 * r + 1))
                            V.tensor_tensor(pa[:, 0:L], pa[:, 0:L], ps[:, 7, 0:L], ALU.mult).then_inc(j.s("fvd"), 1)
                            dve.wait_ge(*j.at("fvd", 2 * r + 1))
                            w0, w1, w2 = [col(V_CONV + t * CB + r) for t in range(3)]
                            chain(V.tensor_scalar(y, pa[:, 0:L], w1, None, ALU.mult))
                            chain(V.scalar_tensor_tensor(out=y[:, 1:L], in0=pa[:, 0:L - 1], scalar=w0, in1=y[:, 1:L], op0=ALU.mult, op1=ALU.add))
                            chain(V.scalar_tensor_tensor(out=y[:, 0:L - 1], in0=pa[:, 1:L], scalar=w2, in1=y[:, 0:L - 1], op0=ALU.mult, op1=ALU.add))
                        elif f == 2:
                            used(n + 1)
                            V.tensor_tensor(y, y, ps[:, 6, 0:L], ALU.mult).then_inc(j.s("fvd"), 1)
                            dve.wait_ge(*j.at("fvd", 2 * r + 2))
                        elif f == 3:
                            dve.wait_ge(*j.at("fva", 2 * r + 2))
                            V.tensor_tensor(y, y, pa[:, 0:L], ALU.mult).then_inc(j.s("ya"), 1)

                    def last_modulation(n):
                        if j is not c0 or LMOD_STEPS[n] is None or LMOD_STEPS[n][0] == P:
                            return
                        g = LMOD_STEPS[n][1]
                        dve.wait_ge(s_lmcol, g + 1)
                        b = vec[:, 1, V_BM + KD * g:V_BM + KD * g + KD]
                        chain(V.tensor_tensor(modv[:, 1, KD * g:KD * g + KD, 0], ps[:, 2, 0:2 * KD:2], b, ALU.add))
                        V.tensor_tensor(modv[:, 1, KD * g:KD * g + KD, 1], ps[:, 2, 1:2 * KD:2], b, ALU.add).then_inc(s_lmv, 1)
                        dve.wait_ge(s_lmv, g + 1)
                        if g == 1:
                            gains(1)

                    gated_units(0, 0)
                    dve.wait_ge(*j.at("dec", 16))
                    for r in range(4):
                        o, ch = r // 2, r % 2
                        cw = slice(256 * ch, 256 * ch + 256)

                        for tt in range(T):
                            dve.wait_ge(*j.at("kgen", r * T + tt + 1))
                            g = kg[:, tt % 2, :]
                            if r * T + tt >= 2:
                                dve.wait_ge(*j.at("kab", r * T + tt - 1))
                                dve.wait_ge(*j.at("kl", r * T + tt - 1))
                            V.tensor_tensor(g.rearrange("p (d c) -> p d c", d=2), ps[:, tt, :].rearrange("p (d c) -> p d c", d=2),
                                            dec[:, tt:tt + 1, cw].to_broadcast([128, 2, 256]), ALU.mult).then_inc(j.s("kd"), 1)
                            dve.wait_ge(*j.at("kd", r * T + tt + 1))
                            if tt == 0:
                                chain(V.memset(kg[0:1, 0, 256:512], 0.0))
                            chain(V.tensor_tensor(kt[:, tt % 2, 0:256], g[:, 0:256], g[:, 256:512], ALU.add))
                            V.tensor_tensor(kt[:, tt % 2, 256:512], g[:, 0:256], g[:, 256:512], ALU.subtract).then_inc(j.s("kt"), 1)
                            dve.wait_ge(*j.at("kt", r * T + tt + 1))
                            if tt == 1:
                                gated_units(r, 1)
                        if j is x1_ and r == 0:
                            head_normed(c1, 0, qraw_c, 4)
                        dve.wait_ge(*j.at("ksum", (r + 1) * T))
                        V.reciprocal(knorm[:, :], ps[:, 5, 0:2]).then_inc(j.s("kn"), 1)
                        dve.wait_ge(*j.at("kn", r + 1))
                        gated(r, 1)
                        gated_units(r, 2)
                        last_modulation(5 * r)
                        last_modulation(5 * r + 1)
                        for ft in range(FT):
                            dve.wait_ge(*j.at("ke", r * FT + ft + 1))
                            for sgn, op in enumerate((ALU.add, ALU.subtract)):
                                ins = V.tensor_tensor(kspec[:, ft, sgn, :, :].rearrange("p a c -> p (a c)"), e_sb[:, :],
                                                      ps[:, 2 * ft + 1, :], op)
                                if sgn == 0:
                                    chain(ins)
                                else:
                                    ins.then_inc(j.s("kuse"), 1)
                                    dve.wait_ge(*j.at("kuse", r * FT + ft + 1))
                        for b in range((T + 1) // 2):
                            dve.wait_ge(*j.at("uh", r * (T // 2) + b + 1))
                            V.tensor_tensor(u_lo[:, 2 * b:2 * b + 2, :].rearrange("p a c -> p (a c)"), ps[:, 4 + b, :],
                                            u_hi[:, 2 * b:2 * b + 2, :].rearrange("p a c -> p (a c)").bitcast(f32), ALU.subtract)\
                             .then_inc(j.s("ul"), 1)
                        gated(r, 2)
                        for ft in range(FT):
                            k = kspec[:, ft]
                            dve.wait_ge(*j.at("ue", r * FT + ft + 1))
                            chain(V.tensor_tensor(uu[:, 0, :, :].rearrange("p a c -> p (a c)"), e_sb[:, :], ps[:, 2 * ft + 1, :], ALU.add))
                            V.tensor_tensor(uu[:, 1, :, :].rearrange("p a c -> p (a c)"), e_sb[:, :], ps[:, 2 * ft + 1, :], ALU.subtract)\
                             .then_inc(j.s("uuse"), 1)
                            dve.wait_ge(*j.at("uuse", r * FT + ft + 1))
                            chain(V.tensor_tensor(p1[:, :, :, :], uu[:, :, :, :], k, ALU.mult))
                            chain(V.tensor_tensor(p1[:, :, 0, :], p1[:, :, 0, :], p1[:, :, 1, :], ALU.subtract))
                            if ft == 0:
                                gated_units(r, 3)
                            if ft == FT - 1 and r < 3:
                                if r < 2 and FT == 1:
                                    gated_units(r, 4)
                                gated_units(r + 1, 0)
                            dve.wait_ge(*j.at("cross", 2 * (r * FT + ft + 1)))
                            chain(V.tensor_tensor(p2[:, :, 0, :], p2[:, :, 0, :], p2[:, :, 1, :], ALU.add))
                            if ft == 0 and FT > 1 and r < 2:
                                gated_units(r, 4)
                            for n, op in enumerate((ALU.add, ALU.subtract)):
                                chain(V.tensor_tensor(uu[:, n, 0, :], p1[:, 0, 0, :], p1[:, 1, 0, :], op))
                                ins = V.tensor_tensor(uu[:, n, 1, :], p2[:, 0, 0, :], p2[:, 1, 0, :], op)
                                if n == 0:
                                    chain(ins)
                                else:
                                    ins.then_inc(j.s("eo"), 1)
                            dve.wait_ge(*j.at("yh", r * FT + ft + 1))
                            V.tensor_tensor(y_lo[:, :, :, :].rearrange("p a b c -> p (a b c)"),
                                            uu[:, :, :, :].rearrange("p a b c -> p (a b c)"),
                                            y_hi[:, :, :, :].rearrange("p a b c -> p (a b c)").bitcast(f32), ALU.subtract)\
                             .then_inc(j.s("yl"), 1)
                            dve.wait_ge(*j.at("yl", r * FT + ft + 1))
                            if ft == 0:
                                gated(r, 3)
                                for n in (2, 3):
                                    last_modulation(5 * r + n)
                        by_parity = lambda a: a.rearrange("p (i two) -> p two i", two=2)
                        for ct in range(2):
                            c = 2 * ch + ct
                            chain(V.tensor_scalar(zt[:, ct, 0:L].rearrange("p (two i) -> p two i", two=2), by_parity(vb[:, c, 0:L]),
                                                  col(V_HB + CB * o + c), None, ALU.mult))
                        dve.wait_ge(*j.at("yi", (r + 1) * FT))
                        for ct in range(2):
                            c = 2 * ch + ct
                            z = zt[:, ct, 0:L].rearrange("p (two i) -> p two i", two=2)
                            u_row = by_parity(vb[:, c, 0:L])
                            chain(V.scalar_tensor_tensor(out=z, in0=ps[:, 4 + ct, 0:L].rearrange("p (two i) -> p two i", two=2), scalar=knorm[:, ct:ct + 1],
                                                         in1=z, op0=ALU.mult, op1=ALU.add))
                            ins = V.tensor_tensor(u_row, z, by_parity(x12[:, o, c, 0:L]), ALU.mult)
                            if ct == 0:
                                chain(ins)
                            else:
                                ins.then_inc(j.s("fin"), 1)
                                dve.wait_ge(*j.at("fin", r + 1))
                        last_modulation(5 * r + 4)

                last_modulation(20)
                dve.wait_ge(*j.at("ya", CB))
                uq = j.u0 + U_QKV
                nm = 5
                for n in range(U_Q):
                    split_lo(uq + n)
                    if n % 2 == 1 and n // 2 < CB:
                        k = n // 2
                        dve.wait_ge(*j.at("bh", k + 1))
                        V.tensor_tensor(ya_lo[:, k, 0:L], ya[:, k, 0:L], ya_hi[k][:, 0:L].bitcast(f32), ALU.subtract).then_inc(j.s("bl"), 1)
                    if n == U_Q - 1:
                        head_norms(j, 2 * nm * T)

                def first_product(d):
                    used(j.u0 + U_FIRST + 3 * d + 2)
                    dve.wait_ge(*j.at("et", d + 1))
                    V.scalar_tensor_tensor(out=mg[:, d, 0:L], in0=te[:, 0:L], scalar=1.0, in1=ps[:, 7, 0:L], op0=ALU.add, op1=ALU.mult)\
                     .then_inc(j.s("em"), 1)

                def first_branch(e, product=True):
                    split_lo(j.u0 + U_FIRST + e)
                    if e % 3 == 2 and product:
                        first_product(e // 3)

                for e in range(5):
                    first_branch(e)
                for m in range(2):
                    head_normed(j, m, qraw, m % 2)
                first_branch(5)
                for m in range(2, nm):
                    head_normed(j, m, qraw, m % 2)
                first_branch(6)
                first_branch(7)

                def rope(m):
                    if who == 1:
                        return
                    dve.wait_ge(*j.at("rope", 16))
                    mask = [(p + 16) % 32 for p in range(32)]
                    chain(V.stream_shuffle(qsh[:, :], qn[m][:, :], mask))
                    chain(V.tensor_tensor(qn[m][:, :], qn[m][:, :], ropes[:, 0, :], ALU.mult))
                    chain(V.tensor_tensor(qsh[:, :], qsh[:, :], ropes[:, 1, :], ALU.mult))
                    V.tensor_tensor(kx[:, 0:SEQ] if m == 0 else qn[m][:, :], qn[m][:, :], qsh[:, :], ALU.add).then_inc(j.s("qr"), 1)
                    dve.wait_ge(*j.at("qr", m + 1))

                def queries(m):
                    for e in range(2):
                        rows = slice(64 * e, 64 * e + 64)
                        other = slice(64 - 64 * e, 128 - 64 * e)
                        h = 2 * (m - 1) + e
                        dve.wait_ge(*j.at("ksp", 4 + h + 1))
                        V.tensor_tensor(q_hl[other, h, 0:L], qn[m][rows, 0:L], q_hl[rows, h, 0:L].bitcast(f32), ALU.subtract)\
                         .then_inc(j.s("ksl"), 1)

                if who == 0:
                    dve.wait_ge(*j.at("vt", 1))
                rope(0)
                rope(1)
                for g in range(NKV):
                    rows = slice(64 * g, 64 * g + 64)
                    dve.wait_ge(*j.at("ksp", 2 * g + 2))
                    for half in range(2):
                        V.tensor_tensor(k_lo[64 * half:64 * half + 64, g, 0:j.nk], kx[rows, j.k0:j.k0 + j.nk],
                                        k_hi[rows, g, 0:j.nk].bitcast(f32), ALU.subtract).then_inc(j.s("ksl"), 1)
                queries(1)
                first_branch(8, product=False)
                dve.wait_ge(*j.at("vh", 1))
                V.tensor_tensor(v_lo[:, 0:j.kt, :].rearrange("p a c -> p (a c)"),
                                ps[:, 0:2, :].rearrange("p a c -> p (a c)")[:, 0:j.nk],
                                v_hi[:, 0:j.kt, :].rearrange("p a c -> p (a c)").bitcast(f32), ALU.subtract).then_inc(j.s("vl"), 1)
                dve.wait_ge(*j.at("vl", 1))
                first_product(2)

                steps = NH * T

                def maxima(s):
                    dve.wait_ge(*j.at("qk", s + 1))
                    chain(V.tensor_reduce(mx[:, s:s + 1], scores_at(j, s, 0, j.nk), AX.X, ALU.max))
                    V.tensor_scalar(nmx[:, s:s + 1], mx[:, s:s + 1], -SCALE, None, ALU.mult).then_inc(j.s("mx"), 1)

                def lo_of_p(s):
                    grp, q = s // 2, s % 2
                    dve.wait_ge(*j.at("ph", s + 1))
                    V.tensor_tensor(pt_lo[:, grp % 2, 0:j.kt, 128 * q:128 * q + 128],
                                    ps[:, 4:6, :].rearrange("p a c -> p (a c)")[:, 0:j.nk].rearrange("p (a c) -> p a c", c=128),
                                    pt_hi[:, grp % 2, 0:j.kt, 128 * q:128 * q + 128].bitcast(f32), ALU.subtract).then_inc(j.s("pl"), 1)

                def recip(s):
                    dve.wait_ge(*j.at("ex", s + 1))
                    V.reciprocal(rden[:, s:s + 1], den[:, s:s + 1]).then_inc(j.s("rd"), 1)

                def out_of(grp):
                    h, q = grp // (T // 2), grp % (T // 2)
                    g = h // (NH // NKV)
                    rows = slice(64 * g, 64 * g + 64)
                    to = slice(64 * (h % 2), 64 * (h % 2) + 64)
                    dve.wait_ge(*j.at("pv", grp + 1))
                    dve.wait_ge(*j.at("rb", grp + 1))
                    V.tensor_tensor(oT[to, h // 2, 256 * q:256 * q + 256], ps[rows, 6, 0:256], rb[rows, grp % 2, :], ALU.mult)\
                     .then_inc(j.s("oout"), 1)

                maxima(0)
                for s in range(steps):
                    if s + 1 < steps:
                        maxima(s + 1)
                    recip(s)
                    lo_of_p(s)
                    if s % 2 == 1 and s >= 3:
                        out_of(s // 2 - 1)
                    if queries_at(j, s):
                        rope(queries_at(j, s))
                    if queries_at(j, s - 1):
                        queries(queries_at(j, s - 1))
                    for e in first_units(j, s):
                        first_branch(e)
                out_of(steps // 2 - 1)
                dve.wait_ge(*j.at("oout", steps // 2))

                dve.wait_ge(*j.at("em", KD))

                for n, src in enumerate((vb, zs)):
                    if n == 1:
                        dve.wait_ge(*j.at("ze", 2))
                        V.tensor_tensor(zs[:, :, 0:L], oT[:, :, 0:L], zs[:, :, 0:L], ALU.mult).then_inc(j.s("yc"), 1)
                        dve.wait_ge(*j.at("yc", 1))
                    dve.wait_ge(*j.at("bh", CB + n + 1))
                    V.tensor_tensor(b_of(j)[1][:, n, :, 0:L], src[:, :, 0:L], b_of(j)[0][:, n, :, 0:L].bitcast(f32), ALU.subtract).then_inc(j.s("bl"), 1)
                ug = j.u0 + U_GATES
                dve.sem_inc(j.s("pm"), 2)
                dve.wait_ge(*j.at("bl", CB + 2))
                with chain.loop(KD, 1) as i:
                    row = mg[:, bass.ds(i, 1), 0:L].rearrange("p o l -> p (o l)")
                    for n in range(2):
                        for q in range(3):
                            split_lo(ug + 3 * n + q, i, 6)
                        used(ug + 3 * n + 2, i, 6)
                        dve.wait_ge(*j.at("sg", 2 * i + (n + 3)))
                        V.scalar_tensor_tensor(out=tg[:, n, 0:L], in0=sg[:, n, 0:L], scalar=1.0, in1=ps[:, 4 + n, 0:L], op0=ALU.add, op1=ALU.mult)\
                         .then_inc(j.s("pm"), 1)
                        dve.wait_ge(*j.at("pm", 2 * i + (n + 3)))
                        ins = V.tensor_tensor(row, row, tg[:, n, 0:L], ALU.add)
                        if n == 0:
                            chain(ins)
                        else:
                            ins.then_inc(j.s("mg"), 1)
                            dve.wait_ge(*j.at("mg", i + 1))
                    dve.wait_ge(*j.at("gh", i + 1))
                    V.scalar_tensor_tensor(out=mg_lo[:, bass.ds(i, 1), 0:L].rearrange("p o l -> p (o l)"), in0=row, scalar=0.5,
                                           in1=mg_hi[:, bass.ds(i, 1), 0:L].rearrange("p o l -> p (o l)").bitcast(f32),
                                           op0=ALU.mult, op1=ALU.subtract).then_inc(j.s("gl"), 1)
                dve.wait_ge(*j.at("xr", 16))
                for d in range(KD):
                    for half in range(2):
                        split_lo(ug + U_G + 2 * d + half)
                    used(ug + U_G + 2 * d + 1)
                    V.scalar_tensor_tensor(out=xr[:, d, 0:L], in0=ps[:, d % 4, 0:L], scalar=modv[:, ly, 2 * KD + d, who:who + 1],
                                           in1=xr[:, d, 0:L], op0=ALU.mult, op1=ALU.add).then_inc(j.s("xo"), 1)
                    for nx in after[j]:
                        if nx.full and d == 0:
                            chain(V.memset(h2[FHID:FHID + 1, :], 1.0))
                            if nx is x1_:
                                arguments(nx, 0)
                        if nx is not x1_ and d == 3:
                            norm(nx)
                        if nx is x1_ and d == 3:
                            arguments(nx, 1)
                        if nx is not x1_ and d >= 5:
                            for k in (2 * d - 10, 2 * d - 9):
                                modulate(nx, k)
                for nx in after[j]:
                    if nx is not x1_:
                        for k in range(6, KD):
                            modulate(nx, k)
                    else:
                        norm(x1_)

        @block.tensor
        def _(pe):
            MM = nc.tensor.matmul

            def w_ready(n, i=0, per=0):
                pe.wait_ge(s_lo, n + 1 + i * per)

            def unit(n, out, m_hi, m_lo, first, last, i=0, per=0):
                w_ready(n, i, per)
                for k in range(4):
                    hi = w_hi[:, n % RING, 128 * k:128 * k + 128]
                    lo = w_lo[:, n % RING, 128 * k:128 * k + 128]
                    ins = mm3(out, hi, lo, m_hi(k), m_lo(k), first and k == 0, last and k == 3)
                ins.then_inc(s_used, 1)

            def tile(n, out, a_hi, a_lo, i=0, per=0):
                for half in range(2):
                    unit(n + half, out, lambda k: a_hi(4 * half + k), lambda k: a_lo(4 * half + k), half == 0, half == 1, i, per)

            def hidden(j, layer):
                if layer == 0:
                    pe.wait_ge(*{c0: (s_fc0, 48), x0: (s_fx0, 16)}.get(j) or j.at("fil", 48))
                    MM(ps[0:FHID, 6, 0:j.L], fw1[:, :], (feats_x0 if j is x0 else feats)[:, 0:j.L], start=True, stop=True).then_inc(j.s("fm"), 1)
                else:
                    pe.wait_ge(*j.at("fs", 1))
                    MM(ps[0:FHID, 6, 0:j.L], fw2[:, :], h1[:, 0:j.L], start=True, stop=True).then_inc(j.s("fm"), 1)

            def squares(j, k):
                pe.wait_ge(*j.at("sq", k + 1))
                for tt in range(j.T):
                    ins = MM(ps[:, (5, 7)[j.who], tt:tt + 1], sq_of(j, k)[:, 128 * tt:128 * tt + 128], ones[:, 0:1],
                             start=(k == 0 and tt == 0), stop=(k == KD - 1), skip_group_check=True)
                ins.then_inc(j.s("nmsd") if k == KD - 1 else j.s("msq"), 1)

            def norm_rows(j):
                pe.wait_ge(*j.at("nrs", 1))
                for tt in range(j.T):
                    ins = nc.tensor.transpose(ps[:, (4, 7)[j.who], 128 * tt:128 * tt + 128],
                                              nrs[:, j.who, tt:tt + 1].to_broadcast([128, 128]), ident[:, :])
                ins.then_inc(j.s("rbc"), 1)

            def head_squares(j, m, squares, bank):
                pe.wait_ge(*j.at("qsq", m + 1))
                for tt in range(j.T):
                    c = 2 * (m * j.T + tt)
                    ins = MM(ps[:, bank, c:c + 2], squares[:, m, 128 * tt:128 * tt + 128], heads2[:, :], start=True, stop=True)
                ins.then_inc(j.s("msd"), 1)

            def head_rows(j, m, rows, bank):
                for tt in range(j.T):
                    c = 2 * (m * j.T + tt)
                    ins = nc.tensor.transpose(ps[:, bank, 128 * tt:128 * tt + 128],
                                              rows[:, c:c + 2, :].rearrange("p a c -> p (a c)"), ident[:, :])
                ins.then_inc(j.s("qbc"), 1)

            pe.wait_ge(s_const, 6)
            pe.wait_ge(s_cs, 1)
            for k in range(KD):
                pe.wait_ge(s_mw[k % MODS], 16 * (k // MODS + 1))
                for b in range(6):
                    ins = MM(ps[0:2, b, :], cs[:, k, :], mw[k % MODS][:, 512 * b:512 * b + 512], start=(k == 0), stop=(k == KD - 1))
                ins.then_inc(s_mused, 1)
                if k == 1:
                    hidden(c0, 0)
                if k == 2:
                    hidden(c0, 1)
                if k == 3:
                    for kk in range(KD):
                        squares(c0, kk)
                if k == 4:
                    norm_rows(c0)
                    pe.wait_ge(*c0.at("fa", 2))
                    hidden(x0, 0)
                if k == 5:
                    hidden(x0, 1)
            pe.wait_ge(*x0.at("fa", 2))
            pe.wait_ge(s_mrow, 1)
            for t in range(24):
                ins = nc.tensor.transpose(ps[:, 6, 2 * t:2 * t + 2], mrow[:, t // 4, 128 * (t % 4):128 * (t % 4) + 128], ident[0:2, 0:2])
            ins.then_inc(s_mcol, 1)

            for j in full_jobs:
                L, T, Lh, FT, ly, who = j.L, j.T, j.Lh, j.FT, j.layer, j.who
                H = lambda k: h_hi[:, k, 0:L]
                Hl = lambda k: h_lo[:, k, 0:L]
                if j is x1_:
                    pe.wait_ge(*c1.at("hl", KD))
                    for ti in range(2):
                        tile(c1.u0 + 2 * ti, ps[:, ti, 0:CTX], lambda k: hc_hi[:, k, 0:CTX], lambda k: hc_lo[:, k, 0:CTX])
                    pe.wait_ge(*c1.at("qraw", 2))
                pe.wait_ge(*j.at("fs", 2))
                pe.wait_ge(*j.at("hl", KD // 2))

                if j.full:
                    with pe.Fori(0, 2, 1) as i:
                        for ti in range(9):
                            pe.wait_ge(*j.at("eva", 9 * i + (9, 2, 3, 4, 5, 6, 7, 8, 10)[ti]))
                            for half in range(2):
                                if ti == 0 and half == 1:
                                    pe.wait_ge(*j.at("hl", KD))
                                unit(j.u0 + 2 * ti + half, ps[:, ti % 8, 0:L], lambda k: H(4 * half + k), lambda k: Hl(4 * half + k),
                                     half == 0, half == 1, i, LOOP)
                    pe.wait_ge(*j.at("eva", 9 + 18))
                    if j is x1_:
                        head_squares(c1, 0, qsq_c, 5)
                        pe.wait_ge(*c1.at("ms", 1))

                    def gated(r, f, halves=(0, 1)):
                        if f == 0 and r in (1, 2):
                            pe.wait_ge(*j.at("ze", r))
                        if f == 4:
                            pe.wait_ge(*j.at("fvd", 2 * r + 2))
                        if f in (0, 1) and r:
                            pe.wait_ge(*j.at("fvd" if f == 0 else "fva", 2 * r))
                        if f in (2, 3):
                            pe.wait_ge(*j.at("fva" if f == 2 else "fvd", 2 * r + 1))
                        for half in halves:
                            unit(gated_unit(j, r, f) + half, ps[:, 6 + f % 2, 0:L], lambda k: H(4 * half + k), lambda k: Hl(4 * half + k),
                                 half == 0, half == 1)

                    pe.wait_ge(*j.at("tabl", CB))
                    fwd = lambda t, cs_, tt, ft: t[:, cs_ * T * Lh + tt * Lh + 128 * ft:cs_ * T * Lh + tt * Lh + 128 * ft + 128]
                    inv = lambda t, cs_, ft, par: t[:, j.TW // 2 + (cs_ * FT + ft) * L + par * Lh:j.TW // 2 + (cs_ * FT + ft) * L + par * Lh + Lh]

                    def transform(ft, m_hi, m_lo, name):
                        for par in range(2):
                            for cs_ in range(2):
                                out = ps[:, 2 * ft + par, 256 * cs_:256 * cs_ + 256]
                                for a in range(T // 2):
                                    tt = par * (T // 2) + a
                                    ins = mm3(out, fwd(tab_hi, cs_, tt, ft), fwd(tab_lo, cs_, tt, ft), m_hi(tt, cs_), m_lo(tt, cs_),
                                              a == 0, a == T // 2 - 1)
                        ins.then_inc(j.s(name), 1)

                    def magnitudes(r, tt):
                        pe.wait_ge(*j.at("kab", r * T + tt + 1))
                        for d in range(2):
                            for ct in range(2):
                                ins = MM(ps[:, 5, ct:ct + 1], kab[:, tt % 2, 256 * d + 128 * ct:256 * d + 128 * ct + 128], ones[:, 0:1],
                                         start=(tt == 0 and d == 0 and ct == 0), stop=(tt == T - 1 and d == 1), skip_group_check=True)
                        ins.then_inc(j.s("ksum"), 1)

                    def filters(r):
                        pe.wait_ge(*j.at("w3", 16 * (r // 2 + 1)))
                        if r:
                            pe.wait_ge(*j.at("uuse", r * FT))
                        for tt in range(T):
                            MM(ps[:, tt, :], h2[:, 128 * tt:128 * tt + 128], w3s[:, r % 2, :], start=True, stop=True)\
                              .then_inc(j.s("kgen"), 1)

                    def last_modulation(n):
                        if j is not c0 or LMOD_STEPS[n] is None:
                            return
                        kind, q = LMOD_STEPS[n]
                        if kind == TURN:
                            pe.wait_ge(s_lmrow, q + 1)
                            for t in range(KD):
                                ins = nc.tensor.transpose(ps[:, 2, 2 * t:2 * t + 2], lmrow[:, t // 4, 128 * (t % 4):128 * (t % 4) + 128],
                                                          ident[0:2, 0:2])
                            ins.then_inc(s_lmcol, 1)
                            return
                        for m in (q, q + 1):
                            k = m % KD
                            if k == 0 and m:
                                pe.wait_ge(s_lmv, m // KD)
                            pe.wait_ge(s_lmw[m % LMODS], 16 * (m // LMODS + 1))
                            for b in range(2):
                                ins = MM(ps[0:2, 2 + b, :], cs[:, k, :], lmw[m % LMODS][:, 512 * b:512 * b + 512], start=(k == 0), stop=(k == KD - 1))
                            ins.then_inc(s_lmused, 1)

                    if j is x0:
                        pe.wait_ge(*j.at("h2", 2))
                    filters(0)
                    gated(0, 0)
                    for r in range(4):
                        o, ch = r // 2, r % 2
                        gated(r, 1)
                        if r:
                            pe.wait_ge(*j.at("fin", r))
                        for tt in range(T):
                            magnitudes(r, tt)
                            if tt == 0:
                                gated(r, 2)
                                last_modulation(5 * r)
                        last_modulation(5 * r + 1)
                        if j is x1_ and r == 0:
                            pe.wait_ge(*c1.at("rsx", 1))
                            head_rows(c1, 0, rsx_c, 4)
                            pe.wait_ge(*c1.at("qn", 1))
                        pe.wait_ge(*j.at("kl", (r + 1) * T))
                        for ft in range(FT):
                            transform(ft, lambda tt, c: kp_hi[:, tt, 256 * c:256 * c + 256],
                                      lambda tt, c: kp_lo[:, tt, 256 * c:256 * c + 256], "kf")
                        pe.wait_ge(*j.at("kn", r + 1))
                        for b in range((T + 1) // 2):
                            for q in range(2):
                                tt = 2 * b + q
                                par, a = tt // (T // 2), tt % (T // 2)
                                t0 = 256 * a + par
                                for ct in range(2):
                                    ins = nc.tensor.transpose(ps[:, 4 + b, 256 * q + 128 * ct:256 * q + 128 * ct + 128],
                                                              vb[:, 2 * ch + ct, t0:t0 + 255:2], ident[:, :])
                            ins.then_inc(j.s("ut"), 1)
                        gated(r, 3, (0,))
                        pe.wait_ge(*j.at("kuse", (r + 1) * FT))
                        pe.wait_ge(*j.at("ul", (r + 1) * (T // 2)))
                        for ft in range(FT):
                            transform(ft, lambda tt, c: u_hi[:, tt, :], lambda tt, c: u_lo[:, tt, :], "uf")
                        gated(r, 3, (1,))
                        if r < 2:
                            gated(r, 4)
                        if FT == 1 and r < 3:
                            filters(r + 1)
                        for n in (2, 3):
                            last_modulation(5 * r + n)
                        for ft in range(FT):
                            if ft == FT - 1 and r < 3 and FT > 1:
                                filters(r + 1)
                                gated(r + 1, 0)
                            pe.wait_ge(*j.at("yl", r * FT + ft + 1))
                            for ct in range(2):
                                for par in range(2):
                                    for cs_ in range(2):
                                        ins = mm3(ps[:, 4 + ct, par * Lh:par * Lh + Lh], y_hi[:, par, cs_, 128 * ct:128 * ct + 128],
                                                  y_lo[:, par, cs_, 128 * ct:128 * ct + 128], inv(tab_hi, cs_, ft, par),
                                                  inv(tab_lo, cs_, ft, par), ft == 0 and cs_ == 0 and par == 0,
                                                  ft == FT - 1 and cs_ == 1, shared=True)
                            ins.then_inc(j.s("yi"), 1)
                        if FT == 1 and r < 3:
                            gated(r + 1, 0)
                        last_modulation(5 * r + 4)
                    pe.wait_ge(*j.at("fin", 4))

                    last_modulation(20)

                uq = j.u0 + U_QKV
                nm = 5
                pe.wait_ge(*j.at("fvd", 2 * CB))
                for ti in range(6):
                    tile(uq + 2 * ti, ps[:, ti, 0:L], H, Hl)
                    if ti == 2:
                        head_squares(j, 0, qsq, 6)
                    if ti > 2:
                        head_squares(j, ti - 2, qsq, 6)
                head_squares(j, nm - 1, qsq, 6)
                pe.wait_ge(*j.at("fva", 2 * CB))

                def first_branch(e):
                    d, q = e // 3, e % 3
                    n = j.u0 + U_FIRST + e
                    if q == 2:
                        pe.wait_ge(*j.at("bl", CB))
                        pe.wait_ge(*j.at("et", d + 1))
                        unit(n, ps[:, 7, 0:L], lambda k: ya_hi[k][:, 0:L], lambda k: ya_lo[:, k, 0:L], True, True)
                    else:
                        if d and q == 0:
                            pe.wait_ge(*j.at("em", d))
                        unit(n, ps[:, 7, 0:L], lambda k: H(4 * q + k), lambda k: Hl(4 * q + k), q == 0, q == 1)

                for e in range(5):
                    first_branch(e)
                pe.wait_ge(*j.at("rsx", 1))
                for m in range(nm):
                    if m >= 2:
                        pe.wait_ge(*j.at("qn", m - 1))
                    head_rows(j, m, rsx, m % 2)
                    if m == 1:
                        first_branch(5)
                pe.wait_ge(*j.at("qn", nm))
                for t in range(j.kt):
                    ins = nc.tensor.transpose(ps[:, t // 4, 128 * (t % 4):128 * (t % 4) + 128],
                                              vx[:, j.k0 + 128 * t:j.k0 + 128 * t + 128], ident[:, :])
                ins.then_inc(j.s("vt"), 1)
                for e in range(6, 3 * E_EARLY):
                    first_branch(e)
                pe.wait_ge(*j.at("vl", 1))
                pe.wait_ge(*j.at("ksl", 4))

                pe.wait_ge(*j.at("ze", 2))
                steps = NH * T

                def scores(s):
                    h, q = s // T, s % T
                    g = h // (NH // NKV)
                    if s >= 2:
                        pe.wait_ge(*j.at("ex", s - 1))
                    if q == 0:
                        pe.wait_ge(*j.at("ksl", 4 + h + 1 + (h + 1) % 2))
                    lhs = q_hl[:, h, 128 * q:128 * q + 128]
                    for k0, k1 in ((0, min(512, j.nk)), (512, j.nk)):
                        if k1 <= k0:
                            continue
                        out = scores_at(j, s, k0, k1)
                        MM(out, lhs, k_hi[:, g, k0:k1], start=True, stop=False)
                        ins = MM(out, lhs, k_lo[:, g, k0:k1], start=False, stop=True)
                    ins.then_inc(j.s("qk"), 1)

                def transposes(s):
                    pe.wait_ge(*j.at("ex", s + 1))
                    if s >= 1:
                        pe.wait_ge(*j.at("pl", s))
                    for t in range(j.kt):
                        ins = nc.tensor.transpose(ps[:, 4 + t // 4, 128 * (t % 4):128 * (t % 4) + 128],
                                                  pb[:, s % 2, 128 * t:128 * t + 128], ident[:, :])
                    ins.then_inc(j.s("tp"), 1)

                def denominators(grp):
                    if grp:
                        pe.wait_ge(*j.at("oout", grp))
                    pe.wait_ge(*j.at("rd", 2 * grp + 2))
                    for q in range(2):
                        s = 2 * grp + q
                        ins = nc.tensor.transpose(ps[:, 6, 256 + 128 * q:256 + 128 * q + 128],
                                                  rden[:, s:s + 1].to_broadcast([128, 128]), ident[:, :])
                    ins.then_inc(j.s("rt2"), 1)

                def values(grp):
                    pe.wait_ge(*j.at("pl", 2 * grp + 2))
                    pe.wait_ge(*j.at("rb", grp + 1))
                    for t in range(j.kt):
                        ins = mm3(ps[:, 6, 0:256], v_hi[:, t, :], v_lo[:, t, :], pt_hi[:, grp % 2, t, :], pt_lo[:, grp % 2, t, :],
                                  t == 0, t == j.kt - 1)
                    ins.then_inc(j.s("pv"), 1)

                scores(0)
                for s in range(steps):
                    if s % 2 == 1 and s >= 3:
                        denominators(s // 2 - 1)
                    if s + 1 < steps:
                        scores(s + 1)
                    transposes(s)
                    if s % 2 == 1 and s >= 3:
                        values(s // 2 - 1)
                    for e in first_units(j, s):
                        first_branch(e)
                denominators(steps // 2 - 1)
                values(steps // 2 - 1)

                ug = j.u0 + U_GATES
                with pe.Fori(0, KD, 1) as i:
                    for n in range(2):
                        pe.wait_ge(*j.at("sg", 2 * i + (n + 1)))
                        tile(ug + 3 * n, ps[:, n, 0:L], H, Hl, i, 6)
                        pe.wait_ge(*j.at("pm", 2 * i + (n + 1)))
                        pe.wait_ge(*j.at("bl", CB + n + 1))
                        unit(ug + 3 * n + 2, ps[:, 4 + n, 0:L], lambda k: b_of(j)[0][:, n, k, 0:L], lambda k: b_of(j)[1][:, n, k, 0:L], True, True, i, 6)
                pe.wait_ge(*j.at("mg", KD))
                if x1_ in after[j]:
                    hidden(x1_, 0)
                for d in range(KD):
                    if d >= 4:
                        pe.wait_ge(*j.at("xo", d - 3))
                    for half in range(2):
                        if d == 0:
                            pe.wait_ge(*j.at("gl", 4 * half + 4))
                        unit(ug + U_G + 2 * d + half, ps[:, d % 4, 0:L], lambda k: mg_hi[:, 4 * half + k, 0:L], lambda k: mg_lo[:, 4 * half + k, 0:L],
                             half == 0, half == 1)
                    for nx in after[j]:
                        if nx is x1_ and d == 2:
                            hidden(nx, 1)
                        if nx is not x1_:
                            for k in range(2 * d, 2 * d + 2):
                                if k < KD:
                                    squares(nx, k)
                            if d == 4:
                                norm_rows(nx)
                        elif d >= 2:
                            squares(nx, d - 2)
                if x1_ in after[j]:
                    squares(x1_, KD - 2)
                    squares(x1_, KD - 1)
                    norm_rows(x1_)


def _tables(L):
    import math
    import numpy as np
    f = np.float32
    order = np.concatenate([np.arange(0, L, 2), np.arange(1, L, 2)])
    T, Lh = L // 128, L // 2
    FT = Lh // 128

    def linspace(a, b, n):
        s = np.arange(n, dtype=f) / f(n - 1)
        out = f(a) * (f(1) - s) + f(b) * s
        out[-1] = f(b)
        return out

    t = linspace(0.0, 1.0, L)
    bands = linspace(1e-4, 15, 16)
    w = f(2.0 * math.pi / L) * np.arange(L, dtype=f)[:, None]
    wb = (w * bands).astype(f).astype(np.float64)
    feats = np.concatenate([t[:, None], np.cos(wb), np.sin(wb)], axis=1).astype(f)
    lo, hi = math.log(1e-2) / 1.5, math.log(1e-2) / 0.3
    deltas = np.abs(linspace(lo, hi, WB))
    dec = np.exp((-t[:, None] * deltas).astype(f).astype(np.float64)).astype(f)
    theta = 2 * np.pi * (np.arange(Lh) + 0.5) / (2 * L)
    ang = order[:, None] * theta[None, :]
    fwd = np.stack([np.cos(ang), np.sin(ang)])
    fwd = fwd.reshape(2, T, 128, Lh).transpose(2, 0, 1, 3).reshape(128, 2 * T * Lh)
    inv = np.stack([np.cos(ang.T), np.sin(ang.T)]) / L
    inv = inv.reshape(2, FT, 128, L).transpose(2, 0, 1, 3).reshape(128, 2 * FT * L)
    tab = np.concatenate([fwd, inv], axis=1).astype(f)
    return (np.ascontiguousarray(feats[order].T), np.ascontiguousarray(dec[order].reshape(T, 128, WB).transpose(1, 0, 2)), tab)


def _rope():
    import numpy as np
    f = np.float32
    inv = (f(10000.0) ** (-(np.arange(16, dtype=f) / f(16)))).astype(f)
    pos = np.stack([np.repeat(np.arange(SEQ // 64), 64), np.tile(np.arange(64), SEQ // 64)]).astype(f)
    ang = (pos[:, :, None] * inv).astype(f).astype(np.float64)
    out = np.zeros((2, 2, 2, 16, SEQ))
    for a in range(2):
        for half in range(2):
            out[0, a, half] = np.cos(ang[a]).T
            out[1, a, half] = np.sin(ang[a]).T * (1 if half else -1)
    out = out.reshape(2, HD, SEQ)
    return np.ascontiguousarray(np.concatenate([out, out], axis=1).transpose(1, 0, 2)).astype(f)


def kernel(x, c, ctx, c_ctx, norm_g, w_mod, b_mod, w_in, conv_a, conv_h, filt_w1, filt_b1, filt_w2, filt_b2, filt_w3, filt_b3,
           filt_freq, hyena_bias, q_norm_g, k_norm_g, w_branch, w_out):
    import numpy as np
    import concourse.bacc as bacc
    from concourse.bass_utils import run_bass_kernel_spmd as run
    A = np.asarray

    def rows(v):
        return A(v).reshape(-1, 128).T

    def tile_units(w, c0):
        t = A(w)[:, c0:c0 + 128].reshape(-1, 4, 128, 128)
        return list(t.transpose(0, 2, 1, 3).reshape(-1, 128, UW))

    def chunks(v):
        return np.ascontiguousarray(A(v)[0].T.reshape(KD, 128, -1).transpose(1, 0, 2))

    XA, BA, CA, ZA, HV, HX1, HX2, HZ = (512 * n for n in range(8))
    QO, KO, VO, ZO, GO = 4096, 4608, 4736, 4864, 5376
    stream, mod, vec, w3 = [], [], [], []
    for l in range(DEPTH):
        units = []
        for n in range(CB):
            for c0 in (HV, HX1, HX2, HZ):
                units += tile_units(w_in[l], c0 + 128 * n)
            if n % 2 == 1:
                units += tile_units(w_in[l], ZO + 128 * (2 + n // 2))
        for n in range(CB):
            for c0 in (CA, XA, BA, ZA) + ((ZO,) if n < 2 else ()):
                units += tile_units(w_in[l], c0 + 128 * n)
        for c0 in (KO, VO, QO, QO + 128, QO + 256, QO + 384):
            units += tile_units(w_in[l], c0)
        for branches in ((0,), (1, 2)):
            for d in range(KD):
                for n in branches:
                    units += tile_units(w_in[l], GO + 1024 * n + 128 * d)
                    units += tile_units(w_branch[l, n], 128 * d)
        for d in range(KD):
            units += tile_units(w_out[l], 128 * d)
        stream.append(np.stack(units))
        mod.append(A(w_mod)[l].reshape(KD, 128, 3 * D))
        v = np.zeros((128, NV), np.float32)
        v[:, V_NG:V_NG + 8] = rows(norm_g[l])
        v[:, V_BM:V_BM + 24] = rows(b_mod[l])
        for kind in range(4):
            for t in range(3):
                taps = A(conv_a)[l, t] if kind == 0 else A(conv_h)[l, t, WB * (kind - 1):WB * kind]
                v[:, V_CONV + (3 * kind + t) * CB:V_CONV + (3 * kind + t + 1) * CB] = rows(taps)
        v[:, V_HB:V_HB + 8] = rows(A(hyena_bias)[l].reshape(-1))
        v[:, V_QG] = np.tile(A(q_norm_g)[l], 2)
        v[:, V_KG] = np.tile(A(k_norm_g)[l], 2)
        v[:FHID, V_FIL] = A(filt_b1)[l]
        v[:FHID, V_FIL + 1] = A(filt_freq)[l, 0]
        v[:FHID, V_FIL + 2] = A(filt_b2)[l]
        v[:FHID, V_FIL + 3] = A(filt_freq)[l, 1]
        vec.append(v)
        w = np.concatenate([A(filt_w3)[l], A(filt_b3)[l][None]]).reshape(FHID + 1, 2, 2, 2, 256)
        w3.append(w.transpose(1, 0, 3, 2, 4).reshape(2, FHID + 1, 2, 512))
    tx, tc = _tables(SEQ), _tables(CTX)
    arrays = dict(
        stream=np.stack(stream), mod=np.stack(mod),
        cc=np.ascontiguousarray(np.stack([rows(A(c)[0]), rows(c_ctx)], axis=2)),
        x=chunks(x), ctx=chunks(A(ctx)), vec=np.ascontiguousarray(np.stack(vec, axis=1)),
        fw1=A(filt_w1), fw2=A(filt_w2), w3=np.ascontiguousarray(np.stack(w3)),
        feats_x=tx[0], feats_c=tc[0], dec_x=tx[1], dec_c=tc[1], tab_x=tx[2], tab_c=tc[2], rope=_rope())
    nc = bacc.Bacc("TRN2", target_bir_lowering=False, num_devices=1)
    f32 = mybir.dt.float32
    a = {k: nc.dram_tensor(f"in_{k}", v.shape, f32, kind="ExternalInput").ap() for k, v in arrays.items()}
    x1 = nc.dram_tensor("x1", (128, KD, SEQ), f32).ap()
    ctx1 = nc.dram_tensor("ctx1", (128, KD, CTX), f32).ap()
    out = nc.dram_tensor("out", (128, KD, SEQ), f32, kind="ExternalOutput").ap()
    build(nc, a["stream"], a["mod"], a["cc"], a["x"], a["ctx"], a["vec"], a["fw1"], a["fw2"], a["w3"],
          (a["feats_x"], a["feats_c"]), (a["dec_x"], a["dec_c"]), (a["tab_x"], a["tab_c"]), a["rope"], x1, ctx1, out)
    r = run(nc, [{f"in_{k}": np.ascontiguousarray(v) for k, v in arrays.items()}], core_ids=[0])
    y = r.results[0]["out"]
    return np.ascontiguousarray(y.transpose(2, 1, 0).reshape(1, SEQ, D))
```
